# Optimizing a Trainium2 kernel written in Bass

```python
import math
import jax, jax.numpy as jnp
from jax import lax
import numpy as np

D_MODEL = 1024
BATCH = 1
SEQ = 1024
DEPTH = 1
DEC_BATCH = 8
DEC_SEQ = 4
PAST_LEN = 1024
PAGE_SIZE = 128

ATT_HEADS = 8
ATT_HEAD_DIM = 64
ATT_QK_W = ATT_HEADS * 2 * ATT_HEAD_DIM
ATT_V_W = ATT_HEADS * 2 * ATT_HEAD_DIM
Q_BLOCK = 128
S5_CH = 16
S5_WIDTH = D_MODEL
S5_GROUPS = S5_WIDTH // S5_CH
S5_STATE = 64
IN_COLS = 2 * ATT_QK_W + ATT_V_W + S5_WIDTH + 2 * D_MODEL
IN_SPLITS = (ATT_QK_W,
             2 * ATT_QK_W,
             2 * ATT_QK_W + ATT_V_W,
             2 * ATT_QK_W + ATT_V_W + S5_WIDTH,
             2 * ATT_QK_W + ATT_V_W + S5_WIDTH + D_MODEL)
PEER_HEADS = 8
PEER_KEY_DIM = 256
PEER_N_KEYS = 128
PEER_N_EXPERTS = PEER_N_KEYS * PEER_N_KEYS
PEER_TOPK = 16
PEER_BLOCK = 128
RMS_EPS = 1e-6

kernel_name = "hybrid_diffattn_s5_peer_step"

def rms_norm(x, g):
    xf = x.astype(jnp.float32)
    y = xf * lax.rsqrt(jnp.mean(xf * xf, axis=-1, keepdims=True) + RMS_EPS)
    return (y * g.astype(jnp.float32)).astype(x.dtype)

def lambda_init(layer):
    return 0.8 - 0.6 * math.exp(-0.3 * layer)

def diff_attention(q, k, v, q_pos, k_pos, lam):
    q1, q2 = q[..., :ATT_HEAD_DIM], q[..., ATT_HEAD_DIM:]
    k1, k2 = k[..., :ATT_HEAD_DIM], k[..., ATT_HEAD_DIM:]
    scale = ATT_HEAD_DIM ** -0.5
    mask = k_pos[None, :] <= q_pos[:, None]

    def probs(qa, ka):
        s = jnp.einsum('bqhd,bkhd->bhqk', qa, ka).astype(jnp.float32) * scale
        s = jnp.where(mask, s, -jnp.inf)
        return jax.nn.softmax(s, axis=-1)

    p = probs(q1, k1) - lam * probs(q2, k2)
    return jnp.einsum('bhqk,bkhe->bqhe', p.astype(v.dtype), v)

def prompt_attention(q, k, v, lam):
    B, S = q.shape[:2]
    nb = S // Q_BLOCK
    qb = jnp.moveaxis(q.reshape(B, nb, Q_BLOCK, ATT_HEADS, 2 * ATT_HEAD_DIM), 1, 0)
    k_pos = jnp.arange(S)

    def one(args):
        i, qi = args
        q_pos = i * Q_BLOCK + jnp.arange(Q_BLOCK)
        return diff_attention(qi, k, v, q_pos, k_pos, lam)

    ob = lax.map(one, (jnp.arange(nb), qb))
    return jnp.moveaxis(ob, 0, 1).reshape(B, S, ATT_HEADS, 2 * ATT_HEAD_DIM)

def sample_attention(q, k_new, v_new, k_past, v_past, lam):
    past = k_past.shape[1]
    n_new = q.shape[1]
    k = jnp.concatenate([k_past, k_new], axis=1)
    v = jnp.concatenate([v_past, v_new], axis=1)
    q_pos = past + jnp.arange(n_new)
    k_pos = jnp.arange(past + n_new)
    return diff_attention(q, k, v, q_pos, k_pos, lam)

def s5_scan(u, h0_re, h0_im, a_re, a_im, log_step, b_re, b_im, c_re, c_im, d_skip):
    f32 = jnp.float32
    Bsz, L, _ = u.shape
    ug = u.reshape(Bsz, L, S5_GROUPS, S5_CH).astype(f32)
    a_re, a_im = a_re.astype(f32), a_im.astype(f32)
    dt = jnp.exp(log_step.astype(f32))[:, None]
    mag = jnp.exp(a_re * dt)
    ang = a_im * dt
    lb_re, lb_im = mag * jnp.cos(ang), mag * jnp.sin(ang)
    num_re, num_im = lb_re - 1.0, lb_im
    den = a_re * a_re + a_im * a_im
    f_re = (num_re * a_re + num_im * a_im) / den
    f_im = (num_im * a_re - num_re * a_im) / den
    b_re, b_im = b_re.astype(f32), b_im.astype(f32)
    bb_re = f_re[..., None] * b_re - f_im[..., None] * b_im
    bb_im = f_re[..., None] * b_im + f_im[..., None] * b_re
    bu_re = jnp.einsum('blgc,gpc->blgp', ug, bb_re)
    bu_im = jnp.einsum('blgc,gpc->blgp', ug, bb_im)
    h0_re, h0_im = h0_re.astype(f32), h0_im.astype(f32)
    bu_re = bu_re.at[:, 0].add(lb_re * h0_re - lb_im * h0_im)
    bu_im = bu_im.at[:, 0].add(lb_re * h0_im + lb_im * h0_re)
    ar = jnp.broadcast_to(lb_re, (1, L, S5_GROUPS, S5_STATE))
    ai = jnp.broadcast_to(lb_im, (1, L, S5_GROUPS, S5_STATE))

    def combine(e1, e2):
        a1r, a1i, b1r, b1i = e1
        a2r, a2i, b2r, b2i = e2
        return (a2r * a1r - a2i * a1i,
                a2r * a1i + a2i * a1r,
                a2r * b1r - a2i * b1i + b2r,
                a2r * b1i + a2i * b1r + b2i)

    _, _, hr, hi = lax.associative_scan(combine, (ar, ai, bu_re, bu_im), axis=1)
    y = (jnp.einsum('blgp,gcp->blgc', hr, c_re.astype(f32))
         - jnp.einsum('blgp,gcp->blgc', hi, c_im.astype(f32))
         + d_skip.astype(f32) * ug)
    return y.reshape(Bsz, L, S5_WIDTH).astype(u.dtype), hr[:, -1], hi[:, -1]

def peer_ffn(h, w_query, sub_keys, expert_u, expert_v):
    B, L, D = h.shape
    T = B * L
    n_blk = -(-T // PEER_BLOCK)
    pad = n_blk * PEER_BLOCK - T
    hf = jnp.pad(h.reshape(T, D), ((0, pad), (0, 0))).reshape(n_blk, PEER_BLOCK, D)
    half = PEER_KEY_DIM // 2

    def one(xb):
        q = (xb @ w_query).reshape(PEER_BLOCK, PEER_HEADS, PEER_KEY_DIM)
        s1 = jnp.einsum('thd,hkd->thk', q[..., :half], sub_keys[:, 0]).astype(jnp.float32)
        s2 = jnp.einsum('thd,hkd->thk', q[..., half:], sub_keys[:, 1]).astype(jnp.float32)
        v1, i1 = lax.top_k(s1, PEER_TOPK)
        v2, i2 = lax.top_k(s2, PEER_TOPK)
        cand = (v1[..., :, None] + v2[..., None, :]).reshape(PEER_BLOCK, PEER_HEADS, PEER_TOPK * PEER_TOPK)
        cidx = (i1[..., :, None] * PEER_N_KEYS + i2[..., None, :]).reshape(PEER_BLOCK, PEER_HEADS, PEER_TOPK * PEER_TOPK)
        sv, si = lax.top_k(cand, PEER_TOPK)
        eidx = jnp.take_along_axis(cidx, si, axis=-1)
        gate = jax.nn.softmax(sv, axis=-1)
        u_rows = expert_u[eidx]
        act = jax.nn.gelu(jnp.einsum('thkd,td->thk', u_rows, xb), approximate=False)
        w = (gate * act.astype(jnp.float32)).astype(xb.dtype)
        return jnp.einsum('thk,thkd->td', w, expert_v[eidx])

    out = lax.map(one, hf).reshape(n_blk * PEER_BLOCK, D)[:T]
    return out.reshape(B, L, D)

def trunk_layer(x, attend, h0_re, h0_im, lw, lam_init):
    B, L = x.shape[:2]
    h = rms_norm(x, lw['norm_mix_g'])
    proj = h @ lw['w_in']
    q, k, v, u, g_att, g_s5 = jnp.split(proj, IN_SPLITS, axis=-1)
    hs = (B, L, ATT_HEADS, 2 * ATT_HEAD_DIM)
    q, k, v = q.reshape(hs), k.reshape(hs), v.reshape(hs)
    att = attend(q, k, v)
    att = (rms_norm(att, lw['subln_g']) * (1.0 - lam_init)).reshape(B, L, ATT_V_W)
    s5y, hT_re, hT_im = s5_scan(u, h0_re, h0_im, lw['s5_a_re'], lw['s5_a_im'], lw['s5_log_step'],
                                lw['s5_b_re'], lw['s5_b_im'], lw['s5_c_re'], lw['s5_c_im'], lw['s5_d'])
    z = jax.nn.gelu(s5y, approximate=False)
    s5o = z * jax.nn.sigmoid(z @ lw['w_glu'] + lw['b_glu'])
    merged = (jax.nn.sigmoid(g_att) * (att @ lw['w_proj_att'])
              + jax.nn.sigmoid(g_s5) * (s5o @ lw['w_proj_s5']))
    x = x + merged @ lw['w_out']
    x = x + peer_ffn(rms_norm(x, lw['norm_ffn_g']), lw['peer_w_query'], lw['peer_sub_keys'],
                     lw['peer_u'], lw['peer_v'])
    return x, k, v, hT_re, hT_im

def setup_inputs(seed: int = 0) -> dict:
    key = jax.random.key(seed)
    ks = iter(jax.random.split(key, 40))
    f32 = jnp.float32

    def nrm(shape, scale):
        return jax.random.normal(next(ks), shape, f32) * scale

    HD2 = 2 * ATT_HEAD_DIM
    n_pages = PAST_LEN // PAGE_SIZE
    n_used = DEC_BATCH * n_pages
    n_phys = n_used + (n_used + 3) // 4
    perm = jax.random.permutation(next(ks), n_phys)
    page_table = perm[:n_used].reshape(DEC_BATCH, n_pages).astype(jnp.int32)
    G, P, C = S5_GROUPS, S5_STATE, S5_CH
    return {
        'x_prompt': nrm((BATCH, SEQ, D_MODEL), 1.0),
        'x_sample': nrm((DEC_BATCH, DEC_SEQ, D_MODEL), 1.0),
        'cache_k': nrm((DEPTH, n_phys, PAGE_SIZE, ATT_HEADS, HD2), 1.0),
        'cache_v': nrm((DEPTH, n_phys, PAGE_SIZE, ATT_HEADS, HD2), 1.0),
        'state_s5_re': nrm((DEPTH, DEC_BATCH, G, P), 0.3),
        'state_s5_im': nrm((DEPTH, DEC_BATCH, G, P), 0.3),
        'page_table': page_table,
        'norm_mix_g': 1.0 + nrm((DEPTH, D_MODEL), 0.02),
        'w_in': nrm((DEPTH, D_MODEL, IN_COLS), D_MODEL ** -0.5),
        'lambda_q1': nrm((DEPTH, ATT_HEAD_DIM), 0.1),
        'lambda_k1': nrm((DEPTH, ATT_HEAD_DIM), 0.1),
        'lambda_q2': nrm((DEPTH, ATT_HEAD_DIM), 0.1),
        'lambda_k2': nrm((DEPTH, ATT_HEAD_DIM), 0.1),
        'subln_g': 1.0 + nrm((DEPTH, HD2), 0.02),
        's5_a_re': -0.5 + nrm((DEPTH, G, P), 0.01),
        's5_a_im': jnp.pi * jnp.arange(P, dtype=f32) + nrm((DEPTH, G, P), 0.01),
        's5_log_step': jax.random.uniform(next(ks), (DEPTH, G), f32, math.log(1e-3), math.log(1e-1)),
        's5_b_re': nrm((DEPTH, G, P, C), C ** -0.5),
        's5_b_im': nrm((DEPTH, G, P, C), C ** -0.5),
        's5_c_re': nrm((DEPTH, G, C, P), P ** -0.5),
        's5_c_im': nrm((DEPTH, G, C, P), P ** -0.5),
        's5_d': nrm((DEPTH, G, C), 1.0),
        'w_glu': nrm((DEPTH, S5_WIDTH, S5_WIDTH), S5_WIDTH ** -0.5),
        'b_glu': nrm((DEPTH, S5_WIDTH), 0.02),
        'w_proj_att': nrm((DEPTH, ATT_V_W, D_MODEL), ATT_V_W ** -0.5),
        'w_proj_s5': nrm((DEPTH, S5_WIDTH, D_MODEL), S5_WIDTH ** -0.5),
        'w_out': nrm((DEPTH, D_MODEL, D_MODEL), D_MODEL ** -0.5),
        'norm_ffn_g': 1.0 + nrm((DEPTH, D_MODEL), 0.02),
        'peer_w_query': nrm((DEPTH, D_MODEL, PEER_HEADS * PEER_KEY_DIM), D_MODEL ** -0.5),
        'peer_sub_keys': nrm((DEPTH, PEER_HEADS, 2, PEER_N_KEYS, PEER_KEY_DIM // 2), (PEER_KEY_DIM // 2) ** -0.5),
        'peer_u': nrm((DEPTH, PEER_N_EXPERTS, D_MODEL), D_MODEL ** -0.5),
        'peer_v': nrm((DEPTH, PEER_N_EXPERTS, D_MODEL), PEER_HEADS ** -0.5),
        'norm_final_g': 1.0 + nrm((D_MODEL,), 0.02),
    }

def reference(x_prompt, x_sample, cache_k, cache_v, state_s5_re, state_s5_im, page_table,
              norm_mix_g, w_in, lambda_q1, lambda_k1, lambda_q2, lambda_k2, subln_g,
              s5_a_re, s5_a_im, s5_log_step, s5_b_re, s5_b_im, s5_c_re, s5_c_im, s5_d,
              w_glu, b_glu, w_proj_att, w_proj_s5, w_out,
              norm_ffn_g, peer_w_query, peer_sub_keys, peer_u, peer_v, norm_final_g):
    f32 = jnp.float32
    xp, xs = x_prompt, x_sample
    n_seq, n_pages = page_table.shape
    kp, vp, srp, sip, ksm, vsm, srs, sis = [], [], [], [], [], [], [], []
    for l in range(DEPTH):
        lam_init = lambda_init(l)
        lam = (jnp.exp(jnp.sum(lambda_q1[l].astype(f32) * lambda_k1[l].astype(f32)))
               - jnp.exp(jnp.sum(lambda_q2[l].astype(f32) * lambda_k2[l].astype(f32)))
               + lam_init)
        lw = {
            'norm_mix_g': norm_mix_g[l], 'w_in': w_in[l], 'subln_g': subln_g[l],
            's5_a_re': s5_a_re[l], 's5_a_im': s5_a_im[l], 's5_log_step': s5_log_step[l],
            's5_b_re': s5_b_re[l], 's5_b_im': s5_b_im[l], 's5_c_re': s5_c_re[l], 's5_c_im': s5_c_im[l],
            's5_d': s5_d[l], 'w_glu': w_glu[l], 'b_glu': b_glu[l],
            'w_proj_att': w_proj_att[l], 'w_proj_s5': w_proj_s5[l], 'w_out': w_out[l],
            'norm_ffn_g': norm_ffn_g[l], 'peer_w_query': peer_w_query[l],
            'peer_sub_keys': peer_sub_keys[l], 'peer_u': peer_u[l], 'peer_v': peer_v[l],
        }
        h0 = jnp.zeros((xp.shape[0], S5_GROUPS, S5_STATE), f32)
        xp, k_p, v_p, hr_p, hi_p = trunk_layer(
            xp, lambda q, k, v: prompt_attention(q, k, v, lam), h0, h0, lw, lam_init)
        k_past = cache_k[l][page_table].reshape(n_seq, n_pages * PAGE_SIZE, ATT_HEADS, 2 * ATT_HEAD_DIM)
        v_past = cache_v[l][page_table].reshape(n_seq, n_pages * PAGE_SIZE, ATT_HEADS, 2 * ATT_HEAD_DIM)
        xs, k_s, v_s, hr_s, hi_s = trunk_layer(
            xs, lambda q, k, v: sample_attention(q, k, v, k_past, v_past, lam),
            state_s5_re[l], state_s5_im[l], lw, lam_init)
        kp.append(k_p); vp.append(v_p); srp.append(hr_p); sip.append(hi_p)
        ksm.append(k_s); vsm.append(v_s); srs.append(hr_s); sis.append(hi_s)
    y_prompt = rms_norm(xp, norm_final_g)
    y_sample = rms_norm(xs, norm_final_g)
    return (y_prompt, y_sample,
            jnp.stack(kp), jnp.stack(vp), jnp.stack(srp), jnp.stack(sip),
            jnp.stack(ksm), jnp.stack(vsm), jnp.stack(srs), jnp.stack(sis))


_drawn_inputs = setup_inputs


def setup_inputs(seed=0):
    import zlib

    import numpy as np

    out = dict(_drawn_inputs(seed))
    spreads = {}
    factors = {'lambda_q1': 3.188,
     'lambda_k1': 7.491,
     'subln_g': 3.288,
     's5_a_re': 15.081,
     'b_glu': 36.666,
     'norm_final_g': 7.503,
     'lambda_k2': 4.144,
     'norm_ffn_g': 3.607}
    for name, (base, spread) in spreads.items():
        noise = np.random.default_rng([zlib.crc32(name.encode()), seed]).standard_normal(out[name].shape)
        drawn = base * np.exp(spread * noise) if base else spread * noise
        out[name] = __import__('jax').numpy.asarray(drawn.astype(out[name].dtype))
    for name, factor in factors.items():
        out[name] = (out[name] * factor).astype(out[name].dtype)
    return out
```

```python
from contextlib import ExitStack
import math

import numpy as np

import concourse.bass as bass
from concourse import mybir

F32 = mybir.dt.float32
U32 = mybir.dt.uint32
I32 = mybir.dt.int32
ALU = mybir.AluOpType
ACT = mybir.ActivationFunctionType
AX = mybir.AxisListType

P = 128
D = 1024
KC = D // P
SEQ = 1024
NSEQ, NNEW = 8, 4
NS = NSEQ * NNEW
T = SEQ + NS
TT = SEQ // P
NC3 = 3
CW = T // NC3
H = 8
HD = 64
G, PS5, CH = 64, 64, 16
GP = G // 2
ST8 = 8
NCH = SEQ // ST8
PAGES = 8
PH, PK, TOPK = 8, 128, 16
NE = PK * PK
EPS = 1e-6
LAM_INIT = 0.8 - 0.6 * math.exp(-0.3 * 0)
NEG = -1e30
LOWEST = -3e38
ARENA = 52900
ROUND = 1.5 * 2 ** 23
TWO_PI = (6.28125, 0.00193500518798828125, 2 * math.pi - 6.28125 - 0.00193500518798828125)
SIN_AT = 12

T_QK, T_GS, T_GLU, T_GA, T_QUERY = 0, 16, 32, 40, 56

START = 1
START_AT_ONE = ("hT_done", "gl_used", "prod", "oT_free", "t_free", "ko_clear", "kt_ready", "on_acc",
                "on_free", "en_ready", "kt_free", "page_used", "ptn_free", "ptn_ready", "sn_ready", "sc_done",
                "s_acc", "tk_done", "idx_cp", "gelu_d", "diag_d", "yo_d", "dots", "init_d")


def hybrid_step(nc, dr, out):
    root = ExitStack()
    with root:
        started = {n: root.enter_context(nc.semaphore(n)) for n in START_AT_ONE}

        def sem(name):
            return started[name] if name in started else root.enter_context(nc.semaphore(name))

        spare = sem("spare")

        def alone(eng):
            eng.sem_inc(spare, 1)

        def sbuf(stack, name, shape, dt=F32):
            return stack.enter_context(nc.sbuf_tensor(name, shape, dt))

        ps = root.enter_context(nc.psum_tensor("ps", [P, 8, 512], F32))

        ident = sbuf(root, "ident", [P, P])
        g_mix = sbuf(root, "g_mix", [P, KC])
        g_ffn = sbuf(root, "g_ffn", [P, KC])
        b_glu = sbuf(root, "b_glu", [P, KC])
        neg_lam = sbuf(root, "neg_lam", [P, 2])
        arena = sbuf(root, "arena", [P, ARENA])

        def lay(at, shape, dt=F32):
            n = int(np.prod(shape))
            assert at + n <= ARENA, (at, shape)
            flat = arena[:, at:at + n]
            if dt != F32:
                flat = flat.bitcast(dt)
            names = [f"d{i}" for i in range(len(shape))]
            if len(shape) == 1:
                return flat
            return flat.rearrange(f"p ({' '.join(names)}) -> p {' '.join(names)}",
                                  **{m: s for m, s in zip(names[1:], shape[1:])})

        w_in = [sem(f"w_in{k}") for k in range(2)]
        acc_ready = [sem(f"acc_ready{k}") for k in range(2)]
        acc_free = [sem(f"acc_free{k}") for k in range(2)]
        pairs = 0

        def stat_load(sp, wbuf, k, tile):
            sp.dma_start(wbuf[:, k, :], tile).then_inc(w_in[k], 16)

        def stat_loads(sp, wbuf, tile0, n, pairs):
            for k in range(2):
                stat_load(sp, wbuf, k, dr["w_stat"][tile0 + k])
            with sp.Fori(1, n) as i:
                for k in range(2):
                    sp.wait_ge(acc_ready[k], i * 3 + 3 * pairs)
                    stat_load(sp, wbuf, k, dr["w_stat"][bass.ds(i * 2 + (tile0 + k), 1)]
                              .rearrange("a p n -> (a p) n"))

        def stat_products(pe, i, k, wbuf, moving, pairs):
            pe.wait_ge(w_in[k], i * 16 + 16 * (pairs + 1))
            for c in range(NC3):
                pe.wait_ge(acc_free[k], i * 3 + (3 * pairs + c + 1))
                for kc in range(KC):
                    last = nc.tensor.matmul(ps[:, 3 * k + c, 0:CW], wbuf[:, k, kc * P:(kc + 1) * P],
                                            moving[:, kc, c * CW:(c + 1) * CW],
                                            start=(kc == 0), stop=(kc == KC - 1))
                last.then_inc(acc_ready[k], 1)

        AT_CL, AT_TOE, AT_UG, AT_HH, AT_UA, AT_HS, AT_H0, AT_WK, AT_PW, AT_HT = np.cumsum(
            [0, GP * 2 * 9 * CH, G * P, G * P, 2 * GP * (NCH + 1), G * NSEQ, 2 * GP * NSEQ, 2 * GP * NSEQ,
             G * P, 9 * 2 * GP]).tolist()
        hT = lay(AT_HT, [KC, T])
        if True:
            xt = lay(AT_HH, [2, D])
            junk = lay(AT_HH + 2 * D, [D])
            lamv = lay(AT_HH + 3 * D, [4, HD])
            junk2 = lay(AT_HH + 4 * D, [2, HD])
            lam = lay(AT_HH + 5 * D, [4])
            ss = lay(AT_HH + 5 * D + 4, [2])
            const_in, lam_in = sem("const_in"), sem("lam_in")
            x_in = [sem(f"x_in{k}") for k in range(2)]
            sq_done, ms_done, rt_done, rc_done = sem("sq_done"), sem("ms_done"), sem("rt_done"), sem("rc_done")
            xn_done, xT_done, hT_done = sem("xn_done"), sem("xT_done"), sem("hT_done")
            lam_v, lam_a = sem("lam_v"), sem("lam_a")

            def norm_tile_act(act, x, ssq, rows, n):
                nc.scalar.activation(junk[0:rows, :], x, ACT.Square, accum_out=ssq).then_inc(sq_done, 1)
                act.wait_ge(ms_done, n + 1)
                nc.scalar.activation(ssq, ssq, ACT.Sqrt).then_inc(rt_done, 1)
                act.wait_ge(rc_done, n + 1)
                nc.scalar.activation(x, x, ACT.Copy, scale=ssq).then_inc(xn_done, 1)

            def norm_tile_dve(dve, ssq, n):
                dve.wait_ge(sq_done, n + 1)
                nc.vector.tensor_scalar(ssq, ssq, 1.0 / D, EPS, ALU.mult, ALU.add).then_inc(ms_done, 1)
                dve.wait_ge(rt_done, n + 1)
                nc.vector.reciprocal(ssq, ssq).then_inc(rc_done, 1)

            with nc.Block() as block:
                @block.sync
                def _(sp):
                    for s in started.values():
                        sp.sem_inc(s, START)
                    sp.dma_start(ident[:, :], dr["ident"]).then_inc(const_in, 16)
                    sp.dma_start(g_mix[:, :], dr["g_mix"]).then_inc(const_in, 16)
                    sp.dma_start(g_ffn[:, :], dr["g_ffn"]).then_inc(const_in, 16)
                    sp.dma_start(b_glu[:, :], dr["b_glu"]).then_inc(const_in, 16)
                    sp.dma_start(lamv[:, :, :].rearrange("p a b -> p (a b)"),
                                 dr["lam"].broadcast_to([P, 4 * HD])).then_inc(lam_in, 16)
                    for k in range(2):
                        sp.dma_start(xt[:, k, :], dr["x"][k * P:(k + 1) * P, :]).then_inc(x_in[k], 16)
                    with sp.Fori(1, TT // 2) as i:
                        for k in range(2):
                            sp.wait_ge(xT_done, i * 2 + (k - 1))
                            sp.dma_start(xt[:, k, :], dr["x"][bass.ds(i * 2 * P + k * P, P), :]).then_inc(x_in[k], 16)
                    sp.wait_ge(xT_done, TT - 1)
                    sp.dma_start(xt[0:NS, 0, :], dr["x"][SEQ:T, :]).then_inc(x_in[0], 16)

                @block.scalar
                def _(act):
                    for k in range(2):
                        act.sem_inc(acc_free[k], 3)
                    with act.Fori(0, TT // 2) as i:
                        for k in range(2):
                            act.wait_ge(x_in[k], (i + 1) * 16)
                            norm_tile_act(act, xt[:, k, :], ss[:, k:k + 1], P, i * 2 + k)
                    act.wait_ge(x_in[0], 16 * (TT // 2 + 1))
                    norm_tile_act(act, xt[0:NS, 0, :], ss[0:NS, 0:1], NS, TT)
                    act.wait_ge(lam_v, 1)
                    nc.scalar.activation(lam[:, 2:4], lam[:, 0:2], ACT.Exp).then_inc(lam_a, 1)

                @block.tensor
                def _(pe):
                    pe.wait_ge(const_in, 64)

                    def transposes(k, rows, n):
                        pe.wait_ge(xn_done, n + 1)
                        if k is not None:
                            pe.wait_ge(hT_done, START + n)
                        for c in range(KC):
                            last = nc.tensor.transpose(ps[:, c // 4, (c % 4) * P:(c % 4) * P + rows],
                                                       xt[0:rows, k, c * P:(c + 1) * P], ident[0:rows, 0:rows])
                        last.then_inc(xT_done, 1)

                    with pe.Fori(0, TT // 2) as i:
                        for k in range(2):
                            transposes(k, P, i * 2 + k)
                    transposes(0, NS, TT)

                @block.vector
                def _(dve):
                    def take_out(rows, col, n):
                        dve.wait_ge(xT_done, n + 1)
                        for b in range(2):
                            last = nc.vector.tensor_tensor(
                                hT[:, 4 * b:4 * b + 4, bass.ds(col, rows)],
                                ps[:, b, :].rearrange("p (c t) -> p c t", c=4)[:, :, 0:rows],
                                g_mix[:, 4 * b:4 * b + 4].unsqueeze(2).broadcast_to([P, 4, rows]), ALU.mult)
                        last.then_inc(hT_done, 1)

                    dve.wait_ge(const_in, 64)
                    with dve.Fori(0, TT // 2) as i:
                        for k in range(2):
                            norm_tile_dve(dve, ss[:, k:k + 1], i * 2 + k)
                            take_out(P, i * 2 * P + k * P, i * 2 + k)
                    norm_tile_dve(dve, ss[0:NS, 0:1], TT)
                    take_out(NS, SEQ, TT)
                    dve.wait_ge(lam_in, 16)
                    for b in range(2):
                        last = nc.vector.tensor_tensor_reduce(junk2[:, b, :], lamv[:, 2 * b, :], lamv[:, 2 * b + 1, :], 1.0, 0.0,
                                                              ALU.mult, ALU.add, lam[:, b:b + 1])
                    last.then_inc(lam_v, 1)
                    dve.wait_ge(lam_a, 1)
                    nc.vector.tensor_tensor(neg_lam[:, 0:1], lam[:, 3:4], lam[:, 2:3], ALU.subtract).then_inc(lam_v, 1)
                    dve.wait_ge(lam_v, 2)
                    nc.vector.tensor_scalar(neg_lam[:, 1:2], neg_lam[:, 0:1], -LAM_INIT, None, ALU.add).then_inc(lam_v, 1)
                    dve.wait_ge(lam_v, 3)
                    nc.vector.memset(neg_lam[:, 0:1], 1.0)

        cl = lay(AT_CL, [GP, 2, 9, CH])
        m_toe = lay(AT_TOE, [G, P])
        ug = lay(AT_UG, [G, P])
        hh = lay(AT_HH, [2, GP, NCH + 1])
        ua = lay(AT_UA, [G, NSEQ])
        hs = lay(AT_HS, [2, GP, NSEQ])
        h0 = lay(AT_H0, [2, GP, NSEQ])
        wk = lay(AT_WK, [GP, 2, ST8, CH])
        kst = lay(AT_WK, [G, ST8, CH])
        z_tok = lay(AT_WK, [ST8, D])
        pw = lay(AT_PW, [9, 2, GP])
        u_tok = lay(AT_TOE, [G, ST8, CH])
        slab = lay(AT_WK, [2, KC, 512])
        us_tok = lay(AT_HH, [G, NNEW, CH])
        bri = lay(AT_HH + 4096, [2, GP, CH])
        cri = lay(AT_HH + 5120, [2, GP, CH])
        bb = lay(AT_HH + 6144, [2, GP, CH])
        tmp = lay(AT_HH + 7168, [GP, CH])
        sm = lay(AT_HH + 7680, [18, GP])
        d_s5 = lay(AT_HT + KC * T, [G])
        scr_h = nc.dram_tensor("scr_h", (P, KC * T), F32, kind="Internal").ap()

        par_in, slab_in = sem("par_in"), [sem(f"slab_in{k}") for k in range(2)]
        u_ready, u_free = sem("u_ready"), sem("u_free")
        ug_ready, ug_free = sem("ug_ready"), sem("ug_free")
        par_a, par_v, spill = sem("par_a"), sem("par_v"), sem("spill")
        NU = 2 * ST8 + 2 * NNEW

        def complex_step(dve, mul, re, im, ar, ai, br, bi, sign, t):
            mul(re, ar, br, ALU.mult)
            mul(t, ai, bi, ALU.mult)
            mul(re, re, t, ALU.subtract)
            mul(im, ar, bi, ALU.mult)
            mul(t, ai, br, ALU.mult)
            if sign > 0:
                mul(im, im, t, ALU.add)
            else:
                par["n"] += 1
                nc.vector.scalar_tensor_tensor(im, im, -1.0, t, ALU.mult, ALU.subtract).then_inc(par_v, 1)
                dve.wait_ge(par_v, par["n"])

        par = {"n": 0}
        with nc.Block() as block:
            @block.sync
            def _(sp):
                for k in range(2):
                    sp.dma_start(slab[:, k, :, :].rearrange("p a b -> p (a b)"), dr["w_mov"][k]).then_inc(slab_in[k], 16)
                for dst, name in ((sm[:, 0, :], "a_re"), (sm[:, 1, :], "a_im"), (sm[:, 2, :], "log_step"),
                                  (bri.rearrange("p r g c -> p (r g c)"), "b_ri"), (cri.rearrange("p r g c -> p (r g c)"), "c_ri"),
                                  (h0.rearrange("p r g q -> p (r g q)"), "h0"), (d_s5[0:CH, :], "d_s5")):
                    sp.dma_start(dst, dr[name]).then_inc(par_in, 16)
                sp.wait_ge(u_ready, NU)
                sp.dma_start(scr_h, hT.rearrange("p c t -> p (c t)")).then_inc(spill, 16)
                sp.wait_ge(spill, 16)

            @block.tensor
            def _(pe):
                n = 0
                for k in range(2):
                    pe.wait_ge(slab_in[k], 16)
                    for s in range(ST8 + NNEW):
                        if n >= 4:
                            pe.wait_ge(u_free, n - 3)
                        rows = P if s < ST8 else NSEQ
                        for kc in range(KC):
                            tok = hT[:, kc, s:SEQ:ST8] if s < ST8 else hT[:, kc, SEQ + s - ST8:T:NNEW]
                            last = nc.tensor.matmul(ps[0:rows, n % 4, :], tok, slab[:, k, kc, :],
                                                    start=(kc == 0), stop=(kc == KC - 1))
                        last.then_inc(u_ready, 1)
                        n += 1
                pe.wait_ge(u_free, NU)
                for q in range(G // 4):
                    if q >= 3:
                        pe.wait_ge(ug_free, q - 2)
                    for j in range(4):
                        g = 4 * q + j
                        last = nc.tensor.transpose(ps[:, 4 + q % 3, j * P:(j + 1) * P],
                                                   u_tok[:, g], ident[:, :])
                    last.then_inc(ug_ready, 1)
                for g in range(G):
                    last = nc.tensor.transpose(ps[0:64, 7, g * NSEQ:(g + 1) * NSEQ],
                                               us_tok[0:NSEQ, g], ident[0:NSEQ, 0:NSEQ])
                last.then_inc(ug_ready, 1)

            @block.scalar
            def _(act):
                dt_, mag, ang, r2 = sm[:, 3, :], sm[:, 4, :], sm[:, 5, :], sm[:, 6:8, :]
                act.wait_ge(par_in, 112)
                nc.scalar.activation(dt_, sm[:, 2, :], ACT.Exp).then_inc(par_a, 1)
                act.wait_ge(par_v, 1)
                nc.scalar.activation(mag, mag, ACT.Exp).then_inc(par_a, 1)
                act.wait_ge(par_v, SIN_AT)
                nc.scalar.activation(r2, r2, ACT.Sin).then_inc(par_a, 1)
                n = 0
                for k in range(2):
                    for s in range(ST8 + NNEW):
                        act.wait_ge(u_ready, n + 1)
                        gs_ = slice(G // 2 * k, G // 2 * (k + 1))
                        rows = P if s < ST8 else NSEQ
                        dst = u_tok[:, gs_, s, :] if s < ST8 else us_tok[0:NSEQ, gs_, s - ST8, :]
                        nc.scalar.activation(dst, ps[0:rows, n % 4, :].rearrange("p (g c) -> p g c", c=CH), ACT.Copy).then_inc(u_free, 1)
                        n += 1
                for q in range(G // 4):
                    act.wait_ge(ug_ready, q + 1)
                    nc.scalar.activation(ug[:, 4 * q:4 * q + 4, :].rearrange("p g t -> p (g t)"), ps[:, 4 + q % 3, :],
                                         ACT.Copy).then_inc(ug_free, 1)
                act.wait_ge(ug_ready, G // 4 + 1)
                nc.scalar.activation(ua[0:64].rearrange("p g q -> p (g q)"), ps[0:64, 7, :], ACT.Copy).then_inc(ug_free, 1)

            @block.vector
            def _(dve):
                def op(ins):
                    par["n"] += 1
                    ins.then_inc(par_v, 1)
                    dve.wait_ge(par_v, par["n"])

                def mul(o, a, b, how):
                    op(nc.vector.tensor_tensor(o, a, b, how))

                a_re, a_im, dt_, mag, ang, r2, q2 = (sm[:, 0, :], sm[:, 1, :], sm[:, 3, :], sm[:, 4, :], sm[:, 5, :],
                                                     sm[:, 6:8, :], sm[:, 8:10, :])
                t0, t1, f_re, f_im, den = (sm[:, j, :] for j in range(10, 15))
                dve.wait_ge(par_a, 1)
                mul(mag, a_re, dt_, ALU.mult)
                mul(ang, a_im, dt_, ALU.mult)
                for j in range(2):
                    op(nc.vector.tensor_scalar(q2[:, j, :], ang, 1 / (2 * math.pi), 0.25 * j, ALU.mult, ALU.add))
                op(nc.vector.tensor_scalar(q2, q2, ROUND, None, ALU.add))
                op(nc.vector.tensor_scalar(q2, q2, -ROUND, None, ALU.add))
                for j in range(2):
                    op(nc.vector.scalar_tensor_tensor(r2[:, j, :], q2[:, j, :], -TWO_PI[0], ang, ALU.mult, ALU.add))
                for part in TWO_PI[1:]:
                    op(nc.vector.scalar_tensor_tensor(r2, q2, -part, r2, ALU.mult, ALU.add))
                op(nc.vector.tensor_scalar(r2[:, 1, :], r2[:, 1, :], math.pi / 2, None, ALU.add))
                op(nc.vector.tensor_scalar(r2, r2, 3.1415925, -3.1415925, ALU.min, ALU.max))
                assert par["n"] == SIN_AT, par
                dve.wait_ge(par_a, 3)
                op(nc.vector.memset(pw[:, 0, 0, :], 1.0))
                op(nc.vector.memset(pw[:, 0, 1, :], 0.0))
                mul(pw[:, 1, 0, :], mag, r2[:, 1, :], ALU.mult)
                mul(pw[:, 1, 1, :], mag, r2[:, 0, :], ALU.mult)
                for j in range(2, 9):
                    complex_step(dve, mul, pw[:, j, 0, :], pw[:, j, 1, :], pw[:, j - 1, 0, :], pw[:, j - 1, 1, :],
                                 pw[:, 1, 0, :], pw[:, 1, 1, :], 1, t0)
                op(nc.vector.tensor_scalar(t1, pw[:, 1, 0, :], -1.0, None, ALU.add))
                mul(den, a_re, a_re, ALU.mult)
                mul(t0, a_im, a_im, ALU.mult)
                mul(den, den, t0, ALU.add)
                op(nc.vector.reciprocal(den, den))
                mul(f_re, t1, a_re, ALU.mult)
                mul(t0, pw[:, 1, 1, :], a_im, ALU.mult)
                mul(f_re, f_re, t0, ALU.add)
                mul(f_im, pw[:, 1, 1, :], a_re, ALU.mult)
                mul(t0, t1, a_im, ALU.mult)
                mul(f_im, f_im, t0, ALU.subtract)
                mul(f_re, f_re, den, ALU.mult)
                mul(f_im, f_im, den, ALU.mult)
                wide = lambda a: a.unsqueeze(2).broadcast_to([P, GP, CH])
                complex_step(dve, mul, bb[:, 0], bb[:, 1], bri[:, 0], bri[:, 1], wide(f_re), wide(f_im), 1, tmp)
                for j in range(9):
                    complex_step(dve, mul, cl[:, :, 0, j, :], cl[:, :, 1, j, :], cri[:, 0], cri[:, 1],
                                 wide(pw[:, j, 0, :]), wide(pw[:, j, 1, :]), -1, tmp)

        k_ready, k_free, k_d = sem("k_ready"), sem("k_free"), sem("k_d")
        toe_zero, toe_in = sem("toe_zero"), sem("toe_in")
        with nc.Block() as block:
            @block.gpsimd
            def _(pool):
                nc.gpsimd.memset(m_toe, 0.0).then_inc(toe_zero, 1)
                pool.wait_ge(toe_zero, 1)
                nc.gpsimd.memset(ua[64:P], 0.0).then_inc(toe_zero, 1)

            @block.tensor
            def _(pe):
                for q in range(G // 8):
                    if q >= 2:
                        pe.wait_ge(k_free, 2 * (q - 1))
                    for j in range(8):
                        gp, par_ = 4 * q + j // 2, j % 2
                        half = slice(64 * par_, 64 * par_ + 64)
                        for ri in range(2):
                            last = nc.tensor.matmul(ps[0:CH, 2 * (q % 2) + par_, j // 2 * P:(j // 2 + 1) * P],
                                                    bb[half, ri, gp, :], cl[half, gp, ri, 0:ST8, :],
                                                    start=(ri == 0), stop=(ri == 1))
                        if j >= 6:
                            last.then_inc(k_ready, 1)

            @block.scalar
            def _(act):
                for q in range(G // 8):
                    for par_ in range(2):
                        act.wait_ge(k_ready, 2 * q + 2)
                        nc.scalar.activation(kst[0:CH, 8 * q + par_:8 * q + 8:2].rearrange("p g t c -> p g (t c)"),
                                             ps[0:CH, 2 * (q % 2) + par_, :].rearrange("p (g m) -> p g m", g=4),
                                             ACT.Copy).then_inc(k_free, 1)

            @block.vector
            def _(dve):
                dd = lay(AT_HH, [G, CH])[0:CH]
                nc.vector.tensor_tensor(dd, ident[0:CH, 0:CH].unsqueeze(1).broadcast_to([CH, G, CH]),
                                        d_s5[0:CH].unsqueeze(2).broadcast_to([CH, G, CH]), ALU.mult).then_inc(k_d, 1)
                dve.wait_ge(k_d, 1)
                dve.wait_ge(k_free, G // 4)
                nc.vector.tensor_tensor(kst[0:CH, :, 0, :], kst[0:CH, :, 0, :], dd, ALU.add).then_inc(k_d, 1)

            @block.sync
            def _(sp):
                sp.wait_ge(k_d, 2)
                sp.wait_ge(toe_zero, 1)
                for s in range(ST8):
                    sp.dma_start(m_toe[s * CH:(s + 1) * CH, :, s * CH:P],
                                 kst[0:CH, :, 0:ST8 - s, :].rearrange("p g t c -> p g (t c)")).then_inc(toe_in, 16)
                sp.wait_ge(toe_in, 16 * ST8)

        st = lay(AT_HT, [2, 2, P])
        st4 = lay(AT_HT + 512, [2, 2, P])
        w_v, wT_ready, wT_free, se_ready, se_free = (sem(n) for n in ("w_v", "wT_ready", "wT_free", "se_ready", "se_free"))
        st_out = sem("st_out")
        with nc.Block() as block:
            @block.vector
            def _(dve):
                n = [0]

                def mul(o, a, b, how):
                    n[0] += 1
                    nc.vector.tensor_tensor(o, a, b, how).then_inc(w_v, 1)
                    dve.wait_ge(w_v, n[0])

                wide = lambda a: a.unsqueeze(2).broadcast_to([P, GP, CH])
                for s in range(ST8):
                    complex_step(dve, mul, wk[:, :, 0, s, :], wk[:, :, 1, s, :], bb[:, 0], bb[:, 1],
                                 wide(pw[:, 7 - s, 0, :]), wide(pw[:, 7 - s, 1, :]), 1, tmp)
                nc.vector.memset(neg_lam[:, 0:1], 1.0).then_inc(w_v, 1)
        NW = 6 * ST8

        with nc.Block() as block:
            @block.tensor
            def _(pe):
                def transposes(gp):
                    if gp >= 2:
                        pe.wait_ge(wT_free, gp - 1)
                    for ri in range(2):
                        nc.tensor.transpose(ps[:, gp % 2, ri * P:(ri + 1) * P], wk[:, gp, ri], ident[:, :])
                    for ri in range(2):
                        last = nc.tensor.transpose(ps[0:64, gp % 2, (2 + ri) * P:(3 + ri) * P],
                                                   wk[:, gp, ri, NNEW:ST8, :], ident[:, :])
                    last.then_inc(wT_ready, 1)

                transposes(0)
                for gp in range(GP):
                    if gp + 1 < GP:
                        transposes(gp + 1)
                    pe.wait_ge(wT_free, gp + 1)
                    if gp >= 2:
                        pe.wait_ge(se_free, gp - 1)
                    for par_ in range(2):
                        half = slice(64 * par_, 64 * par_ + 64)
                        for ri in range(2):
                            nc.tensor.matmul(ps[half, 2 + gp % 2, ri * P:(ri + 1) * P], st[:, gp % 2, ri, half],
                                             ug[:, 2 * gp + par_, :], start=True, stop=True)
                            last = nc.tensor.matmul(ps[half, 2 + gp % 2, 256 + ri * NSEQ:256 + (ri + 1) * NSEQ],
                                                    st4[0:64, gp % 2, ri, half], ua[0:64, 2 * gp + par_, :],
                                                    start=True, stop=True)
                    last.then_inc(se_ready, 1)

            @block.scalar
            def _(act):
                for gp in range(GP):
                    act.wait_ge(wT_ready, gp + 1)
                    if gp >= 2:
                        act.wait_ge(se_ready, gp - 1)
                    nc.scalar.activation(st[:, gp % 2].rearrange("p r m -> p (r m)"), ps[:, gp % 2, 0:256], ACT.Copy)
                    nc.scalar.activation(st4[0:64, gp % 2].rearrange("p r m -> p (r m)"), ps[0:64, gp % 2, 256:512],
                                         ACT.Copy).then_inc(wT_free, 1)

            @block.vector
            def _(dve):
                nc.vector.memset(hh[:, :, :, 0:1], 0.0).then_inc(w_v, 1)
                for gp in range(GP):
                    dve.wait_ge(se_ready, gp + 1)
                    nc.vector.tensor_copy(hs[:, :, gp, :], ps[:, 2 + gp % 2, 256:256 + 2 * NSEQ]
                                          .rearrange("p (r q) -> p r q", r=2)).then_inc(w_v, 1)
                    nc.vector.tensor_copy(hh[:, :, gp, 1:NCH + 1], ps[:, 2 + gp % 2, 0:256]
                                          .rearrange("p (r n) -> p r n", r=2)).then_inc(se_free, 1)

        rec = sem("rec")
        ta, tb = lay(AT_HT, [2, GP]), lay(AT_HT + 64, [2, GP])
        t8 = lay(AT_HT + 128, [GP, NSEQ])
        with nc.Block() as block:
            @block.vector
            def _(dve):
                l_re = pw[:, 8, 0, :].unsqueeze(1).broadcast_to([P, 2, GP])
                l_im = pw[:, 8, 1, :]
                with dve.Fori(0, NCH) as n:
                    now, nxt = hh[:, :, :, bass.ds(n, 1)], hh[:, :, :, bass.ds(n + 1, 1)]
                    sq = lambda a: a.rearrange("p r g o -> p r (g o)")
                    now, nxt = sq(now), sq(nxt)
                    dve.wait_ge(rec, n * 4)
                    nc.vector.tensor_tensor(ta, now, l_re, ALU.mult)
                    nc.vector.tensor_tensor(tb[:, 0, :], now[:, 1, :], l_im, ALU.mult)
                    nc.vector.tensor_tensor(tb[:, 1, :], now[:, 0, :], l_im, ALU.mult).then_inc(rec, 1)
                    dve.wait_ge(rec, n * 4 + 1)
                    nc.vector.tensor_tensor(nxt, nxt, ta, ALU.add).then_inc(rec, 1)
                    dve.wait_ge(rec, n * 4 + 2)
                    nc.vector.tensor_tensor(nxt[:, 0, :], nxt[:, 0, :], tb[:, 0, :], ALU.subtract).then_inc(rec, 1)
                    nc.vector.tensor_tensor(nxt[:, 1, :], nxt[:, 1, :], tb[:, 1, :], ALU.add).then_inc(rec, 1)
                wide = lambda a: a.unsqueeze(2).broadcast_to([P, GP, NSEQ])
                m = 4 * NCH
                for dst, src, lam_, how in ((0, 0, 0, ALU.add), (0, 1, 1, ALU.subtract), (1, 0, 1, ALU.add), (1, 1, 0, ALU.add)):
                    dve.wait_ge(rec, m)
                    nc.vector.tensor_tensor(t8, h0[:, src], wide(pw[:, NNEW, lam_, :]), ALU.mult).then_inc(rec, 1)
                    dve.wait_ge(rec, m + 1)
                    nc.vector.tensor_tensor(hs[:, dst], hs[:, dst], t8, how).then_inc(rec, 1)
                    m += 2

            @block.sync
            def _(sp):
                sp.wait_ge(rec, 4 * NCH + 8)
                sp.dma_start(out["s5_prompt"], hh[:, :, :, NCH:NCH + 1], allow_slow_non_contiguous=True).then_inc(st_out, 16)
                sp.dma_start(out["s5_sample"], hs.rearrange("p r g q -> p (r g q)")).then_inc(st_out, 16)
                sp.wait_ge(st_out, 32)

        zs_tok = lay(AT_HT, [NNEW, D])
        y_ready, y_free = sem("y_ready"), sem("y_free")
        with nc.Block() as block:
            @block.tensor
            def _(pe):
                for q in range(G // 8):
                    if q >= 2:
                        pe.wait_ge(y_free, 2 * (q - 1))
                    for j in range(8):
                        g, par_ = 8 * q + j, j % 2
                        half = slice(64 * par_, 64 * par_ + 64)
                        o = ps[:, 2 * (q % 2) + par_, j // 2 * P:(j // 2 + 1) * P]
                        nc.tensor.matmul(o, ug[:, g, :], m_toe[:, g, :], start=True, stop=False)
                        for ri in range(2):
                            last = nc.tensor.matmul(o, hh[half, ri, g // 2, 0:NCH], cl[half, g // 2, ri, 1:9, :],
                                                    start=False, stop=(ri == 1))
                        if j >= 6:
                            last.then_inc(y_ready, 1)
                for q in range(G // 16):
                    if q >= 2:
                        pe.wait_ge(y_free, G // 4 + 2 * (q - 1))
                    for j in range(16):
                        g, par_ = 16 * q + j, j % 2
                        half = slice(64 * par_, 64 * par_ + 64)
                        o = ps[0:NSEQ, 4 + 2 * (q % 2) + par_, j // 2 * 64:(j // 2 + 1) * 64]
                        nc.tensor.matmul(o, ua[:, g, :], m_toe[:, g, 0:64], start=True, stop=False)
                        for ri in range(2):
                            last = nc.tensor.matmul(o, h0[half, ri, g // 2, :], cl[half, g // 2, ri, 1:1 + NNEW, :],
                                                    start=False, stop=(ri == 1))
                        if j >= 14:
                            last.then_inc(y_ready, 1)

            @block.scalar
            def _(act):
                z_g = z_tok.rearrange("p t (g c) -> p t g c", c=CH)
                for q in range(G // 8):
                    for par_ in range(2):
                        act.wait_ge(y_ready, 2 * q + 2)
                        for t in range(ST8):
                            last = nc.scalar.activation(
                                z_g[:, t, 8 * q + par_:8 * q + 8:2],
                                ps[:, 2 * (q % 2) + par_, :].rearrange("p (g t c) -> p t g c", g=4, t=ST8)[:, t], ACT.Gelu)
                        last.then_inc(y_free, 1)
                zs_g = zs_tok.rearrange("p t (g c) -> p t g c", c=CH)
                for q in range(G // 16):
                    for par_ in range(2):
                        act.wait_ge(y_ready, G // 4 + 2 * q + 2)
                        for t in range(NNEW):
                            last = nc.scalar.activation(
                                zs_g[0:NSEQ, t, 16 * q + par_:16 * q + 16:2],
                                ps[0:NSEQ, 4 + 2 * (q % 2) + par_, :].rearrange("p (g t c) -> p t g c", g=8, t=NNEW)[:, t],
                                ACT.Gelu)
                        last.then_inc(y_free, 1)

        AT_ZT, AT_S5O, AT_MT, AT_WB = 0, AT_TOE, AT_TOE + KC * T, AT_WK
        zT = lay(AT_ZT, [KC, T])
        z_ready, z_free = sem("z_ready"), sem("z_free")
        with nc.Block() as block:
            @block.tensor
            def _(pe):
                for n in range(2 * KC):
                    c, b = n // 2, n % 2
                    if n >= 4:
                        pe.wait_ge(z_free, n - 3)
                    for s in range(4):
                        last = nc.tensor.transpose(ps[:, n % 4, s * P:(s + 1) * P],
                                                   z_tok[:, 4 * b + s, c * P:(c + 1) * P], ident[:, :])
                    last.then_inc(z_ready, 1)
                for c in range(KC):
                    for t in range(NNEW):
                        last = nc.tensor.transpose(ps[:, 4, c * NS + t * NSEQ:c * NS + (t + 1) * NSEQ],
                                                   zs_tok[0:NSEQ, t, c * P:(c + 1) * P], ident[0:NSEQ, 0:NSEQ])
                last.then_inc(z_ready, 1)

            @block.vector
            def _(dve):
                for n in range(2 * KC):
                    c, b = n // 2, n % 2
                    dve.wait_ge(z_ready, n + 1)
                    nc.vector.tensor_copy(zT[:, c, 0:SEQ].rearrange("p (n s) -> p s n", s=ST8)[:, 4 * b:4 * b + 4],
                                          ps[:, n % 4, :].rearrange("p (s n) -> p s n", s=4)).then_inc(z_free, 1)
                dve.wait_ge(z_ready, 2 * KC + 1)
                for c in range(KC):
                    last = nc.vector.tensor_copy(zT[:, c, SEQ:T].rearrange("p (q t) -> p t q", t=NNEW),
                                                 ps[:, 4, c * NS:(c + 1) * NS].rearrange("p (t q) -> p t q", t=NNEW))
                last.then_inc(z_free, 1)

        wbuf = lay(AT_WB, [2, D])
        gate = lay(AT_WB + 2 * D, [2, NC3, CW])
        mul_t = lay(AT_WB + 2 * D + 2 * NC3 * CW, [CW])
        s5oT = lay(AT_S5O, [KC, T])
        mT = lay(AT_MT, [KC, T])
        gl_ready, gl_used, hT_back = sem("gl_ready"), sem("gl_used"), sem("hT_back")
        chunk = lambda c: slice(c * CW, (c + 1) * CW)

        def one(a):
            return a.rearrange("p a n -> p (a n)")

        NGLU = KC // 2
        with nc.Block() as block:
            @block.sync
            def _(sp):
                sp.dma_start(hT.rearrange("p c t -> p (c t)"), scr_h).then_inc(hT_back, 16)
                stat_loads(sp, wbuf, T_GLU, NGLU, pairs)
                sp.wait_ge(hT_back, 16)

            @block.tensor
            def _(pe):
                with pe.Fori(0, NGLU) as i:
                    for k in range(2):
                        stat_products(pe, i, k, wbuf, zT, pairs)

            @block.scalar
            def _(act):
                with act.Fori(0, NGLU) as i:
                    for k in range(2):
                        for c in range(NC3):
                            act.wait_ge(acc_ready[k], i * 3 + (3 * pairs + c + 1))
                            act.wait_ge(gl_used, START + i * 6)
                            alone(act)
                            nc.scalar.activation(gate[:, k, c, :], ps[:, 3 * k + c, 0:CW], ACT.Sigmoid,
                                                 bias=b_glu[:, bass.ds(i * 2 + k, 1)]).then_inc(acc_free[k], 1)

            @block.vector
            def _(dve):
                with dve.Fori(0, NGLU) as i:
                    for k in range(2):
                        for c in range(NC3):
                            dve.wait_ge(acc_free[k], i * 3 + (3 * pairs + c + 4))
                            m = bass.ds(i * 2 + k, 1)
                            nc.vector.tensor_tensor(one(s5oT[:, m, chunk(c)]), one(zT[:, m, chunk(c)]), gate[:, k, c, :],
                                                    ALU.mult).then_inc(gl_used, 1)
        pairs += NGLU

        prod = sem("prod")

        def merge(block, tile0, other, fold, pairs):
            @block.sync
            def _(sp):
                stat_loads(sp, wbuf, tile0, KC, pairs)

            @block.tensor
            def _(pe):
                with pe.Fori(0, KC) as i:
                    stat_products(pe, i, 0, wbuf, hT, pairs)
                    stat_products(pe, i, 1, wbuf, other, pairs)

            @block.scalar
            def _(act):
                with act.Fori(0, KC) as i:
                    for c in range(NC3):
                        act.wait_ge(acc_ready[0], i * 3 + (3 * pairs + c + 1))
                        act.wait_ge(acc_free[1], i * 3 + (3 * pairs + 3))
                        nc.scalar.activation(gate[:, 0, c, :], ps[:, c, 0:CW], ACT.Sigmoid).then_inc(acc_free[0], 1)

            @block.vector
            def _(dve):
                with dve.Fori(0, KC) as i:
                    for c in range(NC3):
                        dve.wait_ge(acc_free[0], i * 3 + (3 * pairs + c + 4))
                        dve.wait_ge(acc_ready[1], i * 3 + (3 * pairs + c + 1))
                        dst = one(mT[:, bass.ds(i, 1), chunk(c)])
                        if not fold:
                            nc.vector.tensor_tensor(dst, ps[:, 3 + c, 0:CW], gate[:, 0, c, :], ALU.mult).then_inc(acc_free[1], 1)
                            continue
                        dve.wait_ge(prod, START + i * 3 + c)
                        nc.vector.tensor_tensor(mul_t, ps[:, 3 + c, 0:CW], gate[:, 0, c, :], ALU.mult).then_inc(acc_free[1], 1)
                        dve.wait_ge(acc_free[1], i * 3 + (3 * pairs + c + 4))
                        nc.vector.tensor_tensor(dst, dst, mul_t, ALU.add).then_inc(prod, 1)

        with nc.Block() as block:
            merge(block, T_GS, s5oT, False, pairs)
        pairs += KC

        attT = lay(0, [KC, T])
        AT_MISC, AT_V = KC * T, AT_MT + KC * T
        vall = lay(AT_V, [TT + 1, D])
        v_slab = lay(AT_WB, [2, KC, 512])
        vs_in = [sem(f"vs_in{k}") for k in range(2)]
        v_ready, v_free, v_out = sem("v_ready"), sem("v_free"), sem("v_out")

        def token_rows(t):
            return (P if t < TT else NS), slice(t * P, t * P + (P if t < TT else NS))

        with nc.Block() as block:
            @block.sync
            def _(sp):
                for k in range(2):
                    sp.dma_start(v_slab[:, k].rearrange("p a b -> p (a b)"), dr["w_mov"][2 + k]).then_inc(vs_in[k], 16)
                for t in range(TT + 1):
                    rows, tok = token_rows(t)
                    sp.wait_ge(v_free, 2 * t + 2)
                    sp.dma_start(out["v"][tok, :], vall[0:rows, t, :]).then_inc(v_out, 16)
                sp.wait_ge(v_out, 16 * (TT + 1))

            @block.tensor
            def _(pe):
                for k in range(2):
                    pe.wait_ge(vs_in[k], 16)
                for t in range(TT + 1):
                    rows, tok = token_rows(t)
                    for k in range(2):
                        n = 2 * t + k
                        if n >= 8:
                            pe.wait_ge(v_free, n - 7)
                        for kc in range(KC):
                            last = nc.tensor.matmul(ps[0:rows, n % 8, :], hT[:, kc, tok], v_slab[:, k, kc, :],
                                                    start=(kc == 0), stop=(kc == KC - 1))
                        last.then_inc(v_ready, 1)

            @block.scalar
            def _(act):
                for t in range(TT + 1):
                    rows, tok = token_rows(t)
                    for k in range(2):
                        act.wait_ge(v_ready, 2 * t + k + 1)
                        nc.scalar.activation(vall[0:rows, t, 512 * k:512 * (k + 1)], ps[0:rows, (2 * t + k) % 8, :],
                                             ACT.Copy).then_inc(v_free, 1)

        A = AT_MISC
        qh, kh = lay(A, [T]), lay(A + T, [T])
        qs, ks = lay(A + 2 * T, [H, NS]), lay(A + 2 * T + 256, [H, NS])
        A += 2 * T + 512
        ex = lay(A, [2, 2, SEQ])
        A += 4 * SEQ
        pT = lay(A, [SEQ // P, P])
        A += SEQ
        osb = lay(A, [TT, P])
        A += SEQ
        nmax, lsum, ssq, subln = lay(A, [2, 2]), lay(A + 4, [2, 2]), lay(A + 8, [TT]), lay(A + 16, [1])
        assert A + 17 <= AT_MT
        causal = lay(AT_WB + 2 * D, [P])
        ko = lay(AT_WB + 2 * D + P, [TT + 1, P])
        junk_a = lay(AT_WB + 2 * D + P + 9 * P, [P])

        names = ("ko_ready", "ko_free", "ko_out", "ko_clear", "s_ready", "s_masked", "m_ready", "e_ready", "l_ready", "p_ready",
                 "t_ready", "t_free", "o_ready", "o_free", "ss_ready", "rt_ready", "on_ready", "oT_ready", "oT_free",
                 "at_in", "qs_ready", "part")
        (ko_ready, ko_free, ko_out, ko_clear, s_ready, s_masked, m_ready, e_ready, l_ready, p_ready, t_ready, t_free,
         o_ready, o_free, ss_ready, rt_ready, on_ready, oT_ready, oT_free, at_in, qs_ready, part) = (sem(n) for n in names)
        with nc.Block() as block:
            @block.sync
            def _(sp):
                sp.dma_start(causal, dr["causal"]).then_inc(at_in, 16)
                sp.dma_start(subln, dr["subln"]).then_inc(at_in, 16)
                for k in range(2):
                    stat_load(sp, wbuf, k, dr["w_stat"][T_QK + k])
                def k_out(h):
                    sp.wait_ge(ko_free, h * 3 + 3)
                    col = bass.ds(h * P, P)
                    sp.dma_start(out["k"][0:SEQ, col].rearrange("(t p) n -> p t n", p=P), ko[:, 0:TT, :]).then_inc(ko_out, 16)
                    sp.dma_start(out["k"][SEQ:T, col], ko[0:NS, TT, :]).then_inc(ko_out, 16)
                    sp.wait_ge(ko_out, h * 32 + 32)
                    sp.sem_inc(ko_clear, 1)

                with sp.Fori(0, H - 1) as h:
                    k_out(h)
                    for k in range(2):
                        sp.wait_ge(acc_ready[k], h * 3 + 3 * (pairs + 1))
                        stat_load(sp, wbuf, k, dr["w_stat"][bass.ds(h * 2 + (T_QK + 2 + k), 1)].rearrange("a p n -> (a p) n"))
                k_out(H - 1)

            @block.tensor
            def _(pe):
                def scores(h, i):
                    n = h * TT + i
                    if i:
                        pe.wait_ge(e_ready, h * 16 + 2 * i)
                    for b in range(2):
                        half = slice(64 * b, 64 * b + 64)
                        for c in range((i // 4) + 1):
                            w = min(512, (i + 1) * P - 512 * c)
                            last = nc.tensor.matmul(ps[:, 2 * b + c, 0:w], qh[half, i * P:(i + 1) * P],
                                                    kh[half, 512 * c:512 * c + w], start=True, stop=True)
                    last.then_inc(s_ready, 1)

                with pe.Fori(0, H) as h:
                    pe.wait_ge(oT_free, START + h * 2)
                    stat_products(pe, h, 0, wbuf, hT, pairs)
                    stat_products(pe, h, 1, wbuf, hT, pairs)
                    for k in range(2):
                        pe.wait_ge(acc_free[k], h * 3 + (3 * pairs + 6))
                    for r in range(3):
                        if r == 2:
                            pe.wait_ge(ko_free, h * 3 + 1)
                        for t in range(4 * r, min(4 * r + 4, TT + 1)):
                            rows, tok = token_rows(t)
                            last = nc.tensor.transpose(ps[0:rows, 6 + r % 2, (t % 4) * P:(t % 4 + 1) * P], kh[:, tok], ident[:, :])
                        last.then_inc(ko_ready, 1)
                    pe.wait_ge(ko_free, h * 3 + 3)
                    scores(h, 0)
                    for i in range(TT):
                        if i + 1 < TT:
                            scores(h, i + 1)
                        pe.wait_ge(p_ready, h * TT + (i + 1))
                        pe.wait_ge(t_free, START + h * TT + i)
                        for j in range(i + 1):
                            last = nc.tensor.transpose(ps[:, 4 + j // 4, (j % 4) * P:(j % 4 + 1) * P],
                                                       ex[:, i % 2, 0, j * P:(j + 1) * P], ident[:, :])
                        last.then_inc(t_ready, 1)
                        pe.wait_ge(t_free, START + h * TT + (i + 1))
                        for j in range(i + 1):
                            last = nc.tensor.matmul(ps[:, 6 + i // 4, (i % 4) * P:(i % 4 + 1) * P], pT[:, j, :],
                                                    vall[:, j, bass.ds(h * P, P)], start=(j == 0), stop=(j == i))
                        last.then_inc(o_ready, 1)
                    pe.wait_ge(on_ready, h + 1)
                    for r in range(2):
                        for t in range(4 * r, 4 * r + 4):
                            last = nc.tensor.transpose(ps[:, 6 + r, (t % 4) * P:(t % 4 + 1) * P], osb[:, t, :], ident[:, :])
                        last.then_inc(oT_ready, 1)

            @block.scalar
            def _(act):
                act.wait_ge(at_in, 32)
                with act.Fori(0, H) as h:
                    for c in range(NC3):
                        act.wait_ge(acc_ready[0], h * 3 + (3 * pairs + c + 1))
                        nc.scalar.activation(qh[:, chunk(c)], ps[:, c, 0:CW], ACT.Copy, scale=HD ** -0.5).then_inc(acc_free[0], 1)
                    act.wait_ge(ko_clear, START + h)
                    for r in range(3):
                        act.wait_ge(ko_ready, h * 3 + (r + 1))
                        if r < 2:
                            nc.scalar.activation(ko[:, 4 * r:4 * r + 4].rearrange("p t n -> p (t n)"), ps[:, 6 + r, :],
                                                 ACT.Copy).then_inc(ko_free, 1)
                        else:
                            nc.scalar.activation(ko[0:NS, TT, :], ps[0:NS, 6, 0:P], ACT.Copy).then_inc(ko_free, 1)

                    def exps(i):
                        act.wait_ge(m_ready, h * TT + (i + 1))
                        if i >= 2:
                            act.wait_ge(t_ready, h * TT + (i - 1))
                        for b in range(2):
                            nc.scalar.activation(ex[:, i % 2, b, 0:(i + 1) * P],
                                                 ps[:, 2 * b:2 * b + 2, :].rearrange("p a n -> p (a n)")[:, 0:(i + 1) * P],
                                                 ACT.Exp, bias=nmax[:, i % 2, b:b + 1],
                                                 accum_out=lsum[:, i % 2, b:b + 1]).then_inc(e_ready, 1)

                    exps(0)
                    for i in range(TT):
                        act.wait_ge(t_ready, h * TT + (i + 1))
                        if i:
                            act.wait_ge(o_ready, h * TT + i)
                        nc.scalar.activation(pT[:, 0:i + 1, :].rearrange("p j n -> p (j n)"),
                                             ps[:, 4:6, :].rearrange("p a n -> p (a n)")[:, 0:(i + 1) * P],
                                             ACT.Copy).then_inc(t_free, 1)
                        if i + 1 < TT:
                            exps(i + 1)
                    act.wait_ge(ss_ready, h + 1)
                    nc.scalar.activation(ssq, ssq, ACT.Sqrt).then_inc(rt_ready, 1)
                    for r in range(2):
                        act.wait_ge(oT_ready, h * 2 + (r + 1))
                        nc.scalar.activation(one(attT[:, bass.ds(h, 1), 512 * r:512 * (r + 1)]), ps[:, 6 + r, :], ACT.Copy,
                                             scale=subln).then_inc(oT_free, 1)

            @block.vector
            def _(dve):
                dve.wait_ge(at_in, 32)
                with dve.Fori(0, H) as h:
                    for c in range(NC3):
                        dve.wait_ge(acc_ready[1], h * 3 + (3 * pairs + c + 1))
                        nc.vector.tensor_copy(kh[:, chunk(c)], ps[:, 3 + c, 0:CW]).then_inc(acc_free[1], 1)
                    dve.wait_ge(acc_free[0], h * 3 + (3 * pairs + 6))
                    dve.wait_ge(acc_free[1], h * 3 + (3 * pairs + 6))
                    nc.vector.tensor_copy(one(qs[:, bass.ds(h, 1), :]), qh[:, SEQ:T])
                    nc.vector.tensor_copy(one(ks[:, bass.ds(h, 1), :]), kh[:, SEQ:T]).then_inc(qs_ready, 1)

                    def maxima(i):
                        dve.wait_ge(s_ready, h * TT + (i + 1))
                        both = ps[:, 0:4, :].rearrange("p (b a) n -> p b (a n)", b=2)
                        diag = both[:, :, i * P:(i + 1) * P]
                        nc.vector.tensor_tensor(diag, diag, causal.unsqueeze(1).broadcast_to([P, 2, P]),
                                                ALU.add).then_inc(s_masked, 1)
                        dve.wait_ge(s_masked, h * TT + (i + 1))
                        nc.vector.tensor_reduce(nmax[:, i % 2, :], both[:, :, 0:(i + 1) * P], AX.X, ALU.max,
                                                negate=True).then_inc(m_ready, 1)

                    maxima(0)
                    for i in range(TT):
                        dve.wait_ge(e_ready, h * 16 + (2 * i + 2))
                        nc.vector.reciprocal(lsum[:, i % 2, :], lsum[:, i % 2, :]).then_inc(l_ready, 1)
                        dve.wait_ge(l_ready, h * 3 * TT + (3 * i + 1))
                        nc.vector.tensor_tensor(lsum[:, i % 2, :], lsum[:, i % 2, :], neg_lam[:, :], ALU.mult).then_inc(l_ready, 1)
                        dve.wait_ge(l_ready, h * 3 * TT + (3 * i + 2))
                        e0, e1 = ex[:, i % 2, 0, 0:(i + 1) * P], ex[:, i % 2, 1, 0:(i + 1) * P]
                        nc.vector.tensor_scalar(e0, e0, lsum[:, i % 2, 0:1], None, ALU.mult).then_inc(l_ready, 1)
                        dve.wait_ge(l_ready, h * 3 * TT + (3 * i + 3))
                        nc.vector.scalar_tensor_tensor(e0, e1, lsum[:, i % 2, 1:2], e0, ALU.mult, ALU.add).then_inc(p_ready, 1)
                        if i + 1 < TT:
                            maxima(i + 1)
                        dve.wait_ge(o_ready, h * TT + (i + 1))
                        nc.vector.tensor_copy(osb[:, i, :], ps[:, 6 + i // 4, (i % 4) * P:(i % 4 + 1) * P]).then_inc(o_free, 1)
                        dve.wait_ge(o_free, h * TT + (i + 1))
                        nc.vector.tensor_tensor_reduce(junk_a, osb[:, i, :], osb[:, i, :], 1.0, 0.0, ALU.mult, ALU.add,
                                                       ssq[:, i:i + 1]).then_inc(part, 1)
                    dve.wait_ge(part, h * TT + TT)
                    s2 = (1.0 - LAM_INIT) ** 2
                    nc.vector.tensor_scalar(ssq, ssq, 1 / (P * s2), EPS / s2, ALU.mult, ALU.add).then_inc(ss_ready, 1)
                    dve.wait_ge(rt_ready, h * 2 + 1)
                    nc.vector.reciprocal(ssq, ssq).then_inc(rt_ready, 1)
                    dve.wait_ge(rt_ready, h * 2 + 2)
                    nc.vector.tensor_tensor(osb, osb, ssq.unsqueeze(2).broadcast_to([P, TT, P]), ALU.mult).then_inc(on_ready, 1)
        pairs += H

        NK = SEQ + NS
        ROWS = 2 * H * NNEW
        vpg = lay(AT_V, [PAGES, D])
        v_new = vall[0:NS, TT, :]
        B = AT_MISC + 2 * T + 512
        qpad = lay(B, [H * (ROWS + 8)])
        es, pTs, o4 = lay(B + 576, [NK]), lay(B + 576 + NK, [PAGES + 1, NS]), lay(B + 576 + NK + 288, [D])
        B += 576 + NK + 288 + D
        sgn, c_new, nm_s, l_s, t_s, first_s = (lay(B + j, [1]) for j in range(6))
        pgs, pgv = lay(B + 8, [NSEQ * PAGES], I32), lay(B + 80, [NSEQ * PAGES], I32)
        ss_s = lay(B + 160, [H])
        kpg, kT = lay(AT_WB, [2, D]), lay(AT_WB + 2 * D, [2, H, P])
        C = AT_WB + 4 * D
        causal_new, pick = lay(C, [NSEQ, NS]), lay(C + 256, [NS])
        osm, osq = lay(C + 288, [H, P]), lay(C + 288 + D, [H, P])
        scr_o = nc.dram_tensor("scr_o", (NS, D), F32, kind="Internal").ap()
        n_phys = dr["cache_k"].shape[0]

        names = ("sc_in", "pg_in", "pgv_in", "vp_in", "q_zero", "qp_ready", "kt_ready", "kt_free", "page_used", "sn_ready",
                 "sn_masked", "mn_ready", "en_ready", "ln_ready", "pn_ready", "ptn_ready", "ptn_free", "on_acc", "on_free",
                 "o_out", "sgn_v")
        (sc_in, pg_in, pgv_in, vp_in, q_zero, qp_ready, kt_ready, kt_free, page_used, sn_ready, sn_masked, mn_ready, en_ready,
         ln_ready, pn_ready, ptn_ready, ptn_free, on_acc, on_free, o_out, sgn_v) = (sem(n) for n in names)
        kp_in = [sem(f"kp_in{k}") for k in range(2)]
        flat_s = ps[0:ROWS, 4:7, :].rearrange("p a n -> p (a n)")
        with nc.Block() as block:
            @block.sync
            def _(sp):
                sp.dma_start(causal_new[0:ROWS].rearrange("p a b -> p (a b)"), dr["causal_new"]).then_inc(sc_in, 16)
                sp.dma_start(pick[0:ROWS, :], dr["pick"]).then_inc(sc_in, 16)
                sp.dma_start(first_s[0:ROWS, :], dr["first"]).then_inc(sc_in, 16)
                sp.dma_start(pgs[0:1, :], dr["pages"]).then_inc(pg_in, 16)
                sp.wait_ge(pg_in, 16)
                with sp.Fori(0, NSEQ) as s:
                    for p in range(PAGES):
                        page = sp.value_load(pgs[0:1, bass.ds(s * PAGES + p, 1)], min_val=0, max_val=n_phys - 1)
                        if p < 2:
                            sp.wait_ge(kt_ready, START + s * PAGES)
                        else:
                            sp.wait_ge(kt_ready, START + s * PAGES + (p - 1))
                        sp.dma_start(kpg[:, p % 2, :], dr["cache_k"][bass.ds(page, 1)].rearrange("a p n -> (a p) n")
                                     ).then_inc(kp_in[p % 2], 16)

            @block.gpsimd
            def _(pool):
                pool.dma_start(pgv[0:1, :], dr["pages"]).then_inc(pgv_in, 16)
                pool.wait_ge(pgv_in, 16)
                with pool.Fori(0, NSEQ) as s:
                    pool.wait_ge(on_acc, START + s)
                    for p in range(PAGES):
                        page = pool.value_load(pgv[0:1, bass.ds(s * PAGES + p, 1)], min_val=0, max_val=n_phys - 1)
                        pool.dma_start(vpg[:, p, :], dr["cache_v"][bass.ds(page, 1)].rearrange("a p n -> (a p) n")
                                       ).then_inc(vp_in, 16)

            @block.tensor
            def _(pe):
                pe.wait_ge(sc_in, 48)
                with pe.Fori(0, NSEQ) as s:
                    def page_scores(p):
                        pe.wait_ge(kt_free, START + s * PAGES + (p + 1))
                        for h in range(H):
                            last = nc.tensor.matmul(flat_s[:, p * P:(p + 1) * P], qpad[:, h * ROWS:(h + 1) * ROWS],
                                                    kT[:, p % 2, h, :], start=(h == 0), stop=(h == H - 1))
                        last.then_inc(page_used, 1)

                    pe.wait_ge(on_free, START + s)
                    pe.wait_ge(qp_ready, s + 1)
                    pe.wait_ge(en_ready, START + s)
                    for p in range(PAGES):
                        pe.wait_ge(kp_in[p % 2], s * 64 + 16 * (p // 2 + 1))
                        pe.wait_ge(kt_free, START + s * PAGES + max(p - 1, 0))
                        for h in range(H):
                            last = nc.tensor.transpose(ps[:, 2 * (p % 2) + h // 4, (h % 4) * P:(h % 4 + 1) * P],
                                                       kpg[:, p % 2, h * P:(h + 1) * P], ident[:, :])
                        last.then_inc(kt_ready, 1)
                        if p:
                            page_scores(p - 1)
                    page_scores(PAGES - 1)
                    for h in range(H):
                        last = nc.tensor.matmul(flat_s[:, SEQ:NK], qpad[:, h * ROWS:(h + 1) * ROWS], ks[:, h, :],
                                                start=(h == 0), stop=(h == H - 1))
                    last.then_inc(sn_ready, 1)
                    pe.wait_ge(pn_ready, s + 1)
                    pe.wait_ge(ptn_free, START + s)
                    for p in range(PAGES + 1):
                        w = P if p < PAGES else NS
                        last = nc.tensor.matmul(ps[0:w, 7, p * NS:(p + 1) * NS], es[0:ROWS, p * P:p * P + w], pick[0:ROWS, :],
                                                start=True, stop=True)
                    last.then_inc(ptn_ready, 1)
                    pe.wait_ge(ptn_free, START + s + 1)
                    pe.wait_ge(vp_in, (s + 1) * 16 * PAGES)
                    for h in range(H):
                        o = ps[0:NNEW, h // 4, (h % 4) * P:(h % 4 + 1) * P]
                        cols = slice(h * P, (h + 1) * P)
                        for p in range(PAGES):
                            nc.tensor.matmul(o, pTs[:, p, NNEW * h:NNEW * (h + 1)], vpg[:, p, cols], start=(p == 0), stop=False)
                        last = nc.tensor.matmul(o, pTs[0:NS, PAGES, NNEW * h:NNEW * (h + 1)], v_new[:, cols], start=False, stop=True)
                    last.then_inc(on_acc, 1)

            @block.scalar
            def _(act):
                with act.Fori(0, NSEQ) as s:
                    for p in range(PAGES):
                        act.wait_ge(kt_ready, START + s * PAGES + (p + 1))
                        act.wait_ge(page_used, START + s * PAGES + max(p - 1, 0))
                        nc.scalar.activation(kT[:, p % 2].rearrange("p h n -> p (h n)"),
                                             ps[:, 2 * (p % 2):2 * (p % 2) + 2, :].rearrange("p a n -> p (a n)"),
                                             ACT.Copy).then_inc(kt_free, 1)
                    act.wait_ge(mn_ready, s + 1)
                    act.wait_ge(ptn_ready, START + s)
                    nc.scalar.activation(es[0:ROWS, :], flat_s[:, 0:NK], ACT.Exp, bias=nm_s[0:ROWS, :],
                                         accum_out=l_s[0:ROWS, :]).then_inc(en_ready, 1)
                    act.wait_ge(on_free, START + s + 1)
                    act.dma_start(scr_o[bass.ds(s * NNEW, NNEW), :], o4[0:NNEW, :]).then_inc(o_out, 16)
                    act.wait_ge(o_out, s * 16 + 16)

            @block.vector
            def _(dve):
                nc.vector.memset(qpad, 0.0).then_inc(q_zero, 1)
                dve.wait_ge(q_zero, 1)
                dve.wait_ge(sc_in, 48)
                nl = neg_lam[0:ROWS, 1:2]
                nc.vector.tensor_scalar(t_s[0:ROWS, :], nl, -1.0, 1.0, ALU.mult, ALU.add).then_inc(sgn_v, 1)
                dve.wait_ge(sgn_v, 1)
                nc.vector.tensor_scalar(sgn[0:ROWS, :], first_s[0:ROWS, :], t_s[0:ROWS, 0:1], nl, ALU.mult, ALU.add).then_inc(sgn_v, 1)
                dve.wait_ge(sgn_v, 2)
                diag = qpad.rearrange("p (h x) -> p h x", x=ROWS + 2 * NNEW)
                with dve.Fori(0, NSEQ) as s:
                    dve.wait_ge(sn_ready, START + s)
                    for b in range(2):
                        half = slice(64 * b, 64 * b + 64)
                        last = nc.vector.tensor_copy(diag[half, :, NNEW * b:NNEW * (b + 1)], qs[half, :, bass.ds(s * NNEW, NNEW)])
                    last.then_inc(qp_ready, 1)
                    dve.wait_ge(sn_ready, START + s + 1)
                    new = flat_s[:, SEQ:NK]
                    nc.vector.tensor_tensor(new, new, one(causal_new[0:ROWS, bass.ds(s, 1), :]), ALU.add).then_inc(sn_masked, 1)
                    dve.wait_ge(sn_masked, s + 1)
                    nc.vector.tensor_reduce(nm_s[0:ROWS, :], flat_s[:, 0:NK], AX.X, ALU.max, negate=True).then_inc(mn_ready, 1)
                    dve.wait_ge(en_ready, START + s + 1)
                    nc.vector.reciprocal(l_s[0:ROWS, :], l_s[0:ROWS, :]).then_inc(ln_ready, 1)
                    dve.wait_ge(ln_ready, s * 2 + 1)
                    nc.vector.tensor_tensor(c_new[0:ROWS, :], l_s[0:ROWS, :], sgn[0:ROWS, :], ALU.mult).then_inc(ln_ready, 1)
                    dve.wait_ge(ln_ready, s * 2 + 2)
                    nc.vector.tensor_scalar(es[0:ROWS, :], es[0:ROWS, :], c_new[0:ROWS, 0:1], None, ALU.mult).then_inc(pn_ready, 1)
                    dve.wait_ge(ptn_ready, START + s + 1)
                    dve.wait_ge(on_acc, START + s)
                    nc.vector.tensor_copy(pTs[:, 0:PAGES, :].rearrange("p a b -> p (a b)"), ps[:, 7, 0:PAGES * NS])
                    nc.vector.tensor_copy(pTs[0:NS, PAGES, :], ps[0:NS, 7, PAGES * NS:(PAGES + 1) * NS]).then_inc(ptn_free, 1)
                    dve.wait_ge(on_acc, START + s + 1)
                    nc.vector.tensor_copy(o4[0:NNEW, :], ps[0:NNEW, 0:2, :].rearrange("p a n -> p (a n)")).then_inc(on_free, 1)

        os_in, n_v, n_a, n_pe = sem("os_in"), sem("n_v"), sem("n_a"), sem("n_pe")
        with nc.Block() as block:
            @block.sync
            def _(sp):
                sp.dma_start(osm[0:NS].rearrange("p h n -> p (h n)"), scr_o).then_inc(os_in, 16)

            @block.vector
            def _(dve):
                dve.wait_ge(os_in, 16)
                o, q, r = osm[0:NS], osq[0:NS], ss_s[0:NS]
                s2 = (1.0 - LAM_INIT) ** 2
                nc.vector.tensor_tensor(q, o, o, ALU.mult).then_inc(n_v, 1)
                dve.wait_ge(n_v, 1)
                nc.vector.tensor_reduce(r, q, AX.X, ALU.add).then_inc(n_v, 1)
                dve.wait_ge(n_v, 2)
                nc.vector.tensor_scalar(r, r, 1 / (P * s2), EPS / s2, ALU.mult, ALU.add).then_inc(n_v, 1)
                dve.wait_ge(n_a, 1)
                nc.vector.reciprocal(r, r).then_inc(n_v, 1)
                dve.wait_ge(n_v, 4)
                nc.vector.tensor_tensor(o, o, r.unsqueeze(2).broadcast_to([NS, H, P]), ALU.mult).then_inc(n_v, 1)

            @block.tensor
            def _(pe):
                pe.wait_ge(n_v, 5)
                for h in range(H):
                    last = nc.tensor.transpose(ps[:, 0, h * NS:(h + 1) * NS], osm[0:NS, h, :], ident[0:NS, 0:NS])
                last.then_inc(n_pe, 1)

            @block.scalar
            def _(act):
                act.wait_ge(n_v, 3)
                nc.scalar.activation(ss_s[0:NS], ss_s[0:NS], ACT.Sqrt).then_inc(n_a, 1)
                act.wait_ge(n_pe, 1)
                nc.scalar.activation(attT[:, :, SEQ:T], ps[:, 0, 0:H * NS].rearrange("p (h t) -> p h t", h=H), ACT.Copy,
                                     scale=subln).then_inc(n_a, 1)

        with nc.Block() as block:
            merge(block, T_GA, attT, True, pairs)
        pairs += KC

        h2T = lay(AT_V, [KC, T])
        o_slab = lay(AT_WB, [2, KC, 512])
        xr, x1, hn = lay(0, [2, D]), lay(2 * D, [2, D]), lay(4 * D, [2, D])
        hg, g_row, junk6, ss6 = lay(6 * D, [2, D]), lay(8 * D, [D]), lay(9 * D, [D]), lay(10 * D, [2])
        scr_x1 = nc.dram_tensor("scr_x1", (T, D), F32, kind="Internal").ap()
        scr_h2 = nc.dram_tensor("scr_h2", (T, D), F32, kind="Internal").ap()
        xs_in = [sem(f"xs_in{k}") for k in range(2)]
        os_w, gr_in = sem("os_w"), sem("gr_in")
        x1_acc, x1_ready, sq6, ms6, rt6, rc6, hn_ready, hT_acc, hT_out, hg_ready = (
            sem(n) for n in ("x1_acc", "x1_ready", "sq6", "ms6", "rt6", "rc6", "hn_ready", "hT_acc", "hT_out", "hg_ready"))
        x1_out = [sem(f"x1_out{k}") for k in range(2)]
        with nc.Block() as block:
            @block.sync
            def _(sp):
                for k in range(2):
                    sp.dma_start(o_slab[:, k].rearrange("p a b -> p (a b)"), dr["w_mov"][4 + k]).then_inc(os_w, 16)
                sp.dma_start(g_row, dr["g_ffn_row"].broadcast_to([P, D])).then_inc(gr_in, 16)
                for t in range(TT + 1):
                    rows, tok = token_rows(t)
                    if t >= 2:
                        sp.wait_ge(x1_ready, t - 1)
                    sp.dma_start(xr[0:rows, t % 2, :], dr["x"][tok, :]).then_inc(xs_in[t % 2], 16)
                    if t >= 1:
                        r2, k2 = token_rows(t - 1)
                        sp.wait_ge(x1_ready, t)
                        sp.dma_start(scr_x1[k2, :], x1[0:r2, (t - 1) % 2, :]).then_inc(x1_out[(t - 1) % 2], 16)
                        sp.wait_ge(hg_ready, t)
                        sp.dma_start(scr_h2[k2, :], hg[0:r2, (t - 1) % 2, :]).then_inc(x1_out[(t - 1) % 2], 16)
                sp.wait_ge(x1_ready, TT + 1)
                sp.dma_start(scr_x1[SEQ:T, :], x1[0:NS, 0, :]).then_inc(x1_out[0], 16)
                sp.wait_ge(hg_ready, TT + 1)
                sp.dma_start(scr_h2[SEQ:T, :], hg[0:NS, 0, :]).then_inc(x1_out[0], 16)
                sp.wait_ge(x1_out[0], 32 * (TT // 2 + 1))
                sp.wait_ge(x1_out[1], 32 * (TT // 2))

            @block.tensor
            def _(pe):
                def turn(t):
                    rows, tok = token_rows(t)
                    pe.wait_ge(hn_ready, t + 1)
                    pe.wait_ge(hT_out, t)
                    for c in range(KC):
                        last = nc.tensor.transpose(ps[:, 4 + c // 4, (c % 4) * P:(c % 4) * P + rows],
                                                   hn[0:rows, t % 2, c * P:(c + 1) * P], ident[0:rows, 0:rows])
                    last.then_inc(hT_acc, 1)

                pe.wait_ge(os_w, 32)
                for t in range(TT + 1):
                    rows, tok = token_rows(t)
                    if t >= 2:
                        pe.wait_ge(x1_ready, t - 1)
                    for k in range(2):
                        for kc in range(KC):
                            last = nc.tensor.matmul(ps[0:rows, 2 * (t % 2) + k, :], mT[:, kc, tok], o_slab[:, k, kc, :],
                                                    start=(kc == 0), stop=(kc == KC - 1))
                    last.then_inc(x1_acc, 1)
                    if t:
                        turn(t - 1)
                turn(TT)

            @block.vector
            def _(dve):
                dve.wait_ge(gr_in, 16)
                for t in range(TT + 1):
                    rows, tok = token_rows(t)
                    k = t % 2
                    dve.wait_ge(x1_acc, t + 1)
                    dve.wait_ge(xs_in[k], 16 * (t // 2 + 1))
                    if t >= 2:
                        dve.wait_ge(x1_out[k], 32 * (t // 2))
                        dve.wait_ge(hn_ready, t - 1)
                    nc.vector.tensor_tensor(x1[0:rows, k, :], xr[0:rows, k, :],
                                            ps[0:rows, 2 * k:2 * k + 2, :].rearrange("p a n -> p (a n)"),
                                            ALU.add).then_inc(x1_ready, 1)
                    s = ss6[0:rows, k:k + 1]
                    dve.wait_ge(sq6, t + 1)
                    nc.vector.tensor_scalar(s, s, 1.0 / D, EPS, ALU.mult, ALU.add).then_inc(ms6, 1)
                    dve.wait_ge(rt6, t + 1)
                    nc.vector.reciprocal(s, s).then_inc(rc6, 1)
                    dve.wait_ge(hn_ready, t + 1)
                    nc.vector.tensor_tensor(hg[0:rows, k, :], hn[0:rows, k, :], g_row[0:rows, :], ALU.mult).then_inc(hg_ready, 1)
                    dve.wait_ge(hT_acc, t + 1)
                    for b in range(2):
                        last = nc.vector.tensor_tensor(
                            h2T[:, 4 * b:4 * b + 4, tok],
                            ps[:, 4 + b, :].rearrange("p (c t) -> p c t", c=4)[:, :, 0:rows],
                            g_ffn[:, 4 * b:4 * b + 4].unsqueeze(2).broadcast_to([P, 4, rows]), ALU.mult)
                    last.then_inc(hT_out, 1)

            @block.scalar
            def _(act):
                for t in range(TT + 1):
                    rows, tok = token_rows(t)
                    k = t % 2
                    s = ss6[0:rows, k:k + 1]
                    act.wait_ge(x1_ready, t + 1)
                    nc.scalar.activation(junk6[0:rows, :], x1[0:rows, k, :], ACT.Square, accum_out=s).then_inc(sq6, 1)
                    act.wait_ge(ms6, t + 1)
                    nc.scalar.activation(s, s, ACT.Sqrt).then_inc(rt6, 1)
                    act.wait_ge(rc6, t + 1)
                    if t >= 2:
                        act.wait_ge(hT_acc, t - 1)
                        act.wait_ge(hg_ready, t - 1)
                    nc.scalar.activation(hn[0:rows, k, :], x1[0:rows, k, :], ACT.Copy, scale=s).then_inc(hn_ready, 1)

        NQ = 2 * PH
        qp = lay(0, [NQ * T + P])
        qpT = qp[:, 0:NQ * T].rearrange("p (m t) -> p m t", t=T)
        keys = lay(NQ * T + P, [NQ, PK])
        keys_in, pad_zero = sem("keys_in"), sem("pad_zero")
        with nc.Block() as block:
            @block.gpsimd
            def _(pool):
                nc.gpsimd.memset(qp[:, NQ * T:], 0.0).then_inc(pad_zero, 1)

            @block.sync
            def _(sp):
                sp.dma_start(keys.rearrange("p m k -> p (m k)"), dr["keys"]).then_inc(keys_in, 16)
                stat_loads(sp, wbuf, T_QUERY, PH, pairs)
                sp.wait_ge(keys_in, 16)

            @block.tensor
            def _(pe):
                with pe.Fori(0, PH) as i:
                    for k in range(2):
                        stat_products(pe, i, k, wbuf, h2T, pairs)

            @block.scalar
            def _(act):
                with act.Fori(0, PH) as i:
                    for c in range(NC3):
                        act.wait_ge(acc_ready[0], i * 3 + (3 * pairs + c + 1))
                        nc.scalar.activation(one(qpT[:, bass.ds(i * 2, 1), chunk(c)]), ps[:, c, 0:CW],
                                             ACT.Copy).then_inc(acc_free[0], 1)

            @block.vector
            def _(dve):
                with dve.Fori(0, PH) as i:
                    for c in range(NC3):
                        dve.wait_ge(acc_ready[1], i * 3 + (3 * pairs + c + 1))
                        nc.vector.tensor_copy(one(qpT[:, bass.ds(i * 2 + 1, 1), chunk(c)]), ps[:, 3 + c, 0:CW]
                                              ).then_inc(acc_free[1], 1)
        pairs += PH

        RING, STEP = 8, TOPK
        PAIR = 2
        A = NQ * T + P + NQ * PK
        def take(shape, dt=F32):
            nonlocal A
            at, A = A, A + int(np.prod(shape))
            return lay(at, shape, dt)
        ring = take([RING, 2 * D])
        h2, x1b, yo, g_fin, junk_y = (take([D]) for _ in range(5))
        junk = take([2, D])
        diag = take([4, P])
        qst = take([2, P])
        sct, s2t = take([2, PK]), take([2, PK])
        vals, idxu, idxf = take([2, TOPK]), take([2, TOPK], U32), take([2, TOPK])
        cand, cand2 = take([TOPK, TOPK]), take([TOPK * TOPK])
        sv, si, sab, sabf = take([TOPK]), take([TOPK], U32), take([2, TOPK], U32), take([2, TOPK])
        hot, e12 = take([2, TOPK, TOPK]), take([2, TOPK])
        iota = take([TOPK])
        logit_next, gates, gsum = take([PH * TOPK]), take([PH, TOPK]), take([PH])
        idx_next, idx_cur, idx_st = take([PH * TOPK], U32), take([PH * TOPK], U32), take([STEP], U32)
        act_in, act_out, wgt = take([STEP]), take([PAIR]), take([PAIR])
        ss8 = take([1])
        assert A <= ARENA
        KCH = 16

        names = ("pc_in", "h2_in", "x1_in", "q_st", "s_acc", "sc_done", "tk_v", "tk_done", "idx_cp", "idx_stg",
                 "slot_free", "dots", "gelu_d", "wgt_d", "diag_d", "init_d", "ex_d", "gt_v", "sq8", "ms8", "rt8", "rc8",
                 "yo_d", "y_out")
        (pc_in, h2_in, x1_in, q_st, s_acc, sc_done, tk_v, tk_done, idx_cp, idx_stg, slot_free, dots, gelu_d, wgt_d, diag_d,
         init_d, ex_d, gt_v, sq8, ms8, rt8, rc8, yo_d, y_out) = (sem(n) for n in names)
        row_in = [sem(f"row_in{k}") for k in range(RING)]
        acc = ps[:, 0:2, :].rearrange("p a n -> p (a n)")

        def choose_act(act, t, b, h):
            act.wait_ge(s_acc, START + t)
            alone(act)
            for k in range(2):
                last = nc.scalar.activation(qst[:, k, :], qp[:, bass.ds(h * (2 * T) + b * P + k * T, P)], ACT.Copy)
            last.then_inc(q_st, 1)
            act.wait_ge(s_acc, START + t + 1)
            act.wait_ge(tk_done, START + t)
            nc.scalar.activation(sct.rearrange("p a n -> p (a n)"), ps[:, 2, 0:2 * PK], ACT.Copy).then_inc(sc_done, 1)

        def choose_pe(pe, t, h):
            pe.wait_ge(q_st, t + 1)
            pe.wait_ge(sc_done, START + t)
            for k in range(2):
                last = nc.tensor.matmul(ps[:, 2, k * PK:(k + 1) * PK], qst[:, k, :], one(keys[:, bass.ds(h * 2 + k, 1), :]),
                                        start=True, stop=True)
            last.then_inc(s_acc, 1)

        def choose_dve(dve, t, h, copied):
            link = [0]

            def done(ins):
                link[0] += 1
                ins.then_inc(tk_v, 1)
                dve.wait_ge(tk_v, t * KCH + link[0])
                alone(dve)

            v = nc.vector
            dve.wait_ge(sc_done, START + t + 1)
            alone(dve)
            for k in range(2):
                last = v.max(vals[:, k, 0:8], sct[:, k, :])
            done(last)
            for k in range(2):
                v.match_replace(s2t[:, k, :], vals[:, k, 0:8], sct[:, k, :], LOWEST)
                last = v.max_index(idxu[:, k, 0:8], vals[:, k, 0:8], sct[:, k, :])
            done(last)
            for k in range(2):
                last = v.max(vals[:, k, 8:16], s2t[:, k, :])
            done(last)
            for k in range(2):
                v.max_index(idxu[:, k, 8:16], vals[:, k, 8:16], s2t[:, k, :])
            last = v.tensor_tensor(cand, vals[:, 0, :].unsqueeze(2).broadcast_to([P, TOPK, TOPK]),
                                   vals[:, 1, :].unsqueeze(1).broadcast_to([P, TOPK, TOPK]), ALU.add)
            done(last)
            flat = cand.rearrange("p a b -> p (a b)")
            last = v.tensor_copy(idxf.rearrange("p a b -> p (a b)"), idxu.rearrange("p a b -> p (a b)"))
            done(v.max(sv[:, 0:8], flat))
            v.match_replace(cand2, sv[:, 0:8], flat, LOWEST)
            done(v.max_index(si[:, 0:8], sv[:, 0:8], flat))
            done(v.max(sv[:, 8:16], cand2))
            done(v.max_index(si[:, 8:16], sv[:, 8:16], cand2))
            v.tensor_scalar(sab[:, 0, :], si, 4, None, ALU.logical_shift_right)
            done(v.tensor_scalar(sab[:, 1, :], si, 15, None, ALU.bitwise_and))
            done(v.tensor_copy(sabf.rearrange("p a b -> p (a b)"), sab.rearrange("p a b -> p (a b)")))
            for k in range(2):
                last = v.tensor_tensor(hot[:, k], sabf[:, k, :].unsqueeze(2).broadcast_to([P, TOPK, TOPK]),
                                       iota.unsqueeze(1).broadcast_to([P, TOPK, TOPK]), ALU.is_equal)
            done(last)
            for k in range(2):
                last = v.tensor_tensor(hot[:, k], hot[:, k], idxf[:, k, :].unsqueeze(1).broadcast_to([P, TOPK, TOPK]), ALU.mult)
            done(last)
            done(v.tensor_reduce(e12.rearrange("p a b -> p (a b)"), hot.rearrange("p k a b -> p (k a) b"), AX.X, ALU.add))
            mine = bass.ds(h * TOPK, TOPK)
            done(v.tensor_scalar(logit_next[:, mine], sv, sv[:, 0:1], None, ALU.subtract))
            done(v.tensor_scalar(e12[:, 0, :], e12[:, 0, :], float(PK), None, ALU.mult))
            dve.wait_ge(idx_cp, START + copied)
            done(v.tensor_tensor(idx_next[:, mine], e12[:, 0, :], e12[:, 1, :], ALU.add))
            assert link[0] == KCH, link
            v.tensor_copy(e12[:, 0, 0:1], e12[:, 1, 0:1]).then_inc(tk_done, 1)

        def gather_pool(pool, g, h, rows):
            for half in range(STEP // RING):
                cols = slice(half * RING, (half + 1) * RING)
                nc.gpsimd.tensor_copy(idx_st[0:rows, cols], idx_cur[0:rows, bass.ds(h * STEP + half * RING, RING)]
                                      ).then_inc(idx_stg, 1)
                pool.wait_ge(idx_stg, g * 2 + (half + 1))
                alone(pool)
                for j in range(half * RING, (half + 1) * RING):
                    pool.wait_ge(slot_free, g * STEP + (j + 1))
                    alone(pool)
                    pool.indirect_dma_start(ring[0:rows, j % RING, :], None, dr["uv"],
                                            bass.IndirectOffsetOnAxis(ap=idx_st[0:rows, j:j + 1], axis=0)
                                            ).then_inc(row_in[j % RING], 16)

        def gather_dve(dve, g, rows, j):
            dve.wait_ge(row_in[j % RING], g * (16 * STEP // RING) + 16 * (j // RING + 1))
            if j == 0:
                dve.wait_ge(gelu_d, START + g * (STEP // PAIR))
            dve.wait_ge(dots, START + g * STEP + max(j - 1, 0))
            ins = nc.vector.tensor_tensor_reduce(junk[0:rows, j % 2, :], ring[0:rows, j % RING, 0:D], h2[0:rows], 1.0, 0.0, ALU.mult,
                                                 ALU.add, act_in[0:rows, j:j + 1])
            ins.then_inc(dots, 1)

        def gather_act(act, g, h, rows, p):
            n = g * (STEP // PAIR) + p
            act.wait_ge(dots, START + g * STEP + PAIR * (p + 1))
            nc.scalar.activation(act_out[0:rows, :], act_in[0:rows, PAIR * p:PAIR * (p + 1)], ACT.Gelu).then_inc(gelu_d, 1)
            act.wait_ge(gelu_d, START + n + 1)
            alone(act)
            for q in range(PAIR):
                col = gates.rearrange("p a b -> p (a b)")[0:rows, bass.ds(h * STEP + (PAIR * p + q), 1)]
                last = nc.scalar.activation(wgt[0:rows, q:q + 1], col, ACT.Copy, scale=act_out[0:rows, q:q + 1])
            last.then_inc(wgt_d, 1)
            act.wait_ge(wgt_d, n + 1)
            for q in range(PAIR):
                j = PAIR * p + q
                act.wait_ge(slot_free, g * STEP + (j + RING - 3))
                nc.scalar.activation(diag[0:rows, j % 4, 0:rows], ident[0:rows, 0:rows], ACT.Copy,
                                     scale=wgt[0:rows, q:q + 1]).then_inc(diag_d, 1)

        def gather_pe(pe, g, rows, j):
            pe.wait_ge(diag_d, START + g * STEP + (j + 1))
            alone(pe)
            for c in range(2):
                last = nc.tensor.matmul(ps[0:rows, c, :], diag[0:rows, j % 4, 0:rows],
                                        ring[0:rows, j % RING, D + 512 * c:D + 512 * (c + 1)],
                                        start=False, stop=False, skip_group_check=True)
            last.then_inc(slot_free, 1)

        def first_act(act, b):
            act.wait_ge(tk_done, START + b * PH + PH)
            act.wait_ge(diag_d, START + b * (PH * STEP))
            nc.scalar.activation(gates.rearrange("p a b -> p (a b)"), logit_next, ACT.Exp).then_inc(ex_d, 1)
            act.wait_ge(gt_v, b * 3 + 3)

        def first_dve(dve, b):
            dve.wait_ge(ex_d, b + 1)
            nc.vector.tensor_reduce(gsum, gates, AX.X, ALU.add).then_inc(gt_v, 1)
            dve.wait_ge(gt_v, b * 3 + 1)
            nc.vector.reciprocal(gsum, gsum).then_inc(gt_v, 1)
            dve.wait_ge(gt_v, b * 3 + 2)
            nc.vector.tensor_tensor(gates, gates, gsum.unsqueeze(2).broadcast_to([P, PH, TOPK]), ALU.mult).then_inc(gt_v, 1)
            dve.wait_ge(h2_in, b * 16 + 16)
            alone(dve)

        def first_pe(pe, b, rows):
            pe.wait_ge(yo_d, START + b)
            pe.wait_ge(x1_in, b * 16 + 16)
            for c in range(2):
                last = nc.tensor.matmul(ps[0:rows, c, :], ident[0:rows, 0:rows], x1b[0:rows, 512 * c:512 * (c + 1)],
                                        start=True, stop=False, skip_group_check=True)
            last.then_inc(init_d, 1)

        def first_sp(sp, b, rows):
            sp.wait_ge(dots, START + b * (PH * STEP))
            sp.dma_start(h2[0:rows], scr_h2[bass.ds(b * P, rows), :]).then_inc(h2_in, 16)
            sp.wait_ge(init_d, START + b)
            sp.dma_start(x1b[0:rows], scr_x1[bass.ds(b * P, rows), :]).then_inc(x1_in, 16)

        def first_pool(pool, b):
            pool.wait_ge(tk_done, START + b * PH + PH)
            alone(pool)
            nc.gpsimd.tensor_copy(idx_cur, idx_next).then_inc(idx_cp, 1)
            pool.wait_ge(idx_cp, START + b + 1)
            alone(pool)

        def last_act(act, b, rows):
            act.wait_ge(slot_free, (b + 1) * (PH * STEP) + RING)
            act.wait_ge(yo_d, START + b)
            nc.scalar.activation(junk_y[0:rows], acc[0:rows], ACT.Square, accum_out=ss8[0:rows]).then_inc(sq8, 1)
            act.wait_ge(ms8, b + 1)
            nc.scalar.activation(ss8[0:rows], ss8[0:rows], ACT.Sqrt).then_inc(rt8, 1)
            act.wait_ge(yo_d, START + b + 1)
            act.dma_start(out["y"][bass.ds(b * P, rows), :], yo[0:rows]).then_inc(y_out, 16)
            act.wait_ge(y_out, b * 16 + 16)

        def last_dve(dve, b, rows):
            s = ss8[0:rows]
            dve.wait_ge(sq8, b + 1)
            nc.vector.tensor_scalar(s, s, 1.0 / D, EPS, ALU.mult, ALU.add).then_inc(ms8, 1)
            dve.wait_ge(rt8, b + 1)
            nc.vector.reciprocal(s, s).then_inc(rc8, 1)
            dve.wait_ge(rc8, b + 1)
            nc.vector.scalar_tensor_tensor(yo[0:rows], acc[0:rows], s, g_fin[0:rows], ALU.mult, ALU.mult).then_inc(yo_d, 1)

        with nc.Block() as block:
            @block.sync
            def _(sp):
                sp.dma_start(iota, dr["iota16"]).then_inc(pc_in, 16)
                sp.dma_start(g_fin, dr["g_fin_row"].broadcast_to([P, D])).then_inc(pc_in, 16)
                with sp.Fori(0, TT) as b:
                    first_sp(sp, b, P)
                first_sp(sp, TT, NS)

            @block.gpsimd
            def _(pool):
                with pool.Fori(0, TT) as b:
                    first_pool(pool, b)
                    with pool.Fori(0, PH) as h:
                        gather_pool(pool, b * PH + h, h, P)
                first_pool(pool, TT)
                with pool.Fori(0, PH) as h:
                    gather_pool(pool, h + TT * PH, h, NS)

            @block.scalar
            def _(act):
                with act.Fori(0, PH) as h:
                    choose_act(act, h, 0, h)
                with act.Fori(0, TT) as b:
                    first_act(act, b)
                    with act.Fori(0, PH) as h:
                        choose_act(act, b * PH + h + PH, b + 1, h)
                        for p in range(STEP // PAIR):
                            gather_act(act, b * PH + h, h, P, p)
                    last_act(act, b, P)
                first_act(act, TT)
                with act.Fori(0, PH) as h:
                    for p in range(STEP // PAIR):
                        gather_act(act, h + TT * PH, h, NS, p)
                last_act(act, TT, NS)

            @block.tensor
            def _(pe):
                pe.sem_inc(slot_free, RING)
                with pe.Fori(0, PH) as h:
                    choose_pe(pe, h, h)
                with pe.Fori(0, TT) as b:
                    first_pe(pe, b, P)
                    with pe.Fori(0, PH) as h:
                        choose_pe(pe, b * PH + h + PH, h)
                        for j in range(STEP):
                            gather_pe(pe, b * PH + h, P, j)
                first_pe(pe, TT, NS)
                with pe.Fori(0, PH) as h:
                    for j in range(STEP):
                        gather_pe(pe, h + TT * PH, NS, j)

            @block.vector
            def _(dve):
                dve.wait_ge(pc_in, 32)
                with dve.Fori(0, PH) as h:
                    choose_dve(dve, h, h, 0)
                with dve.Fori(0, TT) as b:
                    first_dve(dve, b)
                    with dve.Fori(0, PH) as h:
                        for j in range(STEP):
                            gather_dve(dve, b * PH + h, P, j)
                            if j == 3:
                                choose_dve(dve, b * PH + h + PH, h, b + 1)
                    last_dve(dve, b, P)
                first_dve(dve, TT)
                with dve.Fori(0, PH) as h:
                    for j in range(STEP):
                        gather_dve(dve, h + TT * PH, NS, j)
                last_dve(dve, TT, NS)


def _layouts(a):
    import numpy as np
    def f(x):
        return np.ascontiguousarray(x)
    def stationary(w):
        n = w.shape[1] // 128
        return w.reshape(8, 128, n, 128).transpose(2, 1, 0, 3).reshape(n, 128, 1024)
    def moving(w):
        n = w.shape[1] // 512
        return w.reshape(8, 128, n, 512).transpose(2, 1, 0, 3).reshape(n, 128, 4096)
    def pairs(x, y):
        return np.stack([x, y], 1).reshape(-1, 128, 1024)
    def by_state(x):
        return np.moveaxis(x.reshape((32, 2, 64) + x.shape[2:]), 0, 2).reshape((128, 32) + x.shape[2:])
    w_in = a["w_in"][0]
    q, k, v, u, ga, gs = (w_in[:, i * 1024:(i + 1) * 1024] for i in range(6))
    g64 = (64, 64)
    d = {
        "x": np.concatenate([a["x_prompt"].reshape(1024, 1024), a["x_sample"].reshape(32, 1024)]),
        "ident": np.eye(128, dtype=np.float32),
        "g_mix": a["norm_mix_g"].reshape(8, 128).T,
        "g_ffn": a["norm_ffn_g"].reshape(8, 128).T,
        "b_glu": a["b_glu"].reshape(8, 128).T,
        "lam": np.concatenate([a["lambda_q1"], a["lambda_k1"], a["lambda_q2"], a["lambda_k2"]], 1),
        "w_stat": np.concatenate([pairs(stationary(q), stationary(k)),
                                  pairs(stationary(gs), stationary(a["w_proj_s5"][0])),
                                  stationary(a["w_glu"][0]),
                                  pairs(stationary(ga), stationary(a["w_proj_att"][0])),
                                  stationary(a["peer_w_query"][0])]),
        "w_mov": np.concatenate([moving(u), moving(v), moving(a["w_out"][0])]),
        "a_re": by_state(a["s5_a_re"][0]), "a_im": by_state(a["s5_a_im"][0]),
        "log_step": by_state(np.broadcast_to(a["s5_log_step"][0][:, None], g64)),
        "b_ri": np.stack([by_state(a["s5_b_re"][0]), by_state(a["s5_b_im"][0])], 1).reshape(128, -1),
        "c_ri": np.stack([by_state(a["s5_c_re"][0].transpose(0, 2, 1)),
                          by_state(a["s5_c_im"][0].transpose(0, 2, 1))], 1).reshape(128, -1),
        "h0": np.stack([by_state(a["state_s5_re"][0].transpose(1, 2, 0)),
                        by_state(a["state_s5_im"][0].transpose(1, 2, 0))], 1).reshape(128, -1),
        "d_s5": a["s5_d"][0].T,
        "keys": a["peer_sub_keys"][0].transpose(3, 0, 1, 2).reshape(128, 2048),
        "uv": np.concatenate([a["peer_u"][0], a["peer_v"][0]], 1),
        "g_ffn_row": a["norm_ffn_g"], "g_fin_row": a["norm_final_g"].reshape(1, 1024),
        "subln": a["subln_g"].reshape(128, 1),
        "cache_k": a["cache_k"][0].reshape(-1, 128, 1024), "cache_v": a["cache_v"][0].reshape(-1, 128, 1024),
        "pages": a["page_table"].reshape(1, 64),
    }
    i128 = np.arange(128)
    d["causal"] = np.where(i128[None, :] <= i128[:, None], 0, NEG).astype(np.float32)
    row = np.arange(64)
    tok = np.arange(32)
    d["causal_new"] = np.where((tok[None, None, :] // 4 == np.arange(8)[None, :, None])
                               & (tok[None, None, :] % 4 <= (row % 4)[:, None, None]), 0, NEG).astype(np.float32).reshape(64, 256)
    d["pick"] = ((row[:, None] // 8 == tok[None, :] // 4) & (row[:, None] % 4 == tok[None, :] % 4)).astype(np.float32)
    d["first"] = ((row % 8) < 4).astype(np.float32).reshape(64, 1)
    d["iota16"] = np.broadcast_to(np.arange(16, dtype=np.float32), (128, 16))
    return {k: f(v) for k, v in d.items()}


_OUTS = {
    "y": (1056, 1024), "k": (1056, 1024), "v": (1056, 1024), "s5_prompt": (128, 64), "s5_sample": (128, 512),
}


def kernel(**inputs):
    import concourse.bacc as bacc
    from concourse.bass_utils import run_bass_kernel_spmd

    arrays = _layouts({k: np.asarray(v) for k, v in inputs.items()})
    nc = bacc.Bacc("TRN2", target_bir_lowering=False, num_devices=1)
    dr = {n: nc.dram_tensor("in_" + n, a.shape, mybir.dt.from_np(a.dtype), kind="ExternalInput").ap()
          for n, a in arrays.items()}
    out = {n: nc.dram_tensor("out_" + n, s, F32, kind="ExternalOutput").ap() for n, s in _OUTS.items()}
    hybrid_step(nc, dr, out)
    r = run_bass_kernel_spmd(nc, [{"in_" + n: a for n, a in arrays.items()}], core_ids=[0]).results[0]
    y, k, v = r["out_y"], r["out_k"], r["out_v"]
    def by_group(x):
        return np.moveaxis(x.reshape((2, 64) + x.shape[1:]), 2, 0).reshape((64, 64) + x.shape[2:])
    sp = r["out_s5_prompt"].reshape(128, 2, 32)
    ss = r["out_s5_sample"].reshape(128, 2, 32, 8)
    hp = [by_group(sp[:, i]).reshape(1, 1, 64, 64) for i in range(2)]
    hsm = [by_group(ss[:, i]).transpose(2, 0, 1).reshape(1, 8, 64, 64) for i in range(2)]
    f = np.ascontiguousarray
    return (f(y[:1024].reshape(1, 1024, 1024)), f(y[1024:].reshape(8, 4, 1024)),
            f(k[:1024].reshape(1, 1, 1024, 8, 128)), f(v[:1024].reshape(1, 1, 1024, 8, 128)),
            f(hp[0]), f(hp[1]),
            f(k[1024:].reshape(1, 8, 4, 8, 128)), f(v[1024:].reshape(1, 8, 4, 8, 128)),
            f(hsm[0]), f(hsm[1]))
```

```python
from contextlib import ExitStack
import math

import numpy as np

import concourse.bass as bass
from concourse import mybir

F32 = mybir.dt.float32
U32 = mybir.dt.uint32
I32 = mybir.dt.int32
ALU = mybir.AluOpType
ACT = mybir.ActivationFunctionType
AX = mybir.AxisListType

P = 128
D = 1024
KC = D // P
SEQ = 1024
NSEQ, NNEW = 8, 4
NS = NSEQ * NNEW
T = SEQ + NS
TT = SEQ // P
NC3 = 3
CW = T // NC3
H = 8
HD = 64
G, PS5, CH = 64, 64, 16
GP = G // 2
ST8 = 8
NCH = SEQ // ST8
PAGES = 8
PH, PK, TOPK = 8, 128, 16
NE = PK * PK
EPS = 1e-6
LAM_INIT = 0.8 - 0.6 * math.exp(-0.3 * 0)
NEG = -1e30
LOWEST = -3e38
ARENA = 52900
ROUND = 1.5 * 2 ** 23
TWO_PI = (6.28125, 0.00193500518798828125, 2 * math.pi - 6.28125 - 0.00193500518798828125)
SIN_AT = 12

T_QK, T_GS, T_GLU, T_GA, T_QUERY = 0, 16, 32, 40, 56

START = 1
START_AT_ONE = ("hT_done", "acc_out", "yo_clear", "gl_used", "prod", "oT_free", "t_free", "ko_clear", "kt_ready", "on_acc",
                "on_free", "en_ready", "kt_free", "page_used", "ptn_free", "ptn_ready", "sn_ready", "sc_done",
                "s_acc", "tk_done", "idx_cp", "gelu_d", "diag_d", "yo_d", "dots", "init_d")


def hybrid_step(nc, dr, out):
    root = ExitStack()
    with root:
        started = {n: root.enter_context(nc.semaphore(n)) for n in START_AT_ONE}

        def sem(name):
            return started[name] if name in started else root.enter_context(nc.semaphore(name))

        spare = sem("spare")

        def alone(eng):
            eng.sem_inc(spare, 1)

        def sbuf(stack, name, shape, dt=F32):
            return stack.enter_context(nc.sbuf_tensor(name, shape, dt))

        ps = root.enter_context(nc.psum_tensor("ps", [P, 8, 512], F32))

        ident = sbuf(root, "ident", [P, P])
        g_mix = sbuf(root, "g_mix", [P, KC])
        g_ffn = sbuf(root, "g_ffn", [P, KC])
        b_glu = sbuf(root, "b_glu", [P, KC])
        neg_lam = sbuf(root, "neg_lam", [P, 2])
        arena = sbuf(root, "arena", [P, ARENA])

        def lay(at, shape, dt=F32):
            n = int(np.prod(shape))
            assert at + n <= ARENA, (at, shape)
            flat = arena[:, at:at + n]
            if dt != F32:
                flat = flat.bitcast(dt)
            names = [f"d{i}" for i in range(len(shape))]
            if len(shape) == 1:
                return flat
            return flat.rearrange(f"p ({' '.join(names)}) -> p {' '.join(names)}",
                                  **{m: s for m, s in zip(names[1:], shape[1:])})

        w_in = [sem(f"w_in{k}") for k in range(2)]
        acc_ready = [sem(f"acc_ready{k}") for k in range(2)]
        acc_free = [sem(f"acc_free{k}") for k in range(2)]
        pairs = 0

        def stat_load(sp, wbuf, k, tile):
            sp.dma_start(wbuf[:, k, :], tile).then_inc(w_in[k], 16)

        def stat_loads(sp, wbuf, tile0, n, pairs):
            for k in range(2):
                stat_load(sp, wbuf, k, dr["w_stat"][tile0 + k])
            with sp.Fori(1, n) as i:
                for k in range(2):
                    sp.wait_ge(acc_ready[k], i * 3 + 3 * pairs)
                    stat_load(sp, wbuf, k, dr["w_stat"][bass.ds(i * 2 + (tile0 + k), 1)]
                              .rearrange("a p n -> (a p) n"))

        def stat_products(pe, i, k, wbuf, moving, pairs):
            pe.wait_ge(w_in[k], i * 16 + 16 * (pairs + 1))
            for c in range(NC3):
                pe.wait_ge(acc_free[k], i * 3 + (3 * pairs + c + 1))
                for kc in range(KC):
                    last = nc.tensor.matmul(ps[:, 3 * k + c, 0:CW], wbuf[:, k, kc * P:(kc + 1) * P],
                                            moving[:, kc, c * CW:(c + 1) * CW],
                                            start=(kc == 0), stop=(kc == KC - 1))
                last.then_inc(acc_ready[k], 1)

        AT_CL, AT_TOE, AT_UG, AT_HH, AT_UA, AT_HS, AT_H0, AT_WK, AT_PW, AT_HT = np.cumsum(
            [0, GP * 2 * 9 * CH, G * P, G * P, 2 * GP * (NCH + 1), G * NSEQ, 2 * GP * NSEQ, 2 * GP * NSEQ,
             G * P, 9 * 2 * GP]).tolist()
        hT = lay(AT_HT, [KC, T])
        if True:
            xt = lay(AT_HH, [2, D])
            junk = lay(AT_HH + 2 * D, [D])
            lamv = lay(AT_HH + 3 * D, [4, HD])
            junk2 = lay(AT_HH + 4 * D, [2, HD])
            lam = lay(AT_HH + 5 * D, [4])
            ss = lay(AT_HH + 5 * D + 4, [2])
            const_in, lam_in = sem("const_in"), sem("lam_in")
            x_in = [sem(f"x_in{k}") for k in range(2)]
            sq_done, ms_done, rt_done, rc_done = sem("sq_done"), sem("ms_done"), sem("rt_done"), sem("rc_done")
            xn_done, xT_done, hT_done = sem("xn_done"), sem("xT_done"), sem("hT_done")
            lam_v, lam_a = sem("lam_v"), sem("lam_a")

            def norm_tile_act(act, x, ssq, rows, n):
                nc.scalar.activation(junk[0:rows, :], x, ACT.Square, accum_out=ssq).then_inc(sq_done, 1)
                act.wait_ge(ms_done, n + 1)
                nc.scalar.activation(ssq, ssq, ACT.Sqrt).then_inc(rt_done, 1)
                act.wait_ge(rc_done, n + 1)
                nc.scalar.activation(x, x, ACT.Copy, scale=ssq).then_inc(xn_done, 1)

            def norm_tile_dve(dve, ssq, n):
                dve.wait_ge(sq_done, n + 1)
                nc.vector.tensor_scalar(ssq, ssq, 1.0 / D, EPS, ALU.mult, ALU.add).then_inc(ms_done, 1)
                dve.wait_ge(rt_done, n + 1)
                nc.vector.reciprocal(ssq, ssq).then_inc(rc_done, 1)

            with nc.Block() as block:
                @block.sync
                def _(sp):
                    for s in started.values():
                        sp.sem_inc(s, START)
                    sp.dma_start(ident[:, :], dr["ident"]).then_inc(const_in, 16)
                    sp.dma_start(g_mix[:, :], dr["g_mix"]).then_inc(const_in, 16)
                    sp.dma_start(g_ffn[:, :], dr["g_ffn"]).then_inc(const_in, 16)
                    sp.dma_start(b_glu[:, :], dr["b_glu"]).then_inc(const_in, 16)
                    sp.dma_start(lamv[:, :, :].rearrange("p a b -> p (a b)"),
                                 dr["lam"].broadcast_to([P, 4 * HD])).then_inc(lam_in, 16)
                    for k in range(2):
                        sp.dma_start(xt[:, k, :], dr["x"][k * P:(k + 1) * P, :]).then_inc(x_in[k], 16)
                    with sp.Fori(1, TT // 2) as i:
                        for k in range(2):
                            sp.wait_ge(xT_done, i * 2 + (k - 1))
                            sp.dma_start(xt[:, k, :], dr["x"][bass.ds(i * 2 * P + k * P, P), :]).then_inc(x_in[k], 16)
                    sp.wait_ge(xT_done, TT - 1)
                    sp.dma_start(xt[0:NS, 0, :], dr["x"][SEQ:T, :]).then_inc(x_in[0], 16)

                @block.scalar
                def _(act):
                    for k in range(2):
                        act.sem_inc(acc_free[k], 3)
                    with act.Fori(0, TT // 2) as i:
                        for k in range(2):
                            act.wait_ge(x_in[k], (i + 1) * 16)
                            norm_tile_act(act, xt[:, k, :], ss[:, k:k + 1], P, i * 2 + k)
                    act.wait_ge(x_in[0], 16 * (TT // 2 + 1))
                    norm_tile_act(act, xt[0:NS, 0, :], ss[0:NS, 0:1], NS, TT)
                    act.wait_ge(lam_v, 1)
                    nc.scalar.activation(lam[:, 2:4], lam[:, 0:2], ACT.Exp).then_inc(lam_a, 1)

                @block.tensor
                def _(pe):
                    pe.wait_ge(const_in, 64)

                    def transposes(k, rows, n):
                        pe.wait_ge(xn_done, n + 1)
                        if k is not None:
                            pe.wait_ge(hT_done, START + n)
                        for c in range(KC):
                            last = nc.tensor.transpose(ps[:, c // 4, (c % 4) * P:(c % 4) * P + rows],
                                                       xt[0:rows, k, c * P:(c + 1) * P], ident[0:rows, 0:rows])
                        last.then_inc(xT_done, 1)

                    with pe.Fori(0, TT // 2) as i:
                        for k in range(2):
                            transposes(k, P, i * 2 + k)
                    transposes(0, NS, TT)

                @block.vector
                def _(dve):
                    def take_out(rows, col, n):
                        dve.wait_ge(xT_done, n + 1)
                        for b in range(2):
                            last = nc.vector.tensor_tensor(
                                hT[:, 4 * b:4 * b + 4, bass.ds(col, rows)],
                                ps[:, b, :].rearrange("p (c t) -> p c t", c=4)[:, :, 0:rows],
                                g_mix[:, 4 * b:4 * b + 4].unsqueeze(2).broadcast_to([P, 4, rows]), ALU.mult)
                        last.then_inc(hT_done, 1)

                    dve.wait_ge(const_in, 64)
                    with dve.Fori(0, TT // 2) as i:
                        for k in range(2):
                            norm_tile_dve(dve, ss[:, k:k + 1], i * 2 + k)
                            take_out(P, i * 2 * P + k * P, i * 2 + k)
                    norm_tile_dve(dve, ss[0:NS, 0:1], TT)
                    take_out(NS, SEQ, TT)
                    dve.wait_ge(lam_in, 16)
                    for b in range(2):
                        last = nc.vector.tensor_tensor_reduce(junk2[:, b, :], lamv[:, 2 * b, :], lamv[:, 2 * b + 1, :], 1.0, 0.0,
                                                              ALU.mult, ALU.add, lam[:, b:b + 1])
                    last.then_inc(lam_v, 1)
                    dve.wait_ge(lam_a, 1)
                    nc.vector.tensor_tensor(neg_lam[:, 0:1], lam[:, 3:4], lam[:, 2:3], ALU.subtract).then_inc(lam_v, 1)
                    dve.wait_ge(lam_v, 2)
                    nc.vector.tensor_scalar(neg_lam[:, 1:2], neg_lam[:, 0:1], -LAM_INIT, None, ALU.add).then_inc(lam_v, 1)
                    dve.wait_ge(lam_v, 3)
                    nc.vector.memset(neg_lam[:, 0:1], 1.0)

        cl = lay(AT_CL, [GP, 2, 9, CH])
        m_toe = lay(AT_TOE, [G, P])
        ug = lay(AT_UG, [G, P])
        hh = lay(AT_HH, [2, GP, NCH + 1])
        ua = lay(AT_UA, [G, NSEQ])
        hs = lay(AT_HS, [2, GP, NSEQ])
        h0 = lay(AT_H0, [2, GP, NSEQ])
        wk = lay(AT_WK, [GP, 2, ST8, CH])
        kst = lay(AT_WK, [G, ST8, CH])
        z_tok = lay(AT_WK, [ST8, D])
        pw = lay(AT_PW, [9, 2, GP])
        u_tok = lay(AT_TOE, [G, ST8, CH])
        slab = lay(AT_WK, [2, KC, 512])
        us_tok = lay(AT_HH, [G, NNEW, CH])
        bri = lay(AT_HH + 4096, [2, GP, CH])
        cri = lay(AT_HH + 5120, [2, GP, CH])
        bb = lay(AT_HH + 6144, [2, GP, CH])
        tmp = lay(AT_HH + 7168, [GP, CH])
        sm = lay(AT_HH + 7680, [18, GP])
        d_s5 = lay(AT_HT + KC * T, [G])
        scr_h = nc.dram_tensor("scr_h", (P, KC * T), F32, kind="Internal").ap()

        par_in, slab_in = sem("par_in"), [sem(f"slab_in{k}") for k in range(2)]
        u_ready, u_free = sem("u_ready"), sem("u_free")
        ug_ready, ug_free = sem("ug_ready"), sem("ug_free")
        par_a, par_v, spill = sem("par_a"), sem("par_v"), sem("spill")
        NU = 2 * ST8 + 2 * NNEW

        def complex_step(dve, mul, re, im, ar, ai, br, bi, sign, t):
            mul(re, ar, br, ALU.mult)
            mul(t, ai, bi, ALU.mult)
            mul(re, re, t, ALU.subtract)
            mul(im, ar, bi, ALU.mult)
            mul(t, ai, br, ALU.mult)
            if sign > 0:
                mul(im, im, t, ALU.add)
            else:
                par["n"] += 1
                nc.vector.scalar_tensor_tensor(im, im, -1.0, t, ALU.mult, ALU.subtract).then_inc(par_v, 1)
                dve.wait_ge(par_v, par["n"])

        par = {"n": 0}
        with nc.Block() as block:
            @block.sync
            def _(sp):
                for k in range(2):
                    sp.dma_start(slab[:, k, :, :].rearrange("p a b -> p (a b)"), dr["w_mov"][k]).then_inc(slab_in[k], 16)
                for dst, name in ((sm[:, 0, :], "a_re"), (sm[:, 1, :], "a_im"), (sm[:, 2, :], "log_step"),
                                  (bri.rearrange("p r g c -> p (r g c)"), "b_ri"), (cri.rearrange("p r g c -> p (r g c)"), "c_ri"),
                                  (h0.rearrange("p r g q -> p (r g q)"), "h0"), (d_s5[0:CH, :], "d_s5")):
                    sp.dma_start(dst, dr[name]).then_inc(par_in, 16)
                sp.wait_ge(u_ready, NU)
                sp.dma_start(scr_h, hT.rearrange("p c t -> p (c t)")).then_inc(spill, 16)
                sp.wait_ge(spill, 16)

            @block.tensor
            def _(pe):
                n = 0
                for k in range(2):
                    pe.wait_ge(slab_in[k], 16)
                    for s in range(ST8 + NNEW):
                        if n >= 4:
                            pe.wait_ge(u_free, n - 3)
                        rows = P if s < ST8 else NSEQ
                        for kc in range(KC):
                            tok = hT[:, kc, s:SEQ:ST8] if s < ST8 else hT[:, kc, SEQ + s - ST8:T:NNEW]
                            last = nc.tensor.matmul(ps[0:rows, n % 4, :], tok, slab[:, k, kc, :],
                                                    start=(kc == 0), stop=(kc == KC - 1))
                        last.then_inc(u_ready, 1)
                        n += 1
                pe.wait_ge(u_free, NU)
                for q in range(G // 4):
                    if q >= 3:
                        pe.wait_ge(ug_free, q - 2)
                    for j in range(4):
                        g = 4 * q + j
                        last = nc.tensor.transpose(ps[:, 4 + q % 3, j * P:(j + 1) * P],
                                                   u_tok[:, g], ident[:, :])
                    last.then_inc(ug_ready, 1)
                for g in range(G):
                    last = nc.tensor.transpose(ps[0:64, 7, g * NSEQ:(g + 1) * NSEQ],
                                               us_tok[0:NSEQ, g], ident[0:NSEQ, 0:NSEQ])
                last.then_inc(ug_ready, 1)

            @block.scalar
            def _(act):
                dt_, mag, ang, r2 = sm[:, 3, :], sm[:, 4, :], sm[:, 5, :], sm[:, 6:8, :]
                act.wait_ge(par_in, 112)
                nc.scalar.activation(dt_, sm[:, 2, :], ACT.Exp).then_inc(par_a, 1)
                act.wait_ge(par_v, 1)
                nc.scalar.activation(mag, mag, ACT.Exp).then_inc(par_a, 1)
                act.wait_ge(par_v, SIN_AT)
                nc.scalar.activation(r2, r2, ACT.Sin).then_inc(par_a, 1)
                n = 0
                for k in range(2):
                    for s in range(ST8 + NNEW):
                        act.wait_ge(u_ready, n + 1)
                        gs_ = slice(G // 2 * k, G // 2 * (k + 1))
                        rows = P if s < ST8 else NSEQ
                        dst = u_tok[:, gs_, s, :] if s < ST8 else us_tok[0:NSEQ, gs_, s - ST8, :]
                        nc.scalar.activation(dst, ps[0:rows, n % 4, :].rearrange("p (g c) -> p g c", c=CH), ACT.Copy).then_inc(u_free, 1)
                        n += 1
                for q in range(G // 4):
                    act.wait_ge(ug_ready, q + 1)
                    nc.scalar.activation(ug[:, 4 * q:4 * q + 4, :].rearrange("p g t -> p (g t)"), ps[:, 4 + q % 3, :],
                                         ACT.Copy).then_inc(ug_free, 1)
                act.wait_ge(ug_ready, G // 4 + 1)
                nc.scalar.activation(ua[0:64].rearrange("p g q -> p (g q)"), ps[0:64, 7, :], ACT.Copy).then_inc(ug_free, 1)

            @block.vector
            def _(dve):
                def op(ins):
                    par["n"] += 1
                    ins.then_inc(par_v, 1)
                    dve.wait_ge(par_v, par["n"])

                def mul(o, a, b, how):
                    op(nc.vector.tensor_tensor(o, a, b, how))

                a_re, a_im, dt_, mag, ang, r2, q2 = (sm[:, 0, :], sm[:, 1, :], sm[:, 3, :], sm[:, 4, :], sm[:, 5, :],
                                                     sm[:, 6:8, :], sm[:, 8:10, :])
                t0, t1, f_re, f_im, den = (sm[:, j, :] for j in range(10, 15))
                dve.wait_ge(par_a, 1)
                mul(mag, a_re, dt_, ALU.mult)
                mul(ang, a_im, dt_, ALU.mult)
                for j in range(2):
                    op(nc.vector.tensor_scalar(q2[:, j, :], ang, 1 / (2 * math.pi), 0.25 * j, ALU.mult, ALU.add))
                op(nc.vector.tensor_scalar(q2, q2, ROUND, None, ALU.add))
                op(nc.vector.tensor_scalar(q2, q2, -ROUND, None, ALU.add))
                for j in range(2):
                    op(nc.vector.scalar_tensor_tensor(r2[:, j, :], q2[:, j, :], -TWO_PI[0], ang, ALU.mult, ALU.add))
                for part in TWO_PI[1:]:
                    op(nc.vector.scalar_tensor_tensor(r2, q2, -part, r2, ALU.mult, ALU.add))
                op(nc.vector.tensor_scalar(r2[:, 1, :], r2[:, 1, :], math.pi / 2, None, ALU.add))
                op(nc.vector.tensor_scalar(r2, r2, 3.1415925, -3.1415925, ALU.min, ALU.max))
                assert par["n"] == SIN_AT, par
                dve.wait_ge(par_a, 3)
                op(nc.vector.memset(pw[:, 0, 0, :], 1.0))
                op(nc.vector.memset(pw[:, 0, 1, :], 0.0))
                mul(pw[:, 1, 0, :], mag, r2[:, 1, :], ALU.mult)
                mul(pw[:, 1, 1, :], mag, r2[:, 0, :], ALU.mult)
                for j in range(2, 9):
                    complex_step(dve, mul, pw[:, j, 0, :], pw[:, j, 1, :], pw[:, j - 1, 0, :], pw[:, j - 1, 1, :],
                                 pw[:, 1, 0, :], pw[:, 1, 1, :], 1, t0)
                op(nc.vector.tensor_scalar(t1, pw[:, 1, 0, :], -1.0, None, ALU.add))
                mul(den, a_re, a_re, ALU.mult)
                mul(t0, a_im, a_im, ALU.mult)
                mul(den, den, t0, ALU.add)
                op(nc.vector.reciprocal(den, den))
                mul(f_re, t1, a_re, ALU.mult)
                mul(t0, pw[:, 1, 1, :], a_im, ALU.mult)
                mul(f_re, f_re, t0, ALU.add)
                mul(f_im, pw[:, 1, 1, :], a_re, ALU.mult)
                mul(t0, t1, a_im, ALU.mult)
                mul(f_im, f_im, t0, ALU.subtract)
                mul(f_re, f_re, den, ALU.mult)
                mul(f_im, f_im, den, ALU.mult)
                wide = lambda a: a.unsqueeze(2).broadcast_to([P, GP, CH])
                complex_step(dve, mul, bb[:, 0], bb[:, 1], bri[:, 0], bri[:, 1], wide(f_re), wide(f_im), 1, tmp)
                for j in range(9):
                    complex_step(dve, mul, cl[:, :, 0, j, :], cl[:, :, 1, j, :], cri[:, 0], cri[:, 1],
                                 wide(pw[:, j, 0, :]), wide(pw[:, j, 1, :]), -1, tmp)

        k_ready, k_free, k_d = sem("k_ready"), sem("k_free"), sem("k_d")
        toe_zero, toe_in = sem("toe_zero"), sem("toe_in")
        with nc.Block() as block:
            @block.gpsimd
            def _(pool):
                nc.gpsimd.memset(m_toe, 0.0).then_inc(toe_zero, 1)
                pool.wait_ge(toe_zero, 1)
                nc.gpsimd.memset(ua[64:P], 0.0).then_inc(toe_zero, 1)

            @block.tensor
            def _(pe):
                for q in range(G // 8):
                    if q >= 2:
                        pe.wait_ge(k_free, 2 * (q - 1))
                    for j in range(8):
                        gp, par_ = 4 * q + j // 2, j % 2
                        half = slice(64 * par_, 64 * par_ + 64)
                        for ri in range(2):
                            last = nc.tensor.matmul(ps[0:CH, 2 * (q % 2) + par_, j // 2 * P:(j // 2 + 1) * P],
                                                    bb[half, ri, gp, :], cl[half, gp, ri, 0:ST8, :],
                                                    start=(ri == 0), stop=(ri == 1))
                        if j >= 6:
                            last.then_inc(k_ready, 1)

            @block.scalar
            def _(act):
                for q in range(G // 8):
                    for par_ in range(2):
                        act.wait_ge(k_ready, 2 * q + 2)
                        nc.scalar.activation(kst[0:CH, 8 * q + par_:8 * q + 8:2].rearrange("p g t c -> p g (t c)"),
                                             ps[0:CH, 2 * (q % 2) + par_, :].rearrange("p (g m) -> p g m", g=4),
                                             ACT.Copy).then_inc(k_free, 1)

            @block.vector
            def _(dve):
                dd = lay(AT_HH, [G, CH])[0:CH]
                nc.vector.tensor_tensor(dd, ident[0:CH, 0:CH].unsqueeze(1).broadcast_to([CH, G, CH]),
                                        d_s5[0:CH].unsqueeze(2).broadcast_to([CH, G, CH]), ALU.mult).then_inc(k_d, 1)
                dve.wait_ge(k_d, 1)
                dve.wait_ge(k_free, G // 4)
                nc.vector.tensor_tensor(kst[0:CH, :, 0, :], kst[0:CH, :, 0, :], dd, ALU.add).then_inc(k_d, 1)

            @block.sync
            def _(sp):
                sp.wait_ge(k_d, 2)
                sp.wait_ge(toe_zero, 1)
                for s in range(ST8):
                    sp.dma_start(m_toe[s * CH:(s + 1) * CH, :, s * CH:P],
                                 kst[0:CH, :, 0:ST8 - s, :].rearrange("p g t c -> p g (t c)")).then_inc(toe_in, 16)
                sp.wait_ge(toe_in, 16 * ST8)

        st = lay(AT_HT, [2, 2, P])
        st4 = lay(AT_HT + 512, [2, 2, P])
        w_v, wT_ready, wT_free, se_ready, se_free = (sem(n) for n in ("w_v", "wT_ready", "wT_free", "se_ready", "se_free"))
        st_out = sem("st_out")
        with nc.Block() as block:
            @block.vector
            def _(dve):
                n = [0]

                def mul(o, a, b, how):
                    n[0] += 1
                    nc.vector.tensor_tensor(o, a, b, how).then_inc(w_v, 1)
                    dve.wait_ge(w_v, n[0])

                wide = lambda a: a.unsqueeze(2).broadcast_to([P, GP, CH])
                for s in range(ST8):
                    complex_step(dve, mul, wk[:, :, 0, s, :], wk[:, :, 1, s, :], bb[:, 0], bb[:, 1],
                                 wide(pw[:, 7 - s, 0, :]), wide(pw[:, 7 - s, 1, :]), 1, tmp)
                nc.vector.memset(neg_lam[:, 0:1], 1.0).then_inc(w_v, 1)
        NW = 6 * ST8

        with nc.Block() as block:
            @block.tensor
            def _(pe):
                def transposes(gp):
                    if gp >= 2:
                        pe.wait_ge(wT_free, gp - 1)
                    for ri in range(2):
                        nc.tensor.transpose(ps[:, gp % 2, ri * P:(ri + 1) * P], wk[:, gp, ri], ident[:, :])
                    for ri in range(2):
                        last = nc.tensor.transpose(ps[0:64, gp % 2, (2 + ri) * P:(3 + ri) * P],
                                                   wk[:, gp, ri, NNEW:ST8, :], ident[:, :])
                    last.then_inc(wT_ready, 1)

                transposes(0)
                for gp in range(GP):
                    if gp + 1 < GP:
                        transposes(gp + 1)
                    pe.wait_ge(wT_free, gp + 1)
                    if gp >= 2:
                        pe.wait_ge(se_free, gp - 1)
                    for par_ in range(2):
                        half = slice(64 * par_, 64 * par_ + 64)
                        for ri in range(2):
                            nc.tensor.matmul(ps[half, 2 + gp % 2, ri * P:(ri + 1) * P], st[:, gp % 2, ri, half],
                                             ug[:, 2 * gp + par_, :], start=True, stop=True)
                            last = nc.tensor.matmul(ps[half, 2 + gp % 2, 256 + ri * NSEQ:256 + (ri + 1) * NSEQ],
                                                    st4[0:64, gp % 2, ri, half], ua[0:64, 2 * gp + par_, :],
                                                    start=True, stop=True)
                    last.then_inc(se_ready, 1)

            @block.scalar
            def _(act):
                for gp in range(GP):
                    act.wait_ge(wT_ready, gp + 1)
                    if gp >= 2:
                        act.wait_ge(se_ready, gp - 1)
                    nc.scalar.activation(st[:, gp % 2].rearrange("p r m -> p (r m)"), ps[:, gp % 2, 0:256], ACT.Copy)
                    nc.scalar.activation(st4[0:64, gp % 2].rearrange("p r m -> p (r m)"), ps[0:64, gp % 2, 256:512],
                                         ACT.Copy).then_inc(wT_free, 1)

            @block.vector
            def _(dve):
                nc.vector.memset(hh[:, :, :, 0:1], 0.0).then_inc(w_v, 1)
                for gp in range(GP):
                    dve.wait_ge(se_ready, gp + 1)
                    nc.vector.tensor_copy(hs[:, :, gp, :], ps[:, 2 + gp % 2, 256:256 + 2 * NSEQ]
                                          .rearrange("p (r q) -> p r q", r=2)).then_inc(w_v, 1)
                    nc.vector.tensor_copy(hh[:, :, gp, 1:NCH + 1], ps[:, 2 + gp % 2, 0:256]
                                          .rearrange("p (r n) -> p r n", r=2)).then_inc(se_free, 1)

        rec = sem("rec")
        ta, tb = lay(AT_HT, [2, GP]), lay(AT_HT + 64, [2, GP])
        t8 = lay(AT_HT + 128, [GP, NSEQ])
        with nc.Block() as block:
            @block.vector
            def _(dve):
                l_re = pw[:, 8, 0, :].unsqueeze(1).broadcast_to([P, 2, GP])
                l_im = pw[:, 8, 1, :]
                with dve.Fori(0, NCH) as n:
                    now, nxt = hh[:, :, :, bass.ds(n, 1)], hh[:, :, :, bass.ds(n + 1, 1)]
                    sq = lambda a: a.rearrange("p r g o -> p r (g o)")
                    now, nxt = sq(now), sq(nxt)
                    dve.wait_ge(rec, n * 4)
                    nc.vector.tensor_tensor(ta, now, l_re, ALU.mult)
                    nc.vector.tensor_tensor(tb[:, 0, :], now[:, 1, :], l_im, ALU.mult)
                    nc.vector.tensor_tensor(tb[:, 1, :], now[:, 0, :], l_im, ALU.mult).then_inc(rec, 1)
                    dve.wait_ge(rec, n * 4 + 1)
                    nc.vector.tensor_tensor(nxt, nxt, ta, ALU.add).then_inc(rec, 1)
                    dve.wait_ge(rec, n * 4 + 2)
                    nc.vector.tensor_tensor(nxt[:, 0, :], nxt[:, 0, :], tb[:, 0, :], ALU.subtract).then_inc(rec, 1)
                    nc.vector.tensor_tensor(nxt[:, 1, :], nxt[:, 1, :], tb[:, 1, :], ALU.add).then_inc(rec, 1)
                wide = lambda a: a.unsqueeze(2).broadcast_to([P, GP, NSEQ])
                m = 4 * NCH
                for dst, src, lam_, how in ((0, 0, 0, ALU.add), (0, 1, 1, ALU.subtract), (1, 0, 1, ALU.add), (1, 1, 0, ALU.add)):
                    dve.wait_ge(rec, m)
                    nc.vector.tensor_tensor(t8, h0[:, src], wide(pw[:, NNEW, lam_, :]), ALU.mult).then_inc(rec, 1)
                    dve.wait_ge(rec, m + 1)
                    nc.vector.tensor_tensor(hs[:, dst], hs[:, dst], t8, how).then_inc(rec, 1)
                    m += 2

            @block.sync
            def _(sp):
                sp.wait_ge(rec, 4 * NCH + 8)
                sp.dma_start(out["s5_prompt"], hh[:, :, :, NCH:NCH + 1], allow_slow_non_contiguous=True).then_inc(st_out, 16)
                sp.dma_start(out["s5_sample"], hs.rearrange("p r g q -> p (r g q)")).then_inc(st_out, 16)
                sp.wait_ge(st_out, 32)

        zs_tok = lay(AT_HT, [NNEW, D])
        y_ready, y_free = sem("y_ready"), sem("y_free")
        with nc.Block() as block:
            @block.tensor
            def _(pe):
                for q in range(G // 8):
                    if q >= 2:
                        pe.wait_ge(y_free, 2 * (q - 1))
                    for j in range(8):
                        g, par_ = 8 * q + j, j % 2
                        half = slice(64 * par_, 64 * par_ + 64)
                        o = ps[:, 2 * (q % 2) + par_, j // 2 * P:(j // 2 + 1) * P]
                        nc.tensor.matmul(o, ug[:, g, :], m_toe[:, g, :], start=True, stop=False)
                        for ri in range(2):
                            last = nc.tensor.matmul(o, hh[half, ri, g // 2, 0:NCH], cl[half, g // 2, ri, 1:9, :],
                                                    start=False, stop=(ri == 1))
                        if j >= 6:
                            last.then_inc(y_ready, 1)
                for q in range(G // 16):
                    if q >= 2:
                        pe.wait_ge(y_free, G // 4 + 2 * (q - 1))
                    for j in range(16):
                        g, par_ = 16 * q + j, j % 2
                        half = slice(64 * par_, 64 * par_ + 64)
                        o = ps[0:NSEQ, 4 + 2 * (q % 2) + par_, j // 2 * 64:(j // 2 + 1) * 64]
                        nc.tensor.matmul(o, ua[:, g, :], m_toe[:, g, 0:64], start=True, stop=False)
                        for ri in range(2):
                            last = nc.tensor.matmul(o, h0[half, ri, g // 2, :], cl[half, g // 2, ri, 1:1 + NNEW, :],
                                                    start=False, stop=(ri == 1))
                        if j >= 14:
                            last.then_inc(y_ready, 1)

            @block.scalar
            def _(act):
                z_g = z_tok.rearrange("p t (g c) -> p t g c", c=CH)
                for q in range(G // 8):
                    for par_ in range(2):
                        act.wait_ge(y_ready, 2 * q + 2)
                        for t in range(ST8):
                            last = nc.scalar.activation(
                                z_g[:, t, 8 * q + par_:8 * q + 8:2],
                                ps[:, 2 * (q % 2) + par_, :].rearrange("p (g t c) -> p t g c", g=4, t=ST8)[:, t], ACT.Gelu)
                        last.then_inc(y_free, 1)
                zs_g = zs_tok.rearrange("p t (g c) -> p t g c", c=CH)
                for q in range(G // 16):
                    for par_ in range(2):
                        act.wait_ge(y_ready, G // 4 + 2 * q + 2)
                        for t in range(NNEW):
                            last = nc.scalar.activation(
                                zs_g[0:NSEQ, t, 16 * q + par_:16 * q + 16:2],
                                ps[0:NSEQ, 4 + 2 * (q % 2) + par_, :].rearrange("p (g t c) -> p t g c", g=8, t=NNEW)[:, t],
                                ACT.Gelu)
                        last.then_inc(y_free, 1)

        AT_ZT, AT_S5O, AT_MT, AT_WB = 0, AT_TOE, AT_TOE + KC * T, AT_WK
        zT = lay(AT_ZT, [KC, T])
        z_ready, z_free = sem("z_ready"), sem("z_free")
        with nc.Block() as block:
            @block.tensor
            def _(pe):
                for n in range(2 * KC):
                    c, b = n // 2, n % 2
                    if n >= 4:
                        pe.wait_ge(z_free, n - 3)
                    for s in range(4):
                        last = nc.tensor.transpose(ps[:, n % 4, s * P:(s + 1) * P],
                                                   z_tok[:, 4 * b + s, c * P:(c + 1) * P], ident[:, :])
                    last.then_inc(z_ready, 1)
                for c in range(KC):
                    for t in range(NNEW):
                        last = nc.tensor.transpose(ps[:, 4, c * NS + t * NSEQ:c * NS + (t + 1) * NSEQ],
                                                   zs_tok[0:NSEQ, t, c * P:(c + 1) * P], ident[0:NSEQ, 0:NSEQ])
                last.then_inc(z_ready, 1)

            @block.vector
            def _(dve):
                for n in range(2 * KC):
                    c, b = n // 2, n % 2
                    dve.wait_ge(z_ready, n + 1)
                    nc.vector.tensor_copy(zT[:, c, 0:SEQ].rearrange("p (n s) -> p s n", s=ST8)[:, 4 * b:4 * b + 4],
                                          ps[:, n % 4, :].rearrange("p (s n) -> p s n", s=4)).then_inc(z_free, 1)
                dve.wait_ge(z_ready, 2 * KC + 1)
                for c in range(KC):
                    last = nc.vector.tensor_copy(zT[:, c, SEQ:T].rearrange("p (q t) -> p t q", t=NNEW),
                                                 ps[:, 4, c * NS:(c + 1) * NS].rearrange("p (t q) -> p t q", t=NNEW))
                last.then_inc(z_free, 1)

        wbuf = lay(AT_WB, [2, D])
        gate = lay(AT_WB + 2 * D, [2, NC3, CW])
        mul_t = lay(AT_WB + 2 * D + 2 * NC3 * CW, [CW])
        s5oT = lay(AT_S5O, [KC, T])
        mT = lay(AT_MT, [KC, T])
        gl_ready, gl_used, hT_back = sem("gl_ready"), sem("gl_used"), sem("hT_back")
        chunk = lambda c: slice(c * CW, (c + 1) * CW)

        def one(a):
            return a.rearrange("p a n -> p (a n)")

        NGLU = KC // 2
        with nc.Block() as block:
            @block.sync
            def _(sp):
                sp.dma_start(hT.rearrange("p c t -> p (c t)"), scr_h).then_inc(hT_back, 16)
                stat_loads(sp, wbuf, T_GLU, NGLU, pairs)
                sp.wait_ge(hT_back, 16)

            @block.tensor
            def _(pe):
                with pe.Fori(0, NGLU) as i:
                    for k in range(2):
                        stat_products(pe, i, k, wbuf, zT, pairs)

            @block.scalar
            def _(act):
                with act.Fori(0, NGLU) as i:
                    for k in range(2):
                        for c in range(NC3):
                            act.wait_ge(acc_ready[k], i * 3 + (3 * pairs + c + 1))
                            act.wait_ge(gl_used, START + i * 6)
                            alone(act)
                            nc.scalar.activation(gate[:, k, c, :], ps[:, 3 * k + c, 0:CW], ACT.Sigmoid,
                                                 bias=b_glu[:, bass.ds(i * 2 + k, 1)]).then_inc(acc_free[k], 1)

            @block.vector
            def _(dve):
                with dve.Fori(0, NGLU) as i:
                    for k in range(2):
                        for c in range(NC3):
                            dve.wait_ge(acc_free[k], i * 3 + (3 * pairs + c + 4))
                            m = bass.ds(i * 2 + k, 1)
                            nc.vector.tensor_tensor(one(s5oT[:, m, chunk(c)]), one(zT[:, m, chunk(c)]), gate[:, k, c, :],
                                                    ALU.mult).then_inc(gl_used, 1)
        pairs += NGLU

        prod = sem("prod")

        def merge(block, tile0, other, fold, pairs):
            @block.sync
            def _(sp):
                stat_loads(sp, wbuf, tile0, KC, pairs)

            @block.tensor
            def _(pe):
                with pe.Fori(0, KC) as i:
                    stat_products(pe, i, 0, wbuf, hT, pairs)
                    stat_products(pe, i, 1, wbuf, other, pairs)

            @block.scalar
            def _(act):
                with act.Fori(0, KC) as i:
                    for c in range(NC3):
                        act.wait_ge(acc_ready[0], i * 3 + (3 * pairs + c + 1))
                        act.wait_ge(acc_free[1], i * 3 + (3 * pairs + 3))
                        nc.scalar.activation(gate[:, 0, c, :], ps[:, c, 0:CW], ACT.Sigmoid).then_inc(acc_free[0], 1)

            @block.vector
            def _(dve):
                with dve.Fori(0, KC) as i:
                    for c in range(NC3):
                        dve.wait_ge(acc_free[0], i * 3 + (3 * pairs + c + 4))
                        dve.wait_ge(acc_ready[1], i * 3 + (3 * pairs + c + 1))
                        dst = one(mT[:, bass.ds(i, 1), chunk(c)])
                        if not fold:
                            nc.vector.tensor_tensor(dst, ps[:, 3 + c, 0:CW], gate[:, 0, c, :], ALU.mult).then_inc(acc_free[1], 1)
                            continue
                        dve.wait_ge(prod, START + i * 3 + c)
                        nc.vector.tensor_tensor(mul_t, ps[:, 3 + c, 0:CW], gate[:, 0, c, :], ALU.mult).then_inc(acc_free[1], 1)
                        dve.wait_ge(acc_free[1], i * 3 + (3 * pairs + c + 4))
                        nc.vector.tensor_tensor(dst, dst, mul_t, ALU.add).then_inc(prod, 1)

        with nc.Block() as block:
            merge(block, T_GS, s5oT, False, pairs)
        pairs += KC

        attT = lay(0, [KC, T])
        AT_MISC, AT_V = KC * T, AT_MT + KC * T
        vall = lay(AT_V, [TT + 1, D])
        v_slab = lay(AT_WB, [2, KC, 512])
        v_ready, v_free, v_out = sem("v_ready"), sem("v_free"), sem("v_out")

        def token_rows(t):
            return (P if t < TT else NS), slice(t * P, t * P + (P if t < TT else NS))

        with nc.Block() as block:
            @block.sync
            def _(sp):
                for k in range(2):
                    sp.dma_start(v_slab[:, k].rearrange("p a b -> p (a b)"), dr["w_mov"][2 + k]).then_inc(slab_in[k], 16)
                for t in range(TT + 1):
                    rows, tok = token_rows(t)
                    sp.wait_ge(v_free, 2 * t + 2)
                    sp.dma_start(out["v"][tok, :], vall[0:rows, t, :]).then_inc(v_out, 16)
                sp.wait_ge(v_out, 16 * (TT + 1))

            @block.tensor
            def _(pe):
                for k in range(2):
                    pe.wait_ge(slab_in[k], 32)
                for t in range(TT + 1):
                    rows, tok = token_rows(t)
                    for k in range(2):
                        n = 2 * t + k
                        if n >= 8:
                            pe.wait_ge(v_free, n - 7)
                        for kc in range(KC):
                            last = nc.tensor.matmul(ps[0:rows, n % 8, :], hT[:, kc, tok], v_slab[:, k, kc, :],
                                                    start=(kc == 0), stop=(kc == KC - 1))
                        last.then_inc(v_ready, 1)

            @block.scalar
            def _(act):
                for t in range(TT + 1):
                    rows, tok = token_rows(t)
                    for k in range(2):
                        act.wait_ge(v_ready, 2 * t + k + 1)
                        nc.scalar.activation(vall[0:rows, t, 512 * k:512 * (k + 1)], ps[0:rows, (2 * t + k) % 8, :],
                                             ACT.Copy).then_inc(v_free, 1)

        A = AT_MISC
        qk_slots = [(lay(A, [T]), lay(A + T, [T])),
                    (lay(AT_WB + 2 * D + 11 * P, [T]), lay(AT_WB + 2 * D + 11 * P + T, [T]))]
        qs, ks = lay(A + 2 * T, [H, NS]), lay(A + 2 * T + 256, [H, NS])
        A += 2 * T + 512
        ex = lay(A, [2, 2, SEQ])
        A += 4 * SEQ
        pT = lay(A, [SEQ // P, P])
        A += SEQ
        osb = lay(A, [TT, P])
        A += SEQ
        nmax, lsum, ssq, subln = lay(A, [2, 2]), lay(A + 4, [2, 2]), lay(A + 8, [TT]), lay(A + 16, [1])
        assert A + 17 <= AT_MT
        causal = lay(AT_WB + 2 * D, [P])
        ko = lay(AT_WB + 2 * D + P, [TT + 1, P])
        junk_a = lay(AT_WB + 2 * D + P + 9 * P, [P])

        names = ("ko_ready", "ko_free", "ko_out", "ko_clear", "s_ready", "s_masked", "m_ready", "e_ready", "l_ready", "p_ready",
                 "t_ready", "t_free", "o_ready", "o_free", "ss_ready", "rt_ready", "on_ready", "oT_ready", "oT_free",
                 "at_in", "qs_ready", "part")
        (ko_ready, ko_free, ko_out, ko_clear, s_ready, s_masked, m_ready, e_ready, l_ready, p_ready, t_ready, t_free,
         o_ready, o_free, ss_ready, rt_ready, on_ready, oT_ready, oT_free, at_in, qs_ready, part) = (sem(n) for n in names)

        def every_head(eng, head):
            with eng.Fori(0, H // 2 - 1) as pair:
                for slot in range(2):
                    head(pair * 2 + slot, slot, True)
            head(H - 2, 0, True)
            head(H - 1, 1, False)

        with nc.Block() as block:
            @block.sync
            def _(sp):
                sp.dma_start(causal, dr["causal"]).then_inc(at_in, 16)
                sp.dma_start(subln, dr["subln"]).then_inc(at_in, 16)
                for k in (1, 0):
                    stat_load(sp, wbuf, k, dr["w_stat"][T_QK + k])

                def k_out(h):
                    sp.wait_ge(ko_free, h * 3 + 3)
                    col = bass.ds(h * P, P)
                    sp.dma_start(out["k"][0:SEQ, col].rearrange("(t p) n -> p t n", p=P), ko[:, 0:TT, :]).then_inc(ko_out, 16)
                    sp.dma_start(out["k"][SEQ:T, col], ko[0:NS, TT, :]).then_inc(ko_out, 16)
                    sp.wait_ge(ko_out, h * 32 + 32)
                    sp.sem_inc(ko_clear, 1)

                with sp.Fori(0, H - 1) as h:
                    for k in (1, 0):
                        sp.wait_ge(acc_ready[k], h * 3 + 3 * (pairs + 1))
                        stat_load(sp, wbuf, k, dr["w_stat"][bass.ds(h * 2 + (T_QK + 2 + k), 1)].rearrange("a p n -> (a p) n"))
                    k_out(h)
                k_out(H - 1)

            @block.tensor
            def _(pe):
                def qk_chunk(h, n):
                    k, c = (1, n) if n < NC3 else (0, n - NC3)
                    if c == 0:
                        pe.wait_ge(w_in[k], h * 16 + 16 * (pairs + 1))
                    if n == NC3:
                        pe.wait_ge(acc_free[1], h * 3 + (3 * pairs + 6))
                    elif c:
                        pe.wait_ge(acc_free[k], h * 3 + (3 * pairs + 3 + c))
                    for kc in range(KC):
                        last = nc.tensor.matmul(ps[:, 7, 0:CW], wbuf[:, k, kc * P:(kc + 1) * P],
                                                hT[:, kc, chunk(c)], start=(kc == 0), stop=(kc == KC - 1))
                    last.then_inc(acc_ready[k], 1)

                def k_by_token(h, slot, r):
                    if r == 0:
                        pe.wait_ge(acc_free[0], h * 3 + (3 * pairs + 6))
                    else:
                        pe.wait_ge(ko_free, h * 3 + r)
                    for t in range(4 * r, min(4 * r + 4, TT + 1)):
                        rows, tok = token_rows(t)
                        last = nc.tensor.transpose(ps[0:rows, 7, (t % 4) * P:(t % 4 + 1) * P], qk_slots[slot][1][:, tok], ident[:, :])
                    last.then_inc(ko_ready, 1)

                def scores(h, slot, i, first=False):
                    qh, kh = qk_slots[slot]
                    for b in range(2):
                        half = slice(64 * b, 64 * b + 64)
                        if not first:
                            pe.wait_ge(e_ready, h * 16 + (2 * i + b - 1))
                        for c in range((i // 4) + 1):
                            w = min(512, (i + 1) * P - 512 * c)
                            last = nc.tensor.matmul(ps[:, 2 * b + c, 0:w], qh[half, i * P:(i + 1) * P],
                                                    kh[half, 512 * c:512 * c + w], start=True, stop=True)
                        last.then_inc(s_ready, 1)

                def head(h, slot, more):
                    for i in range(TT):
                        if i + 1 < TT:
                            scores(h, slot, i + 1)
                        pe.wait_ge(p_ready, h * TT + (i + 1))
                        pe.wait_ge(t_free, START + h * TT + i)
                        for j in range(i + 1):
                            last = nc.tensor.transpose(ps[:, 4 + j // 4, (j % 4) * P:(j % 4 + 1) * P],
                                                       ex[:, i % 2, 0, j * P:(j + 1) * P], ident[:, :])
                        last.then_inc(t_ready, 1)
                        if i == 0:
                            pe.wait_ge(oT_free, START + h * 2)
                            pe.wait_ge(ko_free, h * 3 + 3)
                        if more and i < 2 * NC3:
                            qk_chunk(h + 1, i)
                        elif more:
                            k_by_token(h + 1, 1 - slot, i - 2 * NC3)
                        pe.wait_ge(t_free, START + h * TT + (i + 1))
                        if i:
                            pe.wait_ge(o_free, h * TT + i)
                        for j in range(i + 1):
                            last = nc.tensor.matmul(ps[:, 6, 0:P], pT[:, j, :],
                                                    vall[:, j, bass.ds(h * P, P)], start=(j == 0), stop=(j == i))
                        last.then_inc(o_ready, 1)
                    if more:
                        k_by_token(h + 1, 1 - slot, 2)
                        scores(h + 1, 1 - slot, 0)
                    pe.wait_ge(on_ready, h + 1)
                    for r in range(2):
                        if more and r:
                            pe.wait_ge(ko_free, h * 3 + 6)
                        for t in range(4 * r, 4 * r + 4):
                            last = nc.tensor.transpose(ps[:, 6 + r, (t % 4) * P:(t % 4 + 1) * P], osb[:, t, :], ident[:, :])
                        last.then_inc(oT_ready, 1)

                for n in range(2 * NC3):
                    qk_chunk(0, n)
                for r in range(3):
                    k_by_token(0, 0, r)
                scores(0, 0, 0, first=True)
                every_head(pe, head)

            @block.scalar
            def _(act):
                def q_in(h, slot, c):
                    act.wait_ge(acc_ready[0], h * 3 + (3 * pairs + c + 1))
                    nc.scalar.activation(qk_slots[slot][0][:, chunk(c)], ps[:, 7, 0:CW], ACT.Copy,
                                         scale=HD ** -0.5).then_inc(acc_free[0], 1)

                def k_tiles(h, r):
                    if r == 0:
                        act.wait_ge(ko_clear, START + h)
                    act.wait_ge(ko_ready, h * 3 + (r + 1))
                    if r < 2:
                        nc.scalar.activation(ko[:, 4 * r:4 * r + 4].rearrange("p t n -> p (t n)"), ps[:, 7, :],
                                             ACT.Copy).then_inc(ko_free, 1)
                    else:
                        nc.scalar.activation(ko[0:NS, TT, :], ps[0:NS, 7, 0:P], ACT.Copy).then_inc(ko_free, 1)

                def exps(h, i):
                    for b in range(2):
                        act.wait_ge(m_ready, h * 16 + (2 * i + b + 1))
                        nc.scalar.activation(ex[:, i % 2, b, 0:(i + 1) * P],
                                             ps[:, 2 * b:2 * b + 2, :].rearrange("p a n -> p (a n)")[:, 0:(i + 1) * P],
                                             ACT.Exp, bias=nmax[:, i % 2, b:b + 1],
                                             accum_out=lsum[:, i % 2, b:b + 1]).then_inc(e_ready, 1)

                def head(h, slot, more):
                    for i in range(TT):
                        if more and NC3 < i <= 2 * NC3:
                            q_in(h + 1, 1 - slot, i - NC3 - 1)
                        if more and i == TT - 1:
                            k_tiles(h + 1, 0)
                        act.wait_ge(t_ready, h * TT + (i + 1))
                        nc.scalar.activation(pT[:, 0:i + 1, :].rearrange("p j n -> p (j n)"),
                                             ps[:, 4:6, :].rearrange("p a n -> p (a n)")[:, 0:(i + 1) * P],
                                             ACT.Copy).then_inc(t_free, 1)
                        if i + 1 < TT:
                            exps(h, i + 1)
                    if more:
                        k_tiles(h + 1, 1)
                        k_tiles(h + 1, 2)
                    act.wait_ge(ss_ready, h + 1)
                    nc.scalar.activation(ssq, ssq, ACT.Sqrt).then_inc(rt_ready, 1)
                    if more:
                        exps(h + 1, 0)
                    for r in range(2):
                        act.wait_ge(oT_ready, h * 2 + (r + 1))
                        nc.scalar.activation(one(attT[:, bass.ds(h, 1), 512 * r:512 * (r + 1)]), ps[:, 6 + r, :], ACT.Copy,
                                             scale=subln).then_inc(oT_free, 1)

                act.wait_ge(at_in, 32)
                for c in range(NC3):
                    q_in(0, 0, c)
                for r in range(3):
                    k_tiles(0, r)
                exps(0, 0)
                every_head(act, head)

            @block.vector
            def _(dve):
                def k_in(h, slot, c):
                    dve.wait_ge(acc_ready[1], h * 3 + (3 * pairs + c + 1))
                    nc.vector.tensor_copy(qk_slots[slot][1][:, chunk(c)], ps[:, 7, 0:CW]).then_inc(acc_free[1], 1)

                def samples_in(h, slot):
                    dve.wait_ge(acc_free[0], h * 3 + (3 * pairs + 6))
                    dve.wait_ge(acc_free[1], h * 3 + (3 * pairs + 6))
                    qh, kh = qk_slots[slot]
                    nc.vector.tensor_copy(one(qs[:, bass.ds(h, 1), :]), qh[:, SEQ:T])
                    nc.vector.tensor_copy(one(ks[:, bass.ds(h, 1), :]), kh[:, SEQ:T]).then_inc(qs_ready, 1)

                def maxima(h, i):
                    for b in range(2):
                        n = h * 16 + (2 * i + b + 1)
                        flat = ps[:, 2 * b:2 * b + 2, :].rearrange("p a n -> p (a n)")
                        dve.wait_ge(s_ready, n)
                        diag = flat[:, i * P:(i + 1) * P]
                        nc.vector.tensor_tensor(diag, diag, causal, ALU.add).then_inc(s_masked, 1)
                        dve.wait_ge(s_masked, n)
                        nc.vector.tensor_reduce(nmax[:, i % 2, b:b + 1], flat[:, 0:(i + 1) * P], AX.X, ALU.max,
                                                negate=True).then_inc(m_ready, 1)

                def probabilities(h, i):
                    dve.wait_ge(e_ready, h * 16 + (2 * i + 2))
                    nc.vector.reciprocal(lsum[:, i % 2, :], lsum[:, i % 2, :]).then_inc(l_ready, 1)
                    dve.wait_ge(l_ready, h * 3 * TT + (3 * i + 1))
                    nc.vector.tensor_tensor(lsum[:, i % 2, :], lsum[:, i % 2, :], neg_lam[:, :], ALU.mult).then_inc(l_ready, 1)
                    dve.wait_ge(l_ready, h * 3 * TT + (3 * i + 2))
                    e0, e1 = ex[:, i % 2, 0, 0:(i + 1) * P], ex[:, i % 2, 1, 0:(i + 1) * P]
                    nc.vector.tensor_scalar(e0, e0, lsum[:, i % 2, 0:1], None, ALU.mult).then_inc(l_ready, 1)
                    dve.wait_ge(l_ready, h * 3 * TT + (3 * i + 3))
                    nc.vector.scalar_tensor_tensor(e0, e1, lsum[:, i % 2, 1:2], e0, ALU.mult, ALU.add).then_inc(p_ready, 1)

                def output_in(h, i):
                    dve.wait_ge(o_ready, h * TT + (i + 1))
                    nc.vector.tensor_copy(osb[:, i, :], ps[:, 6, 0:P]).then_inc(o_free, 1)
                    dve.wait_ge(o_free, h * TT + (i + 1))
                    nc.vector.tensor_tensor_reduce(junk_a, osb[:, i, :], osb[:, i, :], 1.0, 0.0, ALU.mult, ALU.add,
                                                   ssq[:, i:i + 1]).then_inc(part, 1)

                def head(h, slot, more):
                    for i in range(TT):
                        probabilities(h, i)
                        if more and 1 <= i <= NC3:
                            k_in(h + 1, 1 - slot, i - 1)
                        if i + 1 < TT:
                            maxima(h, i + 1)
                        elif more:
                            samples_in(h + 1, 1 - slot)
                        if i:
                            output_in(h, i - 1)
                    output_in(h, TT - 1)
                    dve.wait_ge(part, h * TT + TT)
                    s2 = (1.0 - LAM_INIT) ** 2
                    nc.vector.tensor_scalar(ssq, ssq, 1 / (P * s2), EPS / s2, ALU.mult, ALU.add).then_inc(ss_ready, 1)
                    if more:
                        maxima(h + 1, 0)
                    dve.wait_ge(rt_ready, h * 2 + 1)
                    nc.vector.reciprocal(ssq, ssq).then_inc(rt_ready, 1)
                    dve.wait_ge(rt_ready, h * 2 + 2)
                    nc.vector.tensor_tensor(osb, osb, ssq.unsqueeze(2).broadcast_to([P, TT, P]), ALU.mult).then_inc(on_ready, 1)

                dve.wait_ge(at_in, 32)
                for c in range(NC3):
                    k_in(0, 0, c)
                samples_in(0, 0)
                maxima(0, 0)
                every_head(dve, head)
        pairs += H

        NK = SEQ + NS
        ROWS = 2 * H * NNEW
        vpg = lay(AT_V, [PAGES, D])
        v_new = vall[0:NS, TT, :]
        B = AT_MISC + 2 * T + 512
        qpad = lay(B, [H * (ROWS + 8)])
        es, pTs, o4 = lay(B + 576, [NK]), lay(B + 576 + NK, [PAGES + 1, NS]), lay(B + 576 + NK + 288, [D])
        B += 576 + NK + 288 + D
        sgn, c_new, nm_s, l_s, t_s, first_s = (lay(B + j, [1]) for j in range(6))
        pgs, pgv = lay(B + 8, [NSEQ * PAGES], I32), lay(B + 80, [NSEQ * PAGES], I32)
        ss_s = lay(B + 160, [H])
        kpg, kT = lay(AT_WB, [2, D]), lay(AT_WB + 2 * D, [2, H, P])
        C = AT_WB + 4 * D
        causal_new, pick = lay(C, [NSEQ, NS]), lay(C + 256, [NS])
        osm, osq = lay(C + 288, [H, P]), lay(C + 288 + D, [H, P])
        scr_o = nc.dram_tensor("scr_o", (NS, D), F32, kind="Internal").ap()
        n_phys = dr["cache_k"].shape[0]

        names = ("sc_in", "pg_in", "pgv_in", "vp_in", "q_zero", "qp_ready", "kt_ready", "kt_free", "page_used", "sn_ready",
                 "sn_masked", "mn_ready", "en_ready", "ln_ready", "pn_ready", "ptn_ready", "ptn_free", "on_acc", "on_free",
                 "o_out", "sgn_v")
        (sc_in, pg_in, pgv_in, vp_in, q_zero, qp_ready, kt_ready, kt_free, page_used, sn_ready, sn_masked, mn_ready, en_ready,
         ln_ready, pn_ready, ptn_ready, ptn_free, on_acc, on_free, o_out, sgn_v) = (sem(n) for n in names)
        kp_in = [sem(f"kp_in{k}") for k in range(2)]
        flat_s = ps[0:ROWS, 4:7, :].rearrange("p a n -> p (a n)")
        with nc.Block() as block:
            @block.sync
            def _(sp):
                sp.dma_start(causal_new[0:ROWS].rearrange("p a b -> p (a b)"), dr["causal_new"]).then_inc(sc_in, 16)
                sp.dma_start(pick[0:ROWS, :], dr["pick"]).then_inc(sc_in, 16)
                sp.dma_start(first_s[0:ROWS, :], dr["first"]).then_inc(sc_in, 16)
                sp.dma_start(pgs[0:1, :], dr["pages"]).then_inc(pg_in, 16)
                sp.wait_ge(pg_in, 16)
                with sp.Fori(0, NSEQ) as s:
                    for p in range(PAGES):
                        page = sp.value_load(pgs[0:1, bass.ds(s * PAGES + p, 1)], min_val=0, max_val=n_phys - 1)
                        if p < 2:
                            sp.wait_ge(kt_ready, START + s * PAGES)
                        else:
                            sp.wait_ge(kt_ready, START + s * PAGES + (p - 1))
                        sp.dma_start(kpg[:, p % 2, :], dr["cache_k"][bass.ds(page, 1)].rearrange("a p n -> (a p) n")
                                     ).then_inc(kp_in[p % 2], 16)

            @block.gpsimd
            def _(pool):
                pool.dma_start(pgv[0:1, :], dr["pages"]).then_inc(pgv_in, 16)
                pool.wait_ge(pgv_in, 16)
                with pool.Fori(0, NSEQ) as s:
                    pool.wait_ge(on_acc, START + s)
                    for p in range(PAGES):
                        page = pool.value_load(pgv[0:1, bass.ds(s * PAGES + p, 1)], min_val=0, max_val=n_phys - 1)
                        pool.dma_start(vpg[:, p, :], dr["cache_v"][bass.ds(page, 1)].rearrange("a p n -> (a p) n")
                                       ).then_inc(vp_in, 16)

            @block.tensor
            def _(pe):
                pe.wait_ge(sc_in, 48)
                with pe.Fori(0, NSEQ) as s:
                    def page_scores(p):
                        pe.wait_ge(kt_free, START + s * PAGES + (p + 1))
                        for h in range(H):
                            last = nc.tensor.matmul(flat_s[:, p * P:(p + 1) * P], qpad[:, h * ROWS:(h + 1) * ROWS],
                                                    kT[:, p % 2, h, :], start=(h == 0), stop=(h == H - 1))
                        last.then_inc(page_used, 1)

                    pe.wait_ge(on_free, START + s)
                    pe.wait_ge(qp_ready, s + 1)
                    pe.wait_ge(en_ready, START + s)
                    for p in range(PAGES):
                        pe.wait_ge(kp_in[p % 2], s * 64 + 16 * (p // 2 + 1))
                        pe.wait_ge(kt_free, START + s * PAGES + max(p - 1, 0))
                        for h in range(H):
                            last = nc.tensor.transpose(ps[:, 2 * (p % 2) + h // 4, (h % 4) * P:(h % 4 + 1) * P],
                                                       kpg[:, p % 2, h * P:(h + 1) * P], ident[:, :])
                        last.then_inc(kt_ready, 1)
                        if p:
                            page_scores(p - 1)
                    page_scores(PAGES - 1)
                    for h in range(H):
                        last = nc.tensor.matmul(flat_s[:, SEQ:NK], qpad[:, h * ROWS:(h + 1) * ROWS], ks[:, h, :],
                                                start=(h == 0), stop=(h == H - 1))
                    last.then_inc(sn_ready, 1)
                    pe.wait_ge(pn_ready, s + 1)
                    pe.wait_ge(ptn_free, START + s)
                    for p in range(PAGES + 1):
                        w = P if p < PAGES else NS
                        last = nc.tensor.matmul(ps[0:w, 7, p * NS:(p + 1) * NS], es[0:ROWS, p * P:p * P + w], pick[0:ROWS, :],
                                                start=True, stop=True)
                    last.then_inc(ptn_ready, 1)
                    pe.wait_ge(ptn_free, START + s + 1)
                    pe.wait_ge(vp_in, (s + 1) * 16 * PAGES)
                    for h in range(H):
                        o = ps[0:NNEW, h // 4, (h % 4) * P:(h % 4 + 1) * P]
                        cols = slice(h * P, (h + 1) * P)
                        for p in range(PAGES):
                            nc.tensor.matmul(o, pTs[:, p, NNEW * h:NNEW * (h + 1)], vpg[:, p, cols], start=(p == 0), stop=False)
                        last = nc.tensor.matmul(o, pTs[0:NS, PAGES, NNEW * h:NNEW * (h + 1)], v_new[:, cols], start=False, stop=True)
                    last.then_inc(on_acc, 1)

            @block.scalar
            def _(act):
                with act.Fori(0, NSEQ) as s:
                    for p in range(PAGES):
                        act.wait_ge(kt_ready, START + s * PAGES + (p + 1))
                        act.wait_ge(page_used, START + s * PAGES + max(p - 1, 0))
                        nc.scalar.activation(kT[:, p % 2].rearrange("p h n -> p (h n)"),
                                             ps[:, 2 * (p % 2):2 * (p % 2) + 2, :].rearrange("p a n -> p (a n)"),
                                             ACT.Copy).then_inc(kt_free, 1)
                    act.wait_ge(mn_ready, s + 1)
                    act.wait_ge(ptn_ready, START + s)
                    nc.scalar.activation(es[0:ROWS, :], flat_s[:, 0:NK], ACT.Exp, bias=nm_s[0:ROWS, :],
                                         accum_out=l_s[0:ROWS, :]).then_inc(en_ready, 1)
                    act.wait_ge(on_free, START + s + 1)
                    act.dma_start(scr_o[bass.ds(s * NNEW, NNEW), :], o4[0:NNEW, :]).then_inc(o_out, 16)
                    act.wait_ge(o_out, s * 16 + 16)

            @block.vector
            def _(dve):
                nc.vector.memset(qpad, 0.0).then_inc(q_zero, 1)
                dve.wait_ge(q_zero, 1)
                dve.wait_ge(sc_in, 48)
                nl = neg_lam[0:ROWS, 1:2]
                nc.vector.tensor_scalar(t_s[0:ROWS, :], nl, -1.0, 1.0, ALU.mult, ALU.add).then_inc(sgn_v, 1)
                dve.wait_ge(sgn_v, 1)
                nc.vector.tensor_scalar(sgn[0:ROWS, :], first_s[0:ROWS, :], t_s[0:ROWS, 0:1], nl, ALU.mult, ALU.add).then_inc(sgn_v, 1)
                dve.wait_ge(sgn_v, 2)
                diag = qpad.rearrange("p (h x) -> p h x", x=ROWS + 2 * NNEW)
                with dve.Fori(0, NSEQ) as s:
                    dve.wait_ge(sn_ready, START + s)
                    for b in range(2):
                        half = slice(64 * b, 64 * b + 64)
                        last = nc.vector.tensor_copy(diag[half, :, NNEW * b:NNEW * (b + 1)], qs[half, :, bass.ds(s * NNEW, NNEW)])
                    last.then_inc(qp_ready, 1)
                    dve.wait_ge(sn_ready, START + s + 1)
                    new = flat_s[:, SEQ:NK]
                    nc.vector.tensor_tensor(new, new, one(causal_new[0:ROWS, bass.ds(s, 1), :]), ALU.add).then_inc(sn_masked, 1)
                    dve.wait_ge(sn_masked, s + 1)
                    nc.vector.tensor_reduce(nm_s[0:ROWS, :], flat_s[:, 0:NK], AX.X, ALU.max, negate=True).then_inc(mn_ready, 1)
                    dve.wait_ge(en_ready, START + s + 1)
                    nc.vector.reciprocal(l_s[0:ROWS, :], l_s[0:ROWS, :]).then_inc(ln_ready, 1)
                    dve.wait_ge(ln_ready, s * 2 + 1)
                    nc.vector.tensor_tensor(c_new[0:ROWS, :], l_s[0:ROWS, :], sgn[0:ROWS, :], ALU.mult).then_inc(ln_ready, 1)
                    dve.wait_ge(ln_ready, s * 2 + 2)
                    nc.vector.tensor_scalar(es[0:ROWS, :], es[0:ROWS, :], c_new[0:ROWS, 0:1], None, ALU.mult).then_inc(pn_ready, 1)
                    dve.wait_ge(ptn_ready, START + s + 1)
                    dve.wait_ge(on_acc, START + s)
                    nc.vector.tensor_copy(pTs[:, 0:PAGES, :].rearrange("p a b -> p (a b)"), ps[:, 7, 0:PAGES * NS])
                    nc.vector.tensor_copy(pTs[0:NS, PAGES, :], ps[0:NS, 7, PAGES * NS:(PAGES + 1) * NS]).then_inc(ptn_free, 1)
                    dve.wait_ge(on_acc, START + s + 1)
                    nc.vector.tensor_copy(o4[0:NNEW, :], ps[0:NNEW, 0:2, :].rearrange("p a n -> p (a n)")).then_inc(on_free, 1)

        os_in, n_v, n_a, n_pe = sem("os_in"), sem("n_v"), sem("n_a"), sem("n_pe")
        with nc.Block() as block:
            @block.sync
            def _(sp):
                sp.dma_start(osm[0:NS].rearrange("p h n -> p (h n)"), scr_o).then_inc(os_in, 16)

            @block.vector
            def _(dve):
                dve.wait_ge(os_in, 16)
                o, q, r = osm[0:NS], osq[0:NS], ss_s[0:NS]
                s2 = (1.0 - LAM_INIT) ** 2
                nc.vector.tensor_tensor(q, o, o, ALU.mult).then_inc(n_v, 1)
                dve.wait_ge(n_v, 1)
                nc.vector.tensor_reduce(r, q, AX.X, ALU.add).then_inc(n_v, 1)
                dve.wait_ge(n_v, 2)
                nc.vector.tensor_scalar(r, r, 1 / (P * s2), EPS / s2, ALU.mult, ALU.add).then_inc(n_v, 1)
                dve.wait_ge(n_a, 1)
                nc.vector.reciprocal(r, r).then_inc(n_v, 1)
                dve.wait_ge(n_v, 4)
                nc.vector.tensor_tensor(o, o, r.unsqueeze(2).broadcast_to([NS, H, P]), ALU.mult).then_inc(n_v, 1)

            @block.tensor
            def _(pe):
                pe.wait_ge(n_v, 5)
                for h in range(H):
                    last = nc.tensor.transpose(ps[:, 0, h * NS:(h + 1) * NS], osm[0:NS, h, :], ident[0:NS, 0:NS])
                last.then_inc(n_pe, 1)

            @block.scalar
            def _(act):
                act.wait_ge(n_v, 3)
                nc.scalar.activation(ss_s[0:NS], ss_s[0:NS], ACT.Sqrt).then_inc(n_a, 1)
                act.wait_ge(n_pe, 1)
                nc.scalar.activation(attT[:, :, SEQ:T], ps[:, 0, 0:H * NS].rearrange("p (h t) -> p h t", h=H), ACT.Copy,
                                     scale=subln).then_inc(n_a, 1)

        with nc.Block() as block:
            merge(block, T_GA, attT, True, pairs)
        pairs += KC

        h2T = lay(AT_V, [KC, T])
        o_slab = lay(AT_WB, [2, KC, 512])
        xr, x1, hn = lay(0, [2, D]), lay(2 * D, [2, D]), lay(4 * D, [2, D])
        hg, g_row, junk6, ss6 = lay(6 * D, [2, D]), lay(8 * D, [D]), lay(9 * D, [D]), lay(10 * D, [2])
        scr_x1 = nc.dram_tensor("scr_x1", (T, D), F32, kind="Internal").ap()
        scr_h2 = nc.dram_tensor("scr_h2", (T, D), F32, kind="Internal").ap()
        NB = TT + 1
        os_w, gr_in = sem("os_w"), sem("gr_in")
        x1_acc, x1_ready, hg_ready = sem("x1_acc"), sem("x1_ready"), sem("hg_ready")
        x1_out = [sem(f"x1_out{k}") for k in range(2)]
        with nc.Block() as block:
            @block.sync
            def _(sp):
                for k in range(2):
                    sp.dma_start(o_slab[:, k].rearrange("p a b -> p (a b)"), dr["w_mov"][4 + k]).then_inc(os_w, 16)
                sp.dma_start(g_row, dr["g_ffn_row"].broadcast_to([P, D])).then_inc(gr_in, 16)
                for t in range(TT + 1):
                    rows, tok = token_rows(t)
                    if t >= 2:
                        sp.wait_ge(x1_ready, t - 1)
                    sp.dma_start(xr[0:rows, t % 2, :], dr["x"][tok, :]).then_inc(x_in[t % 2], 16)
                    if t >= 1:
                        r2, k2 = token_rows(t - 1)
                        sp.wait_ge(x1_ready, t)
                        sp.dma_start(scr_x1[k2, :], x1[0:r2, (t - 1) % 2, :]).then_inc(x1_out[(t - 1) % 2], 16)
                        sp.wait_ge(hg_ready, t)
                        sp.dma_start(scr_h2[k2, :], hg[0:r2, (t - 1) % 2, :]).then_inc(x1_out[(t - 1) % 2], 16)
                sp.wait_ge(x1_ready, TT + 1)
                sp.dma_start(scr_x1[SEQ:T, :], x1[0:NS, 0, :]).then_inc(x1_out[0], 16)
                sp.wait_ge(hg_ready, TT + 1)
                sp.dma_start(scr_h2[SEQ:T, :], hg[0:NS, 0, :]).then_inc(x1_out[0], 16)
                sp.wait_ge(x1_out[0], 32 * (TT // 2 + 1))
                sp.wait_ge(x1_out[1], 32 * (TT // 2))

            @block.tensor
            def _(pe):
                def turn(t):
                    rows, tok = token_rows(t)
                    pe.wait_ge(xn_done, NB + t + 1)
                    pe.wait_ge(hT_done, START + NB + t)
                    for c in range(KC):
                        last = nc.tensor.transpose(ps[:, 4 + c // 4, (c % 4) * P:(c % 4) * P + rows],
                                                   hn[0:rows, t % 2, c * P:(c + 1) * P], ident[0:rows, 0:rows])
                    last.then_inc(xT_done, 1)

                pe.wait_ge(os_w, 32)
                for t in range(TT + 1):
                    rows, tok = token_rows(t)
                    if t >= 2:
                        pe.wait_ge(x1_ready, t - 1)
                    for k in range(2):
                        for kc in range(KC):
                            last = nc.tensor.matmul(ps[0:rows, 2 * (t % 2) + k, :], mT[:, kc, tok], o_slab[:, k, kc, :],
                                                    start=(kc == 0), stop=(kc == KC - 1))
                    last.then_inc(x1_acc, 1)
                    if t:
                        turn(t - 1)
                turn(TT)

            @block.vector
            def _(dve):
                dve.wait_ge(gr_in, 16)
                for t in range(TT + 1):
                    rows, tok = token_rows(t)
                    k = t % 2
                    dve.wait_ge(x1_acc, t + 1)
                    dve.wait_ge(x_in[k], 16 * (t // 2 + 1) + 16 * (TT // 2 + 1 - k))
                    if t >= 2:
                        dve.wait_ge(x1_out[k], 32 * (t // 2))
                        dve.wait_ge(xn_done, NB + t - 1)
                    nc.vector.tensor_tensor(x1[0:rows, k, :], xr[0:rows, k, :],
                                            ps[0:rows, 2 * k:2 * k + 2, :].rearrange("p a n -> p (a n)"),
                                            ALU.add).then_inc(x1_ready, 1)
                    s = ss6[0:rows, k:k + 1]
                    dve.wait_ge(sq_done, NB + t + 1)
                    nc.vector.tensor_scalar(s, s, 1.0 / D, EPS, ALU.mult, ALU.add).then_inc(ms_done, 1)
                    dve.wait_ge(rt_done, NB + t + 1)
                    nc.vector.reciprocal(s, s).then_inc(rc_done, 1)
                    dve.wait_ge(xn_done, NB + t + 1)
                    nc.vector.tensor_tensor(hg[0:rows, k, :], hn[0:rows, k, :], g_row[0:rows, :], ALU.mult).then_inc(hg_ready, 1)
                    dve.wait_ge(xT_done, NB + t + 1)
                    for b in range(2):
                        last = nc.vector.tensor_tensor(
                            h2T[:, 4 * b:4 * b + 4, tok],
                            ps[:, 4 + b, :].rearrange("p (c t) -> p c t", c=4)[:, :, 0:rows],
                            g_ffn[:, 4 * b:4 * b + 4].unsqueeze(2).broadcast_to([P, 4, rows]), ALU.mult)
                    last.then_inc(hT_done, 1)

            @block.scalar
            def _(act):
                for t in range(TT + 1):
                    rows, tok = token_rows(t)
                    k = t % 2
                    s = ss6[0:rows, k:k + 1]
                    act.wait_ge(x1_ready, t + 1)
                    nc.scalar.activation(junk6[0:rows, :], x1[0:rows, k, :], ACT.Square, accum_out=s).then_inc(sq_done, 1)
                    act.wait_ge(ms_done, NB + t + 1)
                    nc.scalar.activation(s, s, ACT.Sqrt).then_inc(rt_done, 1)
                    act.wait_ge(rc_done, NB + t + 1)
                    if t >= 2:
                        act.wait_ge(xT_done, NB + t - 1)
                        act.wait_ge(hg_ready, t - 1)
                    nc.scalar.activation(hn[0:rows, k, :], x1[0:rows, k, :], ACT.Copy, scale=s).then_inc(xn_done, 1)

        NQ = 2 * PH
        qp = lay(0, [NQ * T + P])
        qpT = qp[:, 0:NQ * T].rearrange("p (m t) -> p m t", t=T)
        keys = lay(NQ * T + P, [NQ, PK])
        keys_in, pad_zero = sem("keys_in"), sem("pad_zero")
        RING, STEP = 8, TOPK
        PAIR = 2
        A = NQ * T + P + NQ * PK
        def take(shape, dt=F32):
            nonlocal A
            at, A = A, A + int(np.prod(shape))
            return lay(at, shape, dt)
        ring = take([RING, 2 * D])
        h2, x1b, yo, g_fin, junk_y = (take([D]) for _ in range(5))
        junk = take([2, D])
        diag = take([4, P])
        qst = take([2, P])
        sct, s2t = take([2, PK]), take([2, PK])
        vals, idxu, idxf = take([2, TOPK]), take([2, TOPK], U32), take([2, TOPK])
        cand, cand2 = take([TOPK, TOPK]), take([TOPK * TOPK])
        sv, si, sab, sabf = take([TOPK]), take([TOPK], U32), take([2, TOPK], U32), take([2, TOPK])
        hot, e12 = take([2, TOPK, TOPK]), take([2, TOPK])
        iota = take([TOPK])
        logit_next, gates, gsum = take([PH * TOPK]), take([PH, TOPK]), take([PH])
        idx_next, idx_cur, idx_st = take([PH * TOPK], U32), take([PH * TOPK], U32), take([STEP], U32)
        act_in, act_out, wgt = take([STEP]), take([PAIR]), take([PAIR])
        ss8 = take([1])
        assert A <= ARENA
        KCH = 16

        names = ("pc_in", "h2_in", "x1_in", "q_st", "s_acc", "sc_done", "tk_v", "tk_done", "idx_cp", "idx_stg",
                 "slot_free", "dots", "gelu_d", "wgt_d", "diag_d", "init_d", "ex_d", "gt_v",
                 "yo_d", "y_out", "acc_out", "yo_clear")
        (pc_in, h2_in, x1_in, q_st, s_acc, sc_done, tk_v, tk_done, idx_cp, idx_stg, slot_free, dots, gelu_d, wgt_d, diag_d,
         init_d, ex_d, gt_v, yo_d, y_out, acc_out, yo_clear) = (sem(n) for n in names)
        row_in = [sem(f"row_in{k}") for k in range(RING)]
        acc = ps[:, 0:2, :].rearrange("p a n -> p (a n)")

        def choose_act(act, t, b, h):
            act.wait_ge(s_acc, START + t)
            alone(act)
            for k in range(2):
                last = nc.scalar.activation(qst[:, k, :], qp[:, bass.ds(h * (2 * T) + b * P + k * T, P)], ACT.Copy)
            last.then_inc(q_st, 1)
            act.wait_ge(s_acc, START + t + 1)
            act.wait_ge(tk_done, START + t)
            nc.scalar.activation(sct.rearrange("p a n -> p (a n)"), ps[:, 6, 0:2 * PK], ACT.Copy).then_inc(sc_done, 1)

        def choose_pe(pe, t, h):
            pe.wait_ge(q_st, t + 1)
            pe.wait_ge(sc_done, START + t)
            for k in range(2):
                last = nc.tensor.matmul(ps[:, 6, k * PK:(k + 1) * PK], qst[:, k, :], one(keys[:, bass.ds(h * 2 + k, 1), :]),
                                        start=True, stop=True)
            last.then_inc(s_acc, 1)

        def choose_dve(dve, t, h, copied):
            link = [0]

            def done(ins):
                link[0] += 1
                ins.then_inc(tk_v, 1)
                dve.wait_ge(tk_v, t * KCH + link[0])
                alone(dve)

            v = nc.vector
            dve.wait_ge(sc_done, START + t + 1)
            alone(dve)
            for k in range(2):
                last = v.max(vals[:, k, 0:8], sct[:, k, :])
            done(last)
            for k in range(2):
                v.match_replace(s2t[:, k, :], vals[:, k, 0:8], sct[:, k, :], LOWEST)
                last = v.max_index(idxu[:, k, 0:8], vals[:, k, 0:8], sct[:, k, :])
            done(last)
            for k in range(2):
                last = v.max(vals[:, k, 8:16], s2t[:, k, :])
            done(last)
            for k in range(2):
                v.max_index(idxu[:, k, 8:16], vals[:, k, 8:16], s2t[:, k, :])
            last = v.tensor_tensor(cand, vals[:, 0, :].unsqueeze(2).broadcast_to([P, TOPK, TOPK]),
                                   vals[:, 1, :].unsqueeze(1).broadcast_to([P, TOPK, TOPK]), ALU.add)
            done(last)
            flat = cand.rearrange("p a b -> p (a b)")
            last = v.tensor_copy(idxf.rearrange("p a b -> p (a b)"), idxu.rearrange("p a b -> p (a b)"))
            done(v.max(sv[:, 0:8], flat))
            v.match_replace(cand2, sv[:, 0:8], flat, LOWEST)
            done(v.max_index(si[:, 0:8], sv[:, 0:8], flat))
            done(v.max(sv[:, 8:16], cand2))
            done(v.max_index(si[:, 8:16], sv[:, 8:16], cand2))
            v.tensor_scalar(sab[:, 0, :], si, 4, None, ALU.logical_shift_right)
            done(v.tensor_scalar(sab[:, 1, :], si, 15, None, ALU.bitwise_and))
            done(v.tensor_copy(sabf.rearrange("p a b -> p (a b)"), sab.rearrange("p a b -> p (a b)")))
            for k in range(2):
                last = v.tensor_tensor(hot[:, k], sabf[:, k, :].unsqueeze(2).broadcast_to([P, TOPK, TOPK]),
                                       iota.unsqueeze(1).broadcast_to([P, TOPK, TOPK]), ALU.is_equal)
            done(last)
            for k in range(2):
                last = v.tensor_tensor(hot[:, k], hot[:, k], idxf[:, k, :].unsqueeze(1).broadcast_to([P, TOPK, TOPK]), ALU.mult)
            done(last)
            done(v.tensor_reduce(e12.rearrange("p a b -> p (a b)"), hot.rearrange("p k a b -> p (k a) b"), AX.X, ALU.add))
            mine = bass.ds(h * TOPK, TOPK)
            done(v.tensor_scalar(logit_next[:, mine], sv, sv[:, 0:1], None, ALU.subtract))
            done(v.tensor_scalar(e12[:, 0, :], e12[:, 0, :], float(PK), None, ALU.mult))
            dve.wait_ge(idx_cp, START + copied)
            done(v.tensor_tensor(idx_next[:, mine], e12[:, 0, :], e12[:, 1, :], ALU.add))
            assert link[0] == KCH, link
            v.tensor_copy(e12[:, 0, 0:1], e12[:, 1, 0:1]).then_inc(tk_done, 1)

        with nc.Block() as block:
            @block.gpsimd
            def _(pool):
                nc.gpsimd.memset(qp[:, NQ * T:], 0.0).then_inc(pad_zero, 1)

            @block.sync
            def _(sp):
                sp.dma_start(keys.rearrange("p m k -> p (m k)"), dr["keys"]).then_inc(keys_in, 16)
                sp.dma_start(iota, dr["iota16"]).then_inc(pc_in, 16)
                stat_loads(sp, wbuf, T_QUERY, PH, pairs)
                sp.wait_ge(keys_in, 16)

            @block.tensor
            def _(pe):
                pe.wait_ge(keys_in, 16)
                for k in range(2):
                    stat_products(pe, 0, k, wbuf, h2T, pairs)
                with pe.Fori(1, PH) as i:
                    for k in range(2):
                        stat_products(pe, i, k, wbuf, h2T, pairs)
                    choose_pe(pe, i - 1, i - 1)
                choose_pe(pe, PH - 1, PH - 1)

            @block.scalar
            def _(act):
                with act.Fori(0, PH) as i:
                    for c in range(NC3):
                        act.wait_ge(acc_ready[0], i * 3 + (3 * pairs + c + 1))
                        nc.scalar.activation(one(qpT[:, bass.ds(i * 2, 1), chunk(c)]), ps[:, c, 0:CW],
                                             ACT.Copy).then_inc(acc_free[0], 1)
                    for k in range(2):
                        act.wait_ge(acc_free[k], i * 3 + (3 * pairs + 6))
                    choose_act(act, i, 0, i)

            @block.vector
            def _(dve):
                dve.wait_ge(pc_in, 16)
                with dve.Fori(0, PH) as i:
                    for c in range(NC3):
                        dve.wait_ge(acc_ready[1], i * 3 + (3 * pairs + c + 1))
                        nc.vector.tensor_copy(one(qpT[:, bass.ds(i * 2 + 1, 1), chunk(c)]), ps[:, 3 + c, 0:CW]
                                              ).then_inc(acc_free[1], 1)
                    choose_dve(dve, i, i, 0)
        pairs += PH

        def gather_pool(pool, g, col):
            for half in range(STEP // RING):
                cols = slice(half * RING, (half + 1) * RING)
                nc.gpsimd.tensor_copy(idx_st[:, cols], idx_cur[:, bass.ds(col + half * RING, RING)]).then_inc(idx_stg, 1)
                pool.wait_ge(idx_stg, g * 2 + (half + 1))
                alone(pool)
                for j in range(half * RING, (half + 1) * RING):
                    pool.wait_ge(slot_free, g * STEP + (j + 1))
                    alone(pool)
                    pool.indirect_dma_start(ring[:, j % RING, :], None, dr["uv"],
                                            bass.IndirectOffsetOnAxis(ap=idx_st[:, j:j + 1], axis=0)
                                            ).then_inc(row_in[j % RING], 16)

        def gather_dve(dve, g, j):
            dve.wait_ge(row_in[j % RING], g * (16 * STEP // RING) + 16 * (j // RING + 1))
            if j == 0:
                dve.wait_ge(gelu_d, START + g * (STEP // PAIR))
            dve.wait_ge(dots, START + g * STEP + max(j - 1, 0))
            nc.vector.tensor_tensor_reduce(junk[:, j % 2, :], ring[:, j % RING, 0:D], h2, 1.0, 0.0, ALU.mult, ALU.add,
                                           act_in[:, j:j + 1]).then_inc(dots, 1)

        def gather_act(act, g, col, p, gate_of, pattern, m):
            n = g * (STEP // PAIR) + p
            act.wait_ge(dots, START + g * STEP + PAIR * (p + 1))
            nc.scalar.activation(act_out, act_in[:, PAIR * p:PAIR * (p + 1)], ACT.Gelu).then_inc(gelu_d, 1)
            act.wait_ge(gelu_d, START + n + 1)
            alone(act)
            for q in range(PAIR):
                last = nc.scalar.activation(wgt[:, q:q + 1], gate_of[:, bass.ds(col + (PAIR * p + q), 1)], ACT.Copy,
                                            scale=act_out[:, q:q + 1])
            last.then_inc(wgt_d, 1)
            act.wait_ge(wgt_d, n + 1)
            for q in range(PAIR):
                j = PAIR * p + q
                act.wait_ge(slot_free, g * STEP + (j + RING - 3))
                nc.scalar.activation(diag[:, j % 4, 0:m], pattern, ACT.Copy, scale=wgt[:, q:q + 1]).then_inc(diag_d, 1)

        def gather_pe(pe, g, j, m):
            pe.wait_ge(diag_d, START + g * STEP + (j + 1))
            alone(pe)
            for c in range(2):
                last = nc.tensor.matmul(ps[0:m, c, :], diag[:, j % 4, 0:m],
                                        ring[:, j % RING, D + 512 * c:D + 512 * (c + 1)],
                                        start=False, stop=False, skip_group_check=True)
            last.then_inc(slot_free, 1)

        gates_flat = gates.rearrange("p a b -> p (a b)")

        def first_act(act, b):
            act.wait_ge(tk_done, START + b * PH + PH)
            act.wait_ge(diag_d, START + b * (PH * STEP))
            nc.scalar.activation(gates_flat, logit_next, ACT.Exp).then_inc(ex_d, 1)
            act.wait_ge(gt_v, b * 3 + 3)

        def first_dve(dve, b):
            dve.wait_ge(ex_d, b + 1)
            nc.vector.tensor_reduce(gsum, gates, AX.X, ALU.add).then_inc(gt_v, 1)
            dve.wait_ge(gt_v, b * 3 + 1)
            nc.vector.reciprocal(gsum, gsum).then_inc(gt_v, 1)
            dve.wait_ge(gt_v, b * 3 + 2)
            nc.vector.tensor_tensor(gates, gates, gsum.unsqueeze(2).broadcast_to([P, PH, TOPK]), ALU.mult).then_inc(gt_v, 1)
            dve.wait_ge(h2_in, b * 16 + 16)
            alone(dve)

        def first_pe(pe, b, m):
            pe.wait_ge(acc_out, START + b)
            pe.wait_ge(x1_in, b * 16 + 16)
            for c in range(2):
                last = nc.tensor.matmul(ps[0:m, c, :], ident[:, 0:m], x1b[:, 512 * c:512 * (c + 1)],
                                        start=True, stop=False, skip_group_check=True)
            last.then_inc(init_d, 1)

        def first_sp(sp, b):
            sp.wait_ge(dots, START + b * (PH * STEP))
            sp.dma_start(h2, scr_h2[bass.ds(b * P, P), :]).then_inc(h2_in, 16)
            sp.wait_ge(init_d, START + b)
            sp.dma_start(x1b, scr_x1[bass.ds(b * P, P), :]).then_inc(x1_in, 16)

        def first_pool(pool, b):
            pool.wait_ge(tk_done, START + b * PH + PH)
            alone(pool)
            nc.gpsimd.tensor_copy(idx_cur, idx_next).then_inc(idx_cp, 1)
            pool.wait_ge(idx_cp, START + b + 1)
            alone(pool)

        def last_act(act, b, rows):
            act.wait_ge(acc_out, START + b + 1)
            nc.scalar.activation(junk_y[0:rows], yo[0:rows], ACT.Square, accum_out=ss8[0:rows]).then_inc(sq_done, 1)
            act.wait_ge(ms_done, 2 * NB + b + 1)
            nc.scalar.activation(ss8[0:rows], ss8[0:rows], ACT.Sqrt).then_inc(rt_done, 1)

        def last_dve(dve, b, rows):
            dve.wait_ge(slot_free, b * (PH * STEP) + (PH * STEP if b is not TT else 2 * STEP) + RING)
            dve.wait_ge(yo_clear, START + b)
            nc.vector.tensor_copy(yo[0:rows], acc[0:rows]).then_inc(acc_out, 1)

        def norm_dve(dve, b, rows):
            s = ss8[0:rows]
            dve.wait_ge(sq_done, 2 * NB + b + 1)
            nc.vector.tensor_scalar(s, s, 1.0 / D, EPS, ALU.mult, ALU.add).then_inc(ms_done, 1)
            dve.wait_ge(rt_done, 2 * NB + b + 1)
            nc.vector.reciprocal(s, s).then_inc(rc_done, 1)
            dve.wait_ge(rc_done, 2 * NB + b + 1)
            nc.vector.scalar_tensor_tensor(yo[0:rows], yo[0:rows], s, g_fin[0:rows], ALU.mult, ALU.mult).then_inc(yo_d, 1)

        def store_sp(sp, b, rows):
            sp.wait_ge(yo_d, START + b + 1)
            sp.dma_start(out["y"][bass.ds(b * P, rows), :], yo[0:rows]).then_inc(y_out, 16)
            sp.wait_ge(y_out, b * 16 + 16)
            sp.sem_inc(yo_clear, 1)

        spread, gates_s = take([NS]), take([2 * STEP])
        spread_in, spread_i, spread_g, x1_zero = sem("spread_in"), sem("spread_i"), sem("spread_g"), sem("x1_zero")
        QS = P // NS

        with nc.Block() as block:
            @block.sync
            def _(sp):
                sp.dma_start(g_fin, dr["g_fin_row"].broadcast_to([P, D])).then_inc(pc_in, 16)
                sp.dma_start(spread, dr["spread"]).then_inc(pc_in, 16)
                first_sp(sp, 0)
                with sp.Fori(0, TT - 1) as b:
                    first_sp(sp, b + 1)
                    store_sp(sp, b, P)
                sp.wait_ge(tk_done, START + (TT + 1) * PH)
                sp.wait_ge(idx_stg, TT * PH * STEP // RING)
                for q in range(QS):
                    sp.dma_start(idx_cur[q * NS:(q + 1) * NS, 0:NS], idx_next[0:NS, q * NS:(q + 1) * NS]).then_inc(spread_i, 16)
                sp.wait_ge(gt_v, 3 * (TT + 1))
                for q in range(QS):
                    sp.dma_start(gates_s[q * NS:(q + 1) * NS], gates_flat[0:NS, q * NS:(q + 1) * NS]).then_inc(spread_g, 16)
                sp.wait_ge(dots, START + TT * PH * STEP)
                for q in range(QS):
                    sp.dma_start(h2[q * NS:(q + 1) * NS], scr_h2[SEQ:T, :]).then_inc(spread_in, 16)
                sp.wait_ge(x1_zero, 1)
                sp.dma_start(x1b[0:NS], scr_x1[SEQ:T, :]).then_inc(x1_in, 16)
                store_sp(sp, TT - 1, P)
                store_sp(sp, TT, NS)

            @block.gpsimd
            def _(pool):
                with pool.Fori(0, TT) as b:
                    first_pool(pool, b)
                    with pool.Fori(0, PH) as h:
                        gather_pool(pool, b * PH + h, h * STEP)
                pool.wait_ge(spread_i, 16 * QS)
                for s in range(2):
                    gather_pool(pool, TT * PH + s, s * STEP)

            @block.scalar
            def _(act):
                def steps(b):
                    with act.Fori(0, PH) as h:
                        choose_act(act, b * PH + h + PH, b + 1, h)
                        for p in range(STEP // PAIR):
                            gather_act(act, b * PH + h, h * STEP, p, gates_flat, ident[:, :], P)

                first_act(act, 0)
                steps(0)
                with act.Fori(1, TT) as b:
                    first_act(act, b)
                    last_act(act, b - 1, P)
                    steps(b)
                first_act(act, TT)
                last_act(act, TT - 1, P)
                act.wait_ge(spread_g, 16 * QS)
                for s in range(2):
                    for p in range(STEP // PAIR):
                        gather_act(act, TT * PH + s, s * STEP, p, gates_s, spread, NS)
                last_act(act, TT, NS)

            @block.tensor
            def _(pe):
                pe.sem_inc(slot_free, RING)
                with pe.Fori(0, TT) as b:
                    first_pe(pe, b, P)
                    with pe.Fori(0, PH) as h:
                        choose_pe(pe, b * PH + h + PH, h)
                        for j in range(STEP):
                            gather_pe(pe, b * PH + h, j, P)
                first_pe(pe, TT, NS)
                for s in range(2):
                    for j in range(STEP):
                        gather_pe(pe, TT * PH + s, j, NS)

            @block.vector
            def _(dve):
                def steps(b):
                    with dve.Fori(0, PH) as h:
                        for j in range(STEP):
                            gather_dve(dve, b * PH + h, j)
                            if j == 3:
                                choose_dve(dve, b * PH + h + PH, h, b + 1)

                dve.wait_ge(pc_in, 48)
                first_dve(dve, 0)
                steps(0)
                with dve.Fori(1, TT) as b:
                    last_dve(dve, b - 1, P)
                    first_dve(dve, b)
                    norm_dve(dve, b - 1, P)
                    steps(b)
                last_dve(dve, TT - 1, P)
                dve.wait_ge(init_d, START + TT)
                nc.vector.memset(x1b, 0.0).then_inc(x1_zero, 1)
                dve.wait_ge(ex_d, TT + 1)
                nc.vector.tensor_reduce(gsum, gates, AX.X, ALU.add).then_inc(gt_v, 1)
                dve.wait_ge(gt_v, TT * 3 + 1)
                nc.vector.reciprocal(gsum, gsum).then_inc(gt_v, 1)
                dve.wait_ge(gt_v, TT * 3 + 2)
                nc.vector.tensor_tensor(gates, gates, gsum.unsqueeze(2).broadcast_to([P, PH, TOPK]), ALU.mult).then_inc(gt_v, 1)
                norm_dve(dve, TT - 1, P)
                dve.wait_ge(spread_in, 16 * QS)
                for s in range(2):
                    for j in range(STEP):
                        gather_dve(dve, TT * PH + s, j)
                last_dve(dve, TT, NS)
                norm_dve(dve, TT, NS)


def _layouts(a):
    import numpy as np
    def f(x):
        return np.ascontiguousarray(x)
    def stationary(w):
        n = w.shape[1] // 128
        return w.reshape(8, 128, n, 128).transpose(2, 1, 0, 3).reshape(n, 128, 1024)
    def moving(w):
        n = w.shape[1] // 512
        return w.reshape(8, 128, n, 512).transpose(2, 1, 0, 3).reshape(n, 128, 4096)
    def pairs(x, y):
        return np.stack([x, y], 1).reshape(-1, 128, 1024)
    def by_state(x):
        return np.moveaxis(x.reshape((32, 2, 64) + x.shape[2:]), 0, 2).reshape((128, 32) + x.shape[2:])
    w_in = a["w_in"][0]
    q, k, v, u, ga, gs = (w_in[:, i * 1024:(i + 1) * 1024] for i in range(6))
    g64 = (64, 64)
    d = {
        "x": np.concatenate([a["x_prompt"].reshape(1024, 1024), a["x_sample"].reshape(32, 1024)]),
        "ident": np.eye(128, dtype=np.float32),
        "g_mix": a["norm_mix_g"].reshape(8, 128).T,
        "g_ffn": a["norm_ffn_g"].reshape(8, 128).T,
        "b_glu": a["b_glu"].reshape(8, 128).T,
        "lam": np.concatenate([a["lambda_q1"], a["lambda_k1"], a["lambda_q2"], a["lambda_k2"]], 1),
        "w_stat": np.concatenate([pairs(stationary(q), stationary(k)),
                                  pairs(stationary(gs), stationary(a["w_proj_s5"][0])),
                                  stationary(a["w_glu"][0]),
                                  pairs(stationary(ga), stationary(a["w_proj_att"][0])),
                                  stationary(a["peer_w_query"][0])]),
        "w_mov": np.concatenate([moving(u), moving(v), moving(a["w_out"][0])]),
        "a_re": by_state(a["s5_a_re"][0]), "a_im": by_state(a["s5_a_im"][0]),
        "log_step": by_state(np.broadcast_to(a["s5_log_step"][0][:, None], g64)),
        "b_ri": np.stack([by_state(a["s5_b_re"][0]), by_state(a["s5_b_im"][0])], 1).reshape(128, -1),
        "c_ri": np.stack([by_state(a["s5_c_re"][0].transpose(0, 2, 1)),
                          by_state(a["s5_c_im"][0].transpose(0, 2, 1))], 1).reshape(128, -1),
        "h0": np.stack([by_state(a["state_s5_re"][0].transpose(1, 2, 0)),
                        by_state(a["state_s5_im"][0].transpose(1, 2, 0))], 1).reshape(128, -1),
        "d_s5": a["s5_d"][0].T,
        "keys": a["peer_sub_keys"][0].transpose(3, 0, 1, 2).reshape(128, 2048),
        "uv": np.concatenate([a["peer_u"][0], a["peer_v"][0]], 1),
        "g_ffn_row": a["norm_ffn_g"], "g_fin_row": a["norm_final_g"].reshape(1, 1024),
        "subln": a["subln_g"].reshape(128, 1),
        "cache_k": a["cache_k"][0].reshape(-1, 128, 1024), "cache_v": a["cache_v"][0].reshape(-1, 128, 1024),
        "pages": a["page_table"].reshape(1, 64),
    }
    i128 = np.arange(128)
    d["causal"] = np.where(i128[None, :] <= i128[:, None], 0, NEG).astype(np.float32)
    row = np.arange(64)
    tok = np.arange(32)
    d["causal_new"] = np.where((tok[None, None, :] // 4 == np.arange(8)[None, :, None])
                               & (tok[None, None, :] % 4 <= (row % 4)[:, None, None]), 0, NEG).astype(np.float32).reshape(64, 256)
    d["pick"] = ((row[:, None] // 8 == tok[None, :] // 4) & (row[:, None] % 4 == tok[None, :] % 4)).astype(np.float32)
    d["first"] = ((row % 8) < 4).astype(np.float32).reshape(64, 1)
    d["spread"] = np.tile(np.eye(32, dtype=np.float32), (4, 1))
    d["iota16"] = np.broadcast_to(np.arange(16, dtype=np.float32), (128, 16))
    return {k: f(v) for k, v in d.items()}


_OUTS = {
    "y": (1056, 1024), "k": (1056, 1024), "v": (1056, 1024), "s5_prompt": (128, 64), "s5_sample": (128, 512),
}


def kernel(**inputs):
    import concourse.bacc as bacc
    from concourse.bass_utils import run_bass_kernel_spmd

    arrays = _layouts({k: np.asarray(v) for k, v in inputs.items()})
    nc = bacc.Bacc("TRN2", target_bir_lowering=False, num_devices=1)
    dr = {n: nc.dram_tensor("in_" + n, a.shape, mybir.dt.from_np(a.dtype), kind="ExternalInput").ap()
          for n, a in arrays.items()}
    out = {n: nc.dram_tensor("out_" + n, s, F32, kind="ExternalOutput").ap() for n, s in _OUTS.items()}
    hybrid_step(nc, dr, out)
    r = run_bass_kernel_spmd(nc, [{"in_" + n: a for n, a in arrays.items()}], core_ids=[0]).results[0]
    y, k, v = r["out_y"], r["out_k"], r["out_v"]
    def by_group(x):
        return np.moveaxis(x.reshape((2, 64) + x.shape[1:]), 2, 0).reshape((64, 64) + x.shape[2:])
    sp = r["out_s5_prompt"].reshape(128, 2, 32)
    ss = r["out_s5_sample"].reshape(128, 2, 32, 8)
    hp = [by_group(sp[:, i]).reshape(1, 1, 64, 64) for i in range(2)]
    hsm = [by_group(ss[:, i]).transpose(2, 0, 1).reshape(1, 8, 64, 64) for i in range(2)]
    f = np.ascontiguousarray
    return (f(y[:1024].reshape(1, 1024, 1024)), f(y[1024:].reshape(8, 4, 1024)),
            f(k[:1024].reshape(1, 1, 1024, 8, 128)), f(v[:1024].reshape(1, 1, 1024, 8, 128)),
            f(hp[0]), f(hp[1]),
            f(k[1024:].reshape(1, 8, 4, 8, 128)), f(v[1024:].reshape(1, 8, 4, 8, 128)),
            f(hsm[0]), f(hsm[1]))
```

```python
from contextlib import ExitStack
import math

import numpy as np

import concourse.bass as bass
from concourse import mybir

F32 = mybir.dt.float32
U32 = mybir.dt.uint32
I32 = mybir.dt.int32
ALU = mybir.AluOpType
ACT = mybir.ActivationFunctionType
AX = mybir.AxisListType

P = 128
D = 1024
KC = D // P
SEQ = 1024
NSEQ, NNEW = 8, 4
NS = NSEQ * NNEW
T = SEQ + NS
TT = SEQ // P
NC3 = 3
CW = T // NC3
H = 8
HD = 64
G, PS5, CH = 64, 64, 16
GP = G // 2
ST8 = 8
NCH = SEQ // ST8
PAGES = 8
PH, PK, TOPK = 8, 128, 16
NE = PK * PK
EPS = 1e-6
LAM_INIT = 0.8 - 0.6 * math.exp(-0.3 * 0)
NEG = -1e30
LOWEST = -3e38
ARENA = 52900
ROUND = 1.5 * 2 ** 23
TWO_PI = (6.28125, 0.00193500518798828125, 2 * math.pi - 6.28125 - 0.00193500518798828125)
SIN_AT = 12

T_QK, T_GS, T_GLU, T_GA, T_QUERY = 0, 16, 32, 40, 56

START = 1
START_AT_ONE = ("hT_done", "acc_out", "yo_clear", "gl_used", "prod", "oT_free", "t_free", "ko_clear", "kt_ready", "on_acc",
                "on_free", "en_ready", "kt_free", "page_used", "ptn_free", "ptn_ready", "sn_ready", "sc_done",
                "s_acc", "tk_done", "idx_cp", "gelu_d", "diag_d", "yo_d", "dots", "init_d", "o4_clear")


def hybrid_step(nc, dr, out):
    root = ExitStack()
    with root:
        started = {n: root.enter_context(nc.semaphore(n)) for n in START_AT_ONE}

        def sem(name):
            return started[name] if name in started else root.enter_context(nc.semaphore(name))

        spare = sem("spare")

        def alone(eng):
            eng.sem_inc(spare, 1)

        def sbuf(stack, name, shape, dt=F32):
            return stack.enter_context(nc.sbuf_tensor(name, shape, dt))

        ps = root.enter_context(nc.psum_tensor("ps", [P, 8, 512], F32))

        ident = sbuf(root, "ident", [P, P])
        g_mix = sbuf(root, "g_mix", [P, KC])
        g_ffn = sbuf(root, "g_ffn", [P, KC])
        b_glu = sbuf(root, "b_glu", [P, KC])
        neg_lam = sbuf(root, "neg_lam", [P, 2])
        arena = sbuf(root, "arena", [P, ARENA])

        def lay(at, shape, dt=F32):
            n = int(np.prod(shape))
            assert at + n <= ARENA, (at, shape)
            flat = arena[:, at:at + n]
            if dt != F32:
                flat = flat.bitcast(dt)
            names = [f"d{i}" for i in range(len(shape))]
            if len(shape) == 1:
                return flat
            return flat.rearrange(f"p ({' '.join(names)}) -> p {' '.join(names)}",
                                  **{m: s for m, s in zip(names[1:], shape[1:])})

        w_in = [sem(f"w_in{k}") for k in range(2)]
        acc_ready = [sem(f"acc_ready{k}") for k in range(2)]
        acc_free = [sem(f"acc_free{k}") for k in range(2)]
        pairs = 0

        def stat_load(sp, wbuf, k, tile):
            sp.dma_start(wbuf[:, k, :], tile).then_inc(w_in[k], 16)

        def stat_loads(sp, wbuf, tile0, n, pairs):
            for k in range(2):
                stat_load(sp, wbuf, k, dr["w_stat"][tile0 + k])
            with sp.Fori(1, n) as i:
                for k in range(2):
                    sp.wait_ge(acc_ready[k], i * 3 + 3 * pairs)
                    stat_load(sp, wbuf, k, dr["w_stat"][bass.ds(i * 2 + (tile0 + k), 1)]
                              .rearrange("a p n -> (a p) n"))

        def stat_products(pe, i, k, wbuf, moving, pairs):
            pe.wait_ge(w_in[k], i * 16 + 16 * (pairs + 1))
            for c in range(NC3):
                pe.wait_ge(acc_free[k], i * 3 + (3 * pairs + c + 1))
                for kc in range(KC):
                    last = nc.tensor.matmul(ps[:, 3 * k + c, 0:CW], wbuf[:, k, kc * P:(kc + 1) * P],
                                            moving[:, kc, c * CW:(c + 1) * CW],
                                            start=(kc == 0), stop=(kc == KC - 1))
                last.then_inc(acc_ready[k], 1)

        AT_CL, AT_TOE, AT_UG, AT_HH, AT_UA, AT_HS, AT_H0, AT_WK, AT_PW, AT_HT = np.cumsum(
            [0, GP * 2 * 9 * CH, G * P, G * P, 2 * GP * (NCH + 1), G * NSEQ, 2 * GP * NSEQ, 2 * GP * NSEQ,
             G * P, 9 * 2 * GP]).tolist()
        hT = lay(AT_HT, [KC, T])
        xt = lay(AT_HH, [2, D])
        junk = lay(AT_HH + 2 * D, [D])
        lamv = lay(AT_HH + 3 * D, [4, HD])
        junk2 = lay(AT_HH + 4 * D, [2, HD])
        lam = lay(AT_HH + 5 * D, [4])
        ss = lay(AT_HH + 5 * D + 4, [2])
        const_in, lam_in = sem("const_in"), sem("lam_in")
        x_in = [sem(f"x_in{k}") for k in range(2)]
        sq_done, ms_done, rt_done, rc_done = sem("sq_done"), sem("ms_done"), sem("rt_done"), sem("rc_done")
        xn_done, xT_done, hT_done = sem("xn_done"), sem("xT_done"), sem("hT_done")
        lam_v, lam_a = sem("lam_v"), sem("lam_a")

        def norm_tile_act(act, x, ssq, rows, n):
            nc.scalar.activation(junk[0:rows, :], x, ACT.Square, accum_out=ssq).then_inc(sq_done, 1)
            act.wait_ge(ms_done, n + 1)
            nc.scalar.activation(ssq, ssq, ACT.Sqrt).then_inc(rt_done, 1)
            act.wait_ge(rc_done, n + 1)
            nc.scalar.activation(x, x, ACT.Copy, scale=ssq).then_inc(xn_done, 1)

        def norm_tile_dve(dve, ssq, n):
            dve.wait_ge(sq_done, n + 1)
            nc.vector.tensor_scalar(ssq, ssq, 1.0 / D, EPS, ALU.mult, ALU.add).then_inc(ms_done, 1)
            dve.wait_ge(rt_done, n + 1)
            nc.vector.reciprocal(ssq, ssq).then_inc(rc_done, 1)

        with nc.Block() as block:
            @block.sync
            def _(sp):
                for s in started.values():
                    sp.sem_inc(s, START)
                sp.dma_start(ident[:, :], dr["ident"]).then_inc(const_in, 16)
                sp.dma_start(g_mix[:, :], dr["g_mix"]).then_inc(const_in, 16)
                sp.dma_start(g_ffn[:, :], dr["g_ffn"]).then_inc(const_in, 16)
                sp.dma_start(b_glu[:, :], dr["b_glu"]).then_inc(const_in, 16)
                sp.dma_start(lamv[:, :, :].rearrange("p a b -> p (a b)"),
                             dr["lam"].broadcast_to([P, 4 * HD])).then_inc(lam_in, 16)
                for k in range(2):
                    sp.dma_start(xt[:, k, :], dr["x"][k * P:(k + 1) * P, :]).then_inc(x_in[k], 16)
                with sp.Fori(1, TT // 2) as i:
                    for k in range(2):
                        sp.wait_ge(xT_done, i * 2 + (k - 1))
                        sp.dma_start(xt[:, k, :], dr["x"][bass.ds(i * 2 * P + k * P, P), :]).then_inc(x_in[k], 16)
                sp.wait_ge(xT_done, TT - 1)
                sp.dma_start(xt[0:NS, 0, :], dr["x"][SEQ:T, :]).then_inc(x_in[0], 16)

            @block.scalar
            def _(act):
                for k in range(2):
                    act.sem_inc(acc_free[k], 3)
                with act.Fori(0, TT // 2) as i:
                    for k in range(2):
                        act.wait_ge(x_in[k], (i + 1) * 16)
                        norm_tile_act(act, xt[:, k, :], ss[:, k:k + 1], P, i * 2 + k)
                act.wait_ge(x_in[0], 16 * (TT // 2 + 1))
                norm_tile_act(act, xt[0:NS, 0, :], ss[0:NS, 0:1], NS, TT)
                act.wait_ge(lam_v, 1)
                nc.scalar.activation(lam[:, 2:4], lam[:, 0:2], ACT.Exp).then_inc(lam_a, 1)

            @block.tensor
            def _(pe):
                pe.wait_ge(const_in, 64)

                def transposes(k, rows, n):
                    pe.wait_ge(xn_done, n + 1)
                    if k is not None:
                        pe.wait_ge(hT_done, START + n)
                    for c in range(KC):
                        last = nc.tensor.transpose(ps[:, c // 4, (c % 4) * P:(c % 4) * P + rows],
                                                   xt[0:rows, k, c * P:(c + 1) * P], ident[0:rows, 0:rows])
                    last.then_inc(xT_done, 1)

                with pe.Fori(0, TT // 2) as i:
                    for k in range(2):
                        transposes(k, P, i * 2 + k)
                transposes(0, NS, TT)

            @block.vector
            def _(dve):
                def take_out(rows, col, n):
                    dve.wait_ge(xT_done, n + 1)
                    for b in range(2):
                        last = nc.vector.tensor_tensor(
                            hT[:, 4 * b:4 * b + 4, bass.ds(col, rows)],
                            ps[:, b, :].rearrange("p (c t) -> p c t", c=4)[:, :, 0:rows],
                            g_mix[:, 4 * b:4 * b + 4].unsqueeze(2).broadcast_to([P, 4, rows]), ALU.mult)
                    last.then_inc(hT_done, 1)

                dve.wait_ge(const_in, 64)
                with dve.Fori(0, TT // 2) as i:
                    for k in range(2):
                        norm_tile_dve(dve, ss[:, k:k + 1], i * 2 + k)
                        take_out(P, i * 2 * P + k * P, i * 2 + k)
                norm_tile_dve(dve, ss[0:NS, 0:1], TT)
                take_out(NS, SEQ, TT)
                dve.wait_ge(lam_in, 16)
                for b in range(2):
                    last = nc.vector.tensor_tensor_reduce(junk2[:, b, :], lamv[:, 2 * b, :], lamv[:, 2 * b + 1, :], 1.0, 0.0,
                                                          ALU.mult, ALU.add, lam[:, b:b + 1])
                last.then_inc(lam_v, 1)
                dve.wait_ge(lam_a, 1)
                nc.vector.tensor_tensor(neg_lam[:, 0:1], lam[:, 3:4], lam[:, 2:3], ALU.subtract).then_inc(lam_v, 1)
                dve.wait_ge(lam_v, 2)
                nc.vector.tensor_scalar(neg_lam[:, 1:2], neg_lam[:, 0:1], -LAM_INIT, None, ALU.add).then_inc(lam_v, 1)
                dve.wait_ge(lam_v, 3)
                nc.vector.memset(neg_lam[:, 0:1], 1.0)

        cl = lay(AT_CL, [GP, 2, 9, CH])
        m_toe = lay(AT_TOE, [G, P])
        ug = lay(AT_UG, [G, P])
        hh = lay(AT_HH, [2, GP, NCH + 1])
        ua = lay(AT_UA, [G, NSEQ])
        hs = lay(AT_HS, [2, GP, NSEQ])
        h0 = lay(AT_H0, [2, GP, NSEQ])
        wk = lay(AT_HT, [GP, 2, ST8, CH])
        kst = lay(AT_WK, [G, ST8, CH])
        z_tok = lay(AT_WK, [ST8, D])
        pw = lay(AT_PW, [9, 2, GP])
        u_tok = lay(AT_TOE, [G, ST8, CH])
        slab = lay(AT_WK, [2, KC, 512])
        us_tok = lay(AT_HH, [G, NNEW, CH])
        bri = lay(AT_HH + 4096, [2, GP, CH])
        cri = lay(AT_HH + 5120, [2, GP, CH])
        bb = lay(AT_HH + 6144, [2, GP, CH])
        tmp = lay(AT_HH + 7168, [GP, CH])
        sm = lay(AT_HH + 7680, [18, GP])
        d_s5 = lay(AT_HH + 7680 + 15 * GP, [G])
        SUP = 8
        NSUP = NCH // SUP
        pl = lay(AT_HT + G * P, [2, GP, SUP])
        scr_h = nc.dram_tensor("scr_h", (P, KC * T), F32, kind="Internal").ap()

        par_in, slab_in = sem("par_in"), [sem(f"slab_in{k}") for k in range(2)]
        u_ready, u_free = sem("u_ready"), sem("u_free")
        ug_ready, ug_free = sem("ug_ready"), sem("ug_free")
        par_a, par_v, spill = sem("par_a"), sem("par_v"), sem("spill")
        NU = 2 * ST8 + 2 * NNEW

        def complex_step(dve, mul, re, im, ar, ai, br, bi, sign, t):
            mul(re, ar, br, ALU.mult)
            mul(t, ai, bi, ALU.mult)
            mul(re, re, t, ALU.subtract)
            mul(im, ar, bi, ALU.mult)
            mul(t, ai, br, ALU.mult)
            if sign > 0:
                mul(im, im, t, ALU.add)
            else:
                par["n"] += 1
                nc.vector.scalar_tensor_tensor(im, im, -1.0, t, ALU.mult, ALU.subtract).then_inc(par_v, 1)
                dve.wait_ge(par_v, par["n"])

        par = {"n": 0}
        with nc.Block() as block:
            @block.sync
            def _(sp):
                for k in range(2):
                    sp.dma_start(slab[:, k, :, :].rearrange("p a b -> p (a b)"), dr["w_mov"][k]).then_inc(slab_in[k], 16)
                for dst, name in ((sm[:, 0, :], "a_re"), (sm[:, 1, :], "a_im"), (sm[:, 2, :], "log_step"),
                                  (bri.rearrange("p r g c -> p (r g c)"), "b_ri"), (cri.rearrange("p r g c -> p (r g c)"), "c_ri"),
                                  (h0.rearrange("p r g q -> p (r g q)"), "h0"), (d_s5[0:CH, :], "d_s5")):
                    sp.dma_start(dst, dr[name]).then_inc(par_in, 16)
                sp.wait_ge(u_ready, NU)
                sp.dma_start(scr_h, hT.rearrange("p c t -> p (c t)")).then_inc(spill, 16)
                sp.wait_ge(spill, 16)

            @block.tensor
            def _(pe):
                n = 0
                for k in range(2):
                    pe.wait_ge(slab_in[k], 16)
                    for s in range(ST8 + NNEW):
                        if n >= 4:
                            pe.wait_ge(u_free, n - 3)
                        rows = P if s < ST8 else NSEQ
                        for kc in range(KC):
                            tok = hT[:, kc, s:SEQ:ST8] if s < ST8 else hT[:, kc, SEQ + s - ST8:T:NNEW]
                            last = nc.tensor.matmul(ps[0:rows, n % 4, :], tok, slab[:, k, kc, :],
                                                    start=(kc == 0), stop=(kc == KC - 1))
                        last.then_inc(u_ready, 1)
                        n += 1
                pe.wait_ge(u_free, NU)
                for q in range(G // 4):
                    if q >= 3:
                        pe.wait_ge(ug_free, q - 2)
                    for j in range(4):
                        g = 4 * q + j
                        last = nc.tensor.transpose(ps[:, 4 + q % 3, j * P:(j + 1) * P],
                                                   u_tok[:, g], ident[:, :])
                    last.then_inc(ug_ready, 1)
                for g in range(G):
                    last = nc.tensor.transpose(ps[0:64, 7, g * NSEQ:(g + 1) * NSEQ],
                                               us_tok[0:NSEQ, g], ident[0:NSEQ, 0:NSEQ])
                last.then_inc(ug_ready, 1)

            @block.scalar
            def _(act):
                dt_, mag, ang, r2 = sm[:, 3, :], sm[:, 4, :], sm[:, 5, :], sm[:, 6:8, :]
                act.wait_ge(par_in, 112)
                nc.scalar.activation(dt_, sm[:, 2, :], ACT.Exp).then_inc(par_a, 1)
                act.wait_ge(par_v, 1)
                nc.scalar.activation(mag, mag, ACT.Exp).then_inc(par_a, 1)
                act.wait_ge(par_v, SIN_AT)
                nc.scalar.activation(r2, r2, ACT.Sin).then_inc(par_a, 1)
                n = 0
                for k in range(2):
                    for s in range(ST8 + NNEW):
                        act.wait_ge(u_ready, n + 1)
                        gs_ = slice(G // 2 * k, G // 2 * (k + 1))
                        rows = P if s < ST8 else NSEQ
                        dst = u_tok[:, gs_, s, :] if s < ST8 else us_tok[0:NSEQ, gs_, s - ST8, :]
                        nc.scalar.activation(dst, ps[0:rows, n % 4, :].rearrange("p (g c) -> p g c", c=CH), ACT.Copy).then_inc(u_free, 1)
                        n += 1
                for q in range(G // 4):
                    act.wait_ge(ug_ready, q + 1)
                    nc.scalar.activation(ug[:, 4 * q:4 * q + 4, :].rearrange("p g t -> p (g t)"), ps[:, 4 + q % 3, :],
                                         ACT.Copy).then_inc(ug_free, 1)
                act.wait_ge(ug_ready, G // 4 + 1)
                nc.scalar.activation(ua[0:64].rearrange("p g q -> p (g q)"), ps[0:64, 7, :], ACT.Copy).then_inc(ug_free, 1)

            @block.vector
            def _(dve):
                def op(ins):
                    par["n"] += 1
                    ins.then_inc(par_v, 1)
                    dve.wait_ge(par_v, par["n"])

                def mul(o, a, b, how):
                    op(nc.vector.tensor_tensor(o, a, b, how))

                a_re, a_im, dt_, mag, ang, r2, q2 = (sm[:, 0, :], sm[:, 1, :], sm[:, 3, :], sm[:, 4, :], sm[:, 5, :],
                                                     sm[:, 6:8, :], sm[:, 8:10, :])
                t0, t1, f_re, f_im, den = (sm[:, j, :] for j in range(10, 15))
                dve.wait_ge(par_a, 1)
                mul(mag, a_re, dt_, ALU.mult)
                mul(ang, a_im, dt_, ALU.mult)
                for j in range(2):
                    op(nc.vector.tensor_scalar(q2[:, j, :], ang, 1 / (2 * math.pi), 0.25 * j, ALU.mult, ALU.add))
                op(nc.vector.tensor_scalar(q2, q2, ROUND, None, ALU.add))
                op(nc.vector.tensor_scalar(q2, q2, -ROUND, None, ALU.add))
                for j in range(2):
                    op(nc.vector.scalar_tensor_tensor(r2[:, j, :], q2[:, j, :], -TWO_PI[0], ang, ALU.mult, ALU.add))
                for part in TWO_PI[1:]:
                    op(nc.vector.scalar_tensor_tensor(r2, q2, -part, r2, ALU.mult, ALU.add))
                op(nc.vector.tensor_scalar(r2[:, 1, :], r2[:, 1, :], math.pi / 2, None, ALU.add))
                op(nc.vector.tensor_scalar(r2, r2, 3.1415925, -3.1415925, ALU.min, ALU.max))
                assert par["n"] == SIN_AT, par
                dve.wait_ge(par_a, 3)
                op(nc.vector.memset(pw[:, 0, 0, :], 1.0))
                op(nc.vector.memset(pw[:, 0, 1, :], 0.0))
                mul(pw[:, 1, 0, :], mag, r2[:, 1, :], ALU.mult)
                mul(pw[:, 1, 1, :], mag, r2[:, 0, :], ALU.mult)
                for j in range(2, 9):
                    complex_step(dve, mul, pw[:, j, 0, :], pw[:, j, 1, :], pw[:, j - 1, 0, :], pw[:, j - 1, 1, :],
                                 pw[:, 1, 0, :], pw[:, 1, 1, :], 1, t0)
                op(nc.vector.tensor_scalar(t1, pw[:, 1, 0, :], -1.0, None, ALU.add))
                mul(den, a_re, a_re, ALU.mult)
                mul(t0, a_im, a_im, ALU.mult)
                mul(den, den, t0, ALU.add)
                op(nc.vector.reciprocal(den, den))
                mul(f_re, t1, a_re, ALU.mult)
                mul(t0, pw[:, 1, 1, :], a_im, ALU.mult)
                mul(f_re, f_re, t0, ALU.add)
                mul(f_im, pw[:, 1, 1, :], a_re, ALU.mult)
                mul(t0, t1, a_im, ALU.mult)
                mul(f_im, f_im, t0, ALU.subtract)
                mul(f_re, f_re, den, ALU.mult)
                mul(f_im, f_im, den, ALU.mult)
                wide = lambda a: a.unsqueeze(2).broadcast_to([P, GP, CH])
                complex_step(dve, mul, bb[:, 0], bb[:, 1], bri[:, 0], bri[:, 1], wide(f_re), wide(f_im), 1, tmp)
                for j in range(9):
                    complex_step(dve, mul, cl[:, :, 0, j, :], cl[:, :, 1, j, :], cri[:, 0], cri[:, 1],
                                 wide(pw[:, j, 0, :]), wide(pw[:, j, 1, :]), -1, tmp)

        k_ready, k_free, k_d = sem("k_ready"), sem("k_free"), sem("k_d")
        toe_zero, toe_in, w_v = sem("toe_zero"), sem("toe_in"), sem("w_v")
        with nc.Block() as block:
            @block.gpsimd
            def _(pool):
                nc.gpsimd.memset(m_toe, 0.0).then_inc(toe_zero, 1)
                pool.wait_ge(toe_zero, 1)
                nc.gpsimd.memset(ua[64:P], 0.0).then_inc(toe_zero, 1)

            @block.tensor
            def _(pe):
                for q in range(G // 8):
                    if q >= 2:
                        pe.wait_ge(k_free, 2 * (q - 1))
                    for j in range(8):
                        gp, par_ = 4 * q + j // 2, j % 2
                        half = slice(64 * par_, 64 * par_ + 64)
                        for ri in range(2):
                            last = nc.tensor.matmul(ps[0:CH, 2 * (q % 2) + par_, j // 2 * P:(j // 2 + 1) * P],
                                                    bb[half, ri, gp, :], cl[half, gp, ri, 0:ST8, :],
                                                    start=(ri == 0), stop=(ri == 1))
                        if j >= 6:
                            last.then_inc(k_ready, 1)

            @block.scalar
            def _(act):
                for q in range(G // 8):
                    for par_ in range(2):
                        act.wait_ge(k_ready, 2 * q + 2)
                        nc.scalar.activation(kst[0:CH, 8 * q + par_:8 * q + 8:2].rearrange("p g t c -> p g (t c)"),
                                             ps[0:CH, 2 * (q % 2) + par_, :].rearrange("p (g m) -> p g m", g=4),
                                             ACT.Copy).then_inc(k_free, 1)

            @block.vector
            def _(dve):
                def mul(o, a, b, how):
                    n[0] += 1
                    nc.vector.tensor_tensor(o, a, b, how).then_inc(w_v, 1)
                    dve.wait_ge(w_v, n[0])

                n = [0]
                wide = lambda a: a.unsqueeze(2).broadcast_to([P, GP, CH])
                for s in range(ST8):
                    complex_step(dve, mul, wk[:, :, 0, s, :], wk[:, :, 1, s, :], bb[:, 0], bb[:, 1],
                                 wide(pw[:, 7 - s, 0, :]), wide(pw[:, 7 - s, 1, :]), 1, tmp)
                    if s == ST8 // 2:
                        dd = lay(AT_HH, [G, CH])[0:CH]
                        nc.vector.tensor_tensor(dd, ident[0:CH, 0:CH].unsqueeze(1).broadcast_to([CH, G, CH]),
                                                d_s5[0:CH].unsqueeze(2).broadcast_to([CH, G, CH]), ALU.mult).then_inc(k_d, 1)
                        dve.wait_ge(k_d, 1)
                        dve.wait_ge(k_free, G // 4)
                        nc.vector.tensor_tensor(kst[0:CH, :, 0, :], kst[0:CH, :, 0, :], dd, ALU.add).then_inc(k_d, 1)
                for r in range(2):
                    last = nc.vector.tensor_copy(pl[:, r, :, 0], pw[:, 8, r, :])
                n[0] += 1
                last.then_inc(w_v, 1)
                dve.wait_ge(w_v, n[0])
                for m in range(1, SUP):
                    complex_step(dve, mul, pl[:, 0, :, m], pl[:, 1, :, m], pl[:, 0, :, m - 1], pl[:, 1, :, m - 1],
                                 pw[:, 8, 0, :], pw[:, 8, 1, :], 1, tmp[:, :, 0])
                nc.vector.memset(neg_lam[:, 0:1], 1.0).then_inc(w_v, 1)

            @block.sync
            def _(sp):
                sp.wait_ge(k_d, 2)
                sp.wait_ge(toe_zero, 1)
                for s in range(ST8):
                    sp.dma_start(m_toe[s * CH:(s + 1) * CH, :, s * CH:P],
                                 kst[0:CH, :, 0:ST8 - s, :].rearrange("p g t c -> p g (t c)")).then_inc(toe_in, 16)
                sp.wait_ge(toe_in, 16 * ST8)

        st = lay(AT_WK, [2, 2, P])
        st4 = lay(AT_WK + 512, [2, 2, P])
        BG = GP // 4
        sa, sb = lay(AT_WK + 1024, [2, BG, NSUP]), lay(AT_WK + 1024 + 2 * BG * NSUP, [2, BG, NSUP])
        wT_ready, wT_free, se_ready, se_free = (sem(n) for n in ("wT_ready", "wT_free", "se_ready", "se_free"))
        st_out, rec = sem("st_out"), sem("rec")
        hsup = hh[:, :, :, 1:NCH + 1].rearrange("p r g (s j) -> p r g s j", j=SUP)
        N_LOCAL = 4 * 4 * (SUP - 1)
        with nc.Block() as block:
            @block.tensor
            def _(pe):
                def transposes(gp):
                    if gp >= 2:
                        pe.wait_ge(wT_free, gp - 1)
                    for ri in range(2):
                        nc.tensor.transpose(ps[:, gp % 2, ri * P:(ri + 1) * P], wk[:, gp, ri], ident[:, :])
                    for ri in range(2):
                        last = nc.tensor.transpose(ps[0:64, gp % 2, (2 + ri) * P:(3 + ri) * P],
                                                   wk[:, gp, ri, NNEW:ST8, :], ident[:, :])
                    last.then_inc(wT_ready, 1)

                transposes(0)
                for gp in range(GP):
                    if gp + 1 < GP:
                        transposes(gp + 1)
                    pe.wait_ge(wT_free, gp + 1)
                    if gp >= 2:
                        pe.wait_ge(se_free, gp - 1)
                    for par_ in range(2):
                        half = slice(64 * par_, 64 * par_ + 64)
                        for ri in range(2):
                            nc.tensor.matmul(ps[half, 2 + gp % 2, ri * P:(ri + 1) * P], st[:, gp % 2, ri, half],
                                             ug[:, 2 * gp + par_, :], start=True, stop=True)
                            last = nc.tensor.matmul(ps[half, 2 + gp % 2, 256 + ri * NSEQ:256 + (ri + 1) * NSEQ],
                                                    st4[0:64, gp % 2, ri, half], ua[0:64, 2 * gp + par_, :],
                                                    start=True, stop=True)
                    last.then_inc(se_ready, 1)

            @block.scalar
            def _(act):
                def states_in(act, gp):
                    act.wait_ge(se_ready, gp + 1)
                    nc.scalar.activation(hs[:, :, gp, :], ps[:, 2 + gp % 2, 256:256 + 2 * NSEQ]
                                         .rearrange("p (r q) -> p r q", r=2), ACT.Copy)
                    nc.scalar.activation(hh[:, :, gp, 1:NCH + 1], ps[:, 2 + gp % 2, 0:256]
                                         .rearrange("p (r n) -> p r n", r=2), ACT.Copy).then_inc(se_free, 1)

                for gp in range(GP):
                    act.wait_ge(wT_ready, gp + 1)
                    if gp >= 2:
                        act.wait_ge(se_ready, gp - 1)
                    nc.scalar.activation(st[:, gp % 2].rearrange("p r m -> p (r m)"), ps[:, gp % 2, 0:256], ACT.Copy)
                    nc.scalar.activation(st4[0:64, gp % 2].rearrange("p r m -> p (r m)"), ps[0:64, gp % 2, 256:512],
                                         ACT.Copy).then_inc(wT_free, 1)
                    if gp:
                        states_in(act, gp - 1)
                states_in(act, GP - 1)

            @block.vector
            def _(dve):
                nc.vector.memset(hh[:, :, :, 0:1], 0.0).then_inc(w_v, 1)
                n = 0
                for b in range(GP // BG):
                    gs = slice(b * BG, (b + 1) * BG)
                    l_re = pw[:, 8, 0, gs].unsqueeze(2).broadcast_to([P, BG, NSUP])
                    l_im = pw[:, 8, 1, gs].unsqueeze(2).broadcast_to([P, BG, NSUP])
                    dve.wait_ge(se_free, (b + 1) * BG)
                    for j in range(1, SUP):
                        now, nxt = hsup[:, :, gs, :, j - 1], hsup[:, :, gs, :, j]
                        if n:
                            dve.wait_ge(rec, n)
                        for r in range(2):
                            nc.vector.tensor_tensor(sa[:, r], now[:, r], l_re, ALU.mult)
                            last = nc.vector.tensor_tensor(sb[:, r], now[:, 1 - r], l_im, ALU.mult)
                        last.then_inc(rec, 1)
                        dve.wait_ge(rec, n + 1)
                        nc.vector.tensor_tensor(nxt, nxt, sa, ALU.add).then_inc(rec, 1)
                        dve.wait_ge(rec, n + 2)
                        nc.vector.tensor_tensor(nxt[:, 0], nxt[:, 0], sb[:, 0], ALU.subtract).then_inc(rec, 1)
                        nc.vector.tensor_tensor(nxt[:, 1], nxt[:, 1], sb[:, 1], ALU.add).then_inc(rec, 1)
                        n += 4
                assert n == N_LOCAL

        ta, tb = lay(AT_HT, [2, GP]), lay(AT_HT + 64, [2, GP])
        t8 = lay(AT_HT + 128, [GP, NSEQ])
        N_CARRIED = N_LOCAL + 4 * (NSUP - 1) + 8
        with nc.Block() as block:
            @block.vector
            def _(dve):
                l_re = pl[:, 0, :, SUP - 1].unsqueeze(1).broadcast_to([P, 2, GP])
                l_im = pl[:, 1, :, SUP - 1]
                m = N_LOCAL
                for s in range(1, NSUP):
                    now, nxt = hsup[:, :, :, s - 1, SUP - 1], hsup[:, :, :, s, SUP - 1]
                    dve.wait_ge(rec, m)
                    nc.vector.tensor_tensor(ta, now, l_re, ALU.mult)
                    nc.vector.tensor_tensor(tb[:, 0, :], now[:, 1, :], l_im, ALU.mult)
                    nc.vector.tensor_tensor(tb[:, 1, :], now[:, 0, :], l_im, ALU.mult).then_inc(rec, 1)
                    dve.wait_ge(rec, m + 1)
                    nc.vector.tensor_tensor(nxt, nxt, ta, ALU.add).then_inc(rec, 1)
                    dve.wait_ge(rec, m + 2)
                    nc.vector.tensor_tensor(nxt[:, 0, :], nxt[:, 0, :], tb[:, 0, :], ALU.subtract).then_inc(rec, 1)
                    nc.vector.tensor_tensor(nxt[:, 1, :], nxt[:, 1, :], tb[:, 1, :], ALU.add).then_inc(rec, 1)
                    m += 4
                wide = lambda a: a.unsqueeze(2).broadcast_to([P, GP, NSEQ])
                for dst, src, lam_, how in ((0, 0, 0, ALU.add), (0, 1, 1, ALU.subtract), (1, 0, 1, ALU.add), (1, 1, 0, ALU.add)):
                    dve.wait_ge(rec, m)
                    nc.vector.tensor_tensor(t8, h0[:, src], wide(pw[:, NNEW, lam_, :]), ALU.mult).then_inc(rec, 1)
                    dve.wait_ge(rec, m + 1)
                    nc.vector.tensor_tensor(hs[:, dst], hs[:, dst], t8, how).then_inc(rec, 1)
                    m += 2

            @block.sync
            def _(sp):
                sp.wait_ge(rec, N_CARRIED)
                sp.dma_start(out["s5_prompt"], hh[:, :, :, NCH:NCH + 1], allow_slow_non_contiguous=True).then_inc(st_out, 16)
                sp.dma_start(out["s5_sample"], hs.rearrange("p r g q -> p (r g q)")).then_inc(st_out, 16)
                sp.wait_ge(st_out, 32)

        zs_tok = lay(AT_HT, [NNEW, D])
        y_ready, y_free = sem("y_ready"), sem("y_free")
        late = [lay(AT_HT + NNEW * D + j * BG * NSUP * SUP, [BG, NSUP - 1, SUP - 1]) for j in range(4)]
        NYS = 2 * (G // 16)
        with nc.Block() as block:
            @block.tensor
            def _(pe):
                for q in range(G // 16):
                    if q >= 2:
                        pe.wait_ge(y_free, 2 * (q - 1))
                    for j in range(16):
                        g, par_ = 16 * q + j, j % 2
                        half = slice(64 * par_, 64 * par_ + 64)
                        o = ps[0:NSEQ, 4 + 2 * (q % 2) + par_, j // 2 * 64:(j // 2 + 1) * 64]
                        nc.tensor.matmul(o, ua[:, g, :], m_toe[:, g, 0:64], start=True, stop=False)
                        for ri in range(2):
                            last = nc.tensor.matmul(o, h0[half, ri, g // 2, :], cl[half, g // 2, ri, 1:1 + NNEW, :],
                                                    start=False, stop=(ri == 1))
                        if j >= 14:
                            last.then_inc(y_ready, 1)
                for q in range(G // 8):
                    if q >= 2:
                        pe.wait_ge(y_free, NYS + 2 * (q - 1))
                    pe.wait_ge(rec, N_CARRIED + 4 * (4 * q // BG + 1))
                    for j in range(8):
                        g, par_ = 8 * q + j, j % 2
                        half = slice(64 * par_, 64 * par_ + 64)
                        o = ps[:, 2 * (q % 2) + par_, j // 2 * P:(j // 2 + 1) * P]
                        nc.tensor.matmul(o, ug[:, g, :], m_toe[:, g, :], start=True, stop=False)
                        for ri in range(2):
                            last = nc.tensor.matmul(o, hh[half, ri, g // 2, 0:NCH], cl[half, g // 2, ri, 1:9, :],
                                                    start=False, stop=(ri == 1))
                        if j >= 6:
                            last.then_inc(y_ready, 1)

            @block.scalar
            def _(act):
                z_g = z_tok.rearrange("p t (g c) -> p t g c", c=CH)
                zs_g = zs_tok.rearrange("p t (g c) -> p t g c", c=CH)
                for q in range(G // 16):
                    for par_ in range(2):
                        act.wait_ge(y_ready, 2 * q + 2)
                        for t in range(NNEW):
                            last = nc.scalar.activation(
                                zs_g[0:NSEQ, t, 16 * q + par_:16 * q + 16:2],
                                ps[0:NSEQ, 4 + 2 * (q % 2) + par_, :].rearrange("p (g t c) -> p t g c", g=8, t=NNEW)[:, t],
                                ACT.Gelu)
                        last.then_inc(y_free, 1)
                for q in range(G // 8):
                    for par_ in range(2):
                        act.wait_ge(y_ready, NYS + 2 * q + 2)
                        for t in range(ST8):
                            last = nc.scalar.activation(
                                z_g[:, t, 8 * q + par_:8 * q + 8:2],
                                ps[:, 2 * (q % 2) + par_, :].rearrange("p (g t c) -> p t g c", g=4, t=ST8)[:, t], ACT.Gelu)
                        last.then_inc(y_free, 1)

            @block.vector
            def _(dve):
                n = N_CARRIED
                for b in range(GP // BG):
                    gs = slice(b * BG, (b + 1) * BG)
                    shape = [P, BG, NSUP - 1, SUP - 1]
                    l_ = [pl[:, r, gs, 0:SUP - 1].unsqueeze(2).broadcast_to(shape) for r in range(2)]
                    h_ = [hsup[:, r, gs, 0:NSUP - 1, SUP - 1].unsqueeze(3).broadcast_to(shape) for r in range(2)]
                    to = [hsup[:, r, gs, 1:NSUP, 0:SUP - 1] for r in range(2)]
                    dve.wait_ge(rec, n)
                    for k, (r, q) in enumerate(((0, 0), (1, 0), (1, 1), (0, 1))):
                        last = nc.vector.tensor_tensor(late[k], h_[r], l_[q], ALU.mult)
                    last.then_inc(rec, 1)
                    dve.wait_ge(rec, n + 1)
                    nc.vector.tensor_tensor(to[0], to[0], late[0], ALU.add)
                    nc.vector.tensor_tensor(to[1], to[1], late[1], ALU.add).then_inc(rec, 1)
                    dve.wait_ge(rec, n + 2)
                    nc.vector.tensor_tensor(to[0], to[0], late[2], ALU.subtract).then_inc(rec, 1)
                    nc.vector.tensor_tensor(to[1], to[1], late[3], ALU.add).then_inc(rec, 1)
                    n += 4

        AT_ZT, AT_S5O, AT_MT, AT_WB = 0, AT_TOE, AT_TOE + KC * T, AT_WK
        zT = lay(AT_ZT, [KC, T])
        z_ready, z_free = sem("z_ready"), sem("z_free")
        with nc.Block() as block:
            @block.tensor
            def _(pe):
                for n in range(2 * KC):
                    c, b = n // 2, n % 2
                    if n >= 4:
                        pe.wait_ge(z_free, n - 3)
                    for s in range(4):
                        last = nc.tensor.transpose(ps[:, n % 4, s * P:(s + 1) * P],
                                                   z_tok[:, 4 * b + s, c * P:(c + 1) * P], ident[:, :])
                    last.then_inc(z_ready, 1)
                for c in range(KC):
                    for t in range(NNEW):
                        last = nc.tensor.transpose(ps[:, 4, c * NS + t * NSEQ:c * NS + (t + 1) * NSEQ],
                                                   zs_tok[0:NSEQ, t, c * P:(c + 1) * P], ident[0:NSEQ, 0:NSEQ])
                last.then_inc(z_ready, 1)

            @block.vector
            def _(dve):
                for n in range(2 * KC):
                    c, b = n // 2, n % 2
                    dve.wait_ge(z_ready, n + 1)
                    nc.vector.tensor_copy(zT[:, c, 0:SEQ].rearrange("p (n s) -> p s n", s=ST8)[:, 4 * b:4 * b + 4],
                                          ps[:, n % 4, :].rearrange("p (s n) -> p s n", s=4)).then_inc(z_free, 1)
                dve.wait_ge(z_ready, 2 * KC + 1)
                for c in range(KC):
                    last = nc.vector.tensor_copy(zT[:, c, SEQ:T].rearrange("p (q t) -> p t q", t=NNEW),
                                                 ps[:, 4, c * NS:(c + 1) * NS].rearrange("p (t q) -> p t q", t=NNEW))
                last.then_inc(z_free, 1)

        wbuf = lay(AT_WB, [2, D])
        gate = lay(AT_WB + 2 * D, [2, NC3, CW])
        mul_t = lay(AT_WB + 2 * D + 2 * NC3 * CW, [CW])
        s5oT = lay(AT_S5O, [KC, T])
        mT = lay(AT_MT, [KC, T])
        gl_ready, gl_used, hT_back = sem("gl_ready"), sem("gl_used"), sem("hT_back")
        chunk = lambda c: slice(c * CW, (c + 1) * CW)

        def one(a):
            return a.rearrange("p a n -> p (a n)")

        NGLU = KC // 2
        with nc.Block() as block:
            @block.sync
            def _(sp):
                sp.dma_start(hT.rearrange("p c t -> p (c t)"), scr_h).then_inc(hT_back, 16)
                stat_loads(sp, wbuf, T_GLU, NGLU, pairs)
                sp.wait_ge(hT_back, 16)

            @block.tensor
            def _(pe):
                with pe.Fori(0, NGLU) as i:
                    for k in range(2):
                        stat_products(pe, i, k, wbuf, zT, pairs)

            @block.scalar
            def _(act):
                with act.Fori(0, NGLU) as i:
                    for k in range(2):
                        for c in range(NC3):
                            act.wait_ge(acc_ready[k], i * 3 + (3 * pairs + c + 1))
                            act.wait_ge(gl_used, START + i * 6)
                            alone(act)
                            nc.scalar.activation(gate[:, k, c, :], ps[:, 3 * k + c, 0:CW], ACT.Sigmoid,
                                                 bias=b_glu[:, bass.ds(i * 2 + k, 1)]).then_inc(acc_free[k], 1)

            @block.vector
            def _(dve):
                with dve.Fori(0, NGLU) as i:
                    for k in range(2):
                        for c in range(NC3):
                            dve.wait_ge(acc_free[k], i * 3 + (3 * pairs + c + 4))
                            m = bass.ds(i * 2 + k, 1)
                            nc.vector.tensor_tensor(one(s5oT[:, m, chunk(c)]), one(zT[:, m, chunk(c)]), gate[:, k, c, :],
                                                    ALU.mult).then_inc(gl_used, 1)
        pairs += NGLU

        prod = sem("prod")

        def merge(block, tile0, other, fold, pairs):
            @block.sync
            def _(sp):
                stat_loads(sp, wbuf, tile0, KC, pairs)

            @block.tensor
            def _(pe):
                with pe.Fori(0, KC) as i:
                    stat_products(pe, i, 0, wbuf, hT, pairs)
                    stat_products(pe, i, 1, wbuf, other, pairs)

            @block.scalar
            def _(act):
                with act.Fori(0, KC) as i:
                    for c in range(NC3):
                        act.wait_ge(acc_ready[0], i * 3 + (3 * pairs + c + 1))
                        act.wait_ge(acc_free[1], i * 3 + (3 * pairs + 3))
                        nc.scalar.activation(gate[:, 0, c, :], ps[:, c, 0:CW], ACT.Sigmoid).then_inc(acc_free[0], 1)

            @block.vector
            def _(dve):
                with dve.Fori(0, KC) as i:
                    for c in range(NC3):
                        dve.wait_ge(acc_free[0], i * 3 + (3 * pairs + c + 4))
                        dve.wait_ge(acc_ready[1], i * 3 + (3 * pairs + c + 1))
                        dst = one(mT[:, bass.ds(i, 1), chunk(c)])
                        if not fold:
                            nc.vector.tensor_tensor(dst, ps[:, 3 + c, 0:CW], gate[:, 0, c, :], ALU.mult).then_inc(acc_free[1], 1)
                            continue
                        dve.wait_ge(prod, START + i * 3 + c)
                        nc.vector.tensor_tensor(mul_t, ps[:, 3 + c, 0:CW], gate[:, 0, c, :], ALU.mult).then_inc(acc_free[1], 1)
                        dve.wait_ge(acc_free[1], i * 3 + (3 * pairs + c + 4))
                        nc.vector.tensor_tensor(dst, dst, mul_t, ALU.add).then_inc(prod, 1)

        with nc.Block() as block:
            merge(block, T_GS, s5oT, False, pairs)
        pairs += KC

        attT = lay(0, [KC, T])
        AT_MISC, AT_V = KC * T, AT_MT + KC * T
        vall = lay(AT_V, [TT + 1, D])
        v_slab = lay(AT_WB, [2, KC, 512])
        v_ready, v_free, v_out = sem("v_ready"), sem("v_free"), sem("v_out")

        def token_rows(t):
            return (P if t < TT else NS), slice(t * P, t * P + (P if t < TT else NS))

        with nc.Block() as block:
            @block.sync
            def _(sp):
                for k in range(2):
                    sp.dma_start(v_slab[:, k].rearrange("p a b -> p (a b)"), dr["w_mov"][2 + k]).then_inc(slab_in[k], 16)
                for t in range(TT + 1):
                    rows, tok = token_rows(t)
                    sp.wait_ge(v_free, 2 * t + 2)
                    sp.dma_start(out["v"][tok, :], vall[0:rows, t, :]).then_inc(v_out, 16)
                sp.wait_ge(v_out, 16 * (TT + 1))

            @block.tensor
            def _(pe):
                for k in range(2):
                    pe.wait_ge(slab_in[k], 32)
                for t in range(TT + 1):
                    rows, tok = token_rows(t)
                    for k in range(2):
                        n = 2 * t + k
                        if n >= 8:
                            pe.wait_ge(v_free, n - 7)
                        for kc in range(KC):
                            last = nc.tensor.matmul(ps[0:rows, n % 8, :], hT[:, kc, tok], v_slab[:, k, kc, :],
                                                    start=(kc == 0), stop=(kc == KC - 1))
                        last.then_inc(v_ready, 1)

            @block.scalar
            def _(act):
                for t in range(TT + 1):
                    rows, tok = token_rows(t)
                    for k in range(2):
                        act.wait_ge(v_ready, 2 * t + k + 1)
                        nc.scalar.activation(vall[0:rows, t, 512 * k:512 * (k + 1)], ps[0:rows, (2 * t + k) % 8, :],
                                             ACT.Copy).then_inc(v_free, 1)

        A = AT_MISC
        qk_slots = [(lay(A, [T]), lay(A + T, [T])),
                    (lay(AT_WB + 2 * D + 11 * P, [T]), lay(AT_WB + 2 * D + 11 * P + T, [T]))]
        qs, ks = lay(A + 2 * T, [H, NS]), lay(A + 2 * T + 256, [H, NS])
        A += 2 * T + 512
        ex = lay(A, [2, 2, SEQ])
        A += 4 * SEQ
        pT = lay(A, [SEQ // P, P])
        A += SEQ
        osb = lay(A, [TT, P])
        A += SEQ
        nmax, lsum, ssq, subln = lay(A, [2, 2]), lay(A + 4, [2, 2]), lay(A + 8, [TT]), lay(A + 16, [1])
        assert A + 17 <= AT_MT
        causal = lay(AT_WB + 2 * D, [P])
        ko = lay(AT_WB + 2 * D + P, [TT + 1, P])
        junk_a = lay(AT_WB + 2 * D + P + 9 * P, [P])

        names = ("ko_ready", "ko_free", "ko_out", "ko_clear", "s_ready", "s_masked", "m_ready", "e_ready", "l_ready", "p_ready",
                 "t_ready", "t_free", "o_ready", "o_free", "ss_ready", "rt_ready", "on_ready", "oT_ready", "oT_free",
                 "at_in", "qs_ready", "part")
        (ko_ready, ko_free, ko_out, ko_clear, s_ready, s_masked, m_ready, e_ready, l_ready, p_ready, t_ready, t_free,
         o_ready, o_free, ss_ready, rt_ready, on_ready, oT_ready, oT_free, at_in, qs_ready, part) = (sem(n) for n in names)

        def every_head(eng, head):
            with eng.Fori(0, H // 2 - 1) as pair:
                for slot in range(2):
                    head(pair * 2 + slot, slot, True)
            head(H - 2, 0, True)
            head(H - 1, 1, False)

        with nc.Block() as block:
            @block.sync
            def _(sp):
                sp.dma_start(causal, dr["causal"]).then_inc(at_in, 16)
                sp.dma_start(subln, dr["subln"]).then_inc(at_in, 16)
                for k in (1, 0):
                    stat_load(sp, wbuf, k, dr["w_stat"][T_QK + k])

                def k_out(h):
                    sp.wait_ge(ko_free, h * 3 + 3)
                    col = bass.ds(h * P, P)
                    sp.dma_start(out["k"][0:SEQ, col].rearrange("(t p) n -> p t n", p=P), ko[:, 0:TT, :]).then_inc(ko_out, 16)
                    sp.dma_start(out["k"][SEQ:T, col], ko[0:NS, TT, :]).then_inc(ko_out, 16)
                    sp.wait_ge(ko_out, h * 32 + 32)
                    sp.sem_inc(ko_clear, 1)

                with sp.Fori(0, H - 1) as h:
                    for k in (1, 0):
                        sp.wait_ge(acc_ready[k], h * 3 + 3 * (pairs + 1))
                        stat_load(sp, wbuf, k, dr["w_stat"][bass.ds(h * 2 + (T_QK + 2 + k), 1)].rearrange("a p n -> (a p) n"))
                    k_out(h)
                k_out(H - 1)

            @block.tensor
            def _(pe):
                def qk_chunk(h, n):
                    k, c = (1, n) if n < NC3 else (0, n - NC3)
                    if c == 0:
                        pe.wait_ge(w_in[k], h * 16 + 16 * (pairs + 1))
                    if n == NC3:
                        pe.wait_ge(acc_free[1], h * 3 + (3 * pairs + 6))
                    elif c:
                        pe.wait_ge(acc_free[k], h * 3 + (3 * pairs + 3 + c))
                    for kc in range(KC):
                        last = nc.tensor.matmul(ps[:, 7, 0:CW], wbuf[:, k, kc * P:(kc + 1) * P],
                                                hT[:, kc, chunk(c)], start=(kc == 0), stop=(kc == KC - 1))
                    last.then_inc(acc_ready[k], 1)

                def k_by_token(h, slot, r):
                    if r == 0:
                        pe.wait_ge(acc_free[0], h * 3 + (3 * pairs + 6))
                    else:
                        pe.wait_ge(ko_free, h * 3 + r)
                    for t in range(4 * r, min(4 * r + 4, TT + 1)):
                        rows, tok = token_rows(t)
                        last = nc.tensor.transpose(ps[0:rows, 7, (t % 4) * P:(t % 4 + 1) * P], qk_slots[slot][1][:, tok], ident[:, :])
                    last.then_inc(ko_ready, 1)

                def scores(h, slot, i, first=False):
                    qh, kh = qk_slots[slot]
                    for b in range(2):
                        half = slice(64 * b, 64 * b + 64)
                        if not first:
                            pe.wait_ge(e_ready, h * 16 + (2 * i + b - 1))
                        for c in range((i // 4) + 1):
                            w = min(512, (i + 1) * P - 512 * c)
                            last = nc.tensor.matmul(ps[:, 2 * b + c, 0:w], qh[half, i * P:(i + 1) * P],
                                                    kh[half, 512 * c:512 * c + w], start=True, stop=True)
                        last.then_inc(s_ready, 1)

                def head(h, slot, more):
                    for i in range(TT):
                        if i + 1 < TT:
                            scores(h, slot, i + 1)
                        pe.wait_ge(p_ready, h * TT + (i + 1))
                        pe.wait_ge(t_free, START + h * TT + i)
                        for j in range(i + 1):
                            last = nc.tensor.transpose(ps[:, 4 + j // 4, (j % 4) * P:(j % 4 + 1) * P],
                                                       ex[:, i % 2, 0, j * P:(j + 1) * P], ident[:, :])
                        last.then_inc(t_ready, 1)
                        if i == 0:
                            pe.wait_ge(oT_free, START + h * 2)
                            pe.wait_ge(ko_free, h * 3 + 3)
                        if more and i < 2 * NC3:
                            qk_chunk(h + 1, i)
                        elif more:
                            k_by_token(h + 1, 1 - slot, i - 2 * NC3)
                        pe.wait_ge(t_free, START + h * TT + (i + 1))
                        if i:
                            pe.wait_ge(o_free, h * TT + i)
                        for j in range(i + 1):
                            last = nc.tensor.matmul(ps[:, 6, 0:P], pT[:, j, :],
                                                    vall[:, j, bass.ds(h * P, P)], start=(j == 0), stop=(j == i))
                        last.then_inc(o_ready, 1)
                    if more:
                        k_by_token(h + 1, 1 - slot, 2)
                        scores(h + 1, 1 - slot, 0)
                    pe.wait_ge(on_ready, h + 1)
                    for r in range(2):
                        if more and r:
                            pe.wait_ge(ko_free, h * 3 + 6)
                        for t in range(4 * r, 4 * r + 4):
                            last = nc.tensor.transpose(ps[:, 6 + r, (t % 4) * P:(t % 4 + 1) * P], osb[:, t, :], ident[:, :])
                        last.then_inc(oT_ready, 1)

                for n in range(2 * NC3):
                    qk_chunk(0, n)
                for r in range(3):
                    k_by_token(0, 0, r)
                scores(0, 0, 0, first=True)
                every_head(pe, head)

            @block.scalar
            def _(act):
                def q_in(h, slot, c):
                    act.wait_ge(acc_ready[0], h * 3 + (3 * pairs + c + 1))
                    nc.scalar.activation(qk_slots[slot][0][:, chunk(c)], ps[:, 7, 0:CW], ACT.Copy,
                                         scale=HD ** -0.5).then_inc(acc_free[0], 1)

                def k_tiles(h, r):
                    if r == 0:
                        act.wait_ge(ko_clear, START + h)
                    act.wait_ge(ko_ready, h * 3 + (r + 1))
                    if r < 2:
                        nc.scalar.activation(ko[:, 4 * r:4 * r + 4].rearrange("p t n -> p (t n)"), ps[:, 7, :],
                                             ACT.Copy).then_inc(ko_free, 1)
                    else:
                        nc.scalar.activation(ko[0:NS, TT, :], ps[0:NS, 7, 0:P], ACT.Copy).then_inc(ko_free, 1)

                def exps(h, i):
                    for b in range(2):
                        act.wait_ge(m_ready, h * 16 + (2 * i + b + 1))
                        nc.scalar.activation(ex[:, i % 2, b, 0:(i + 1) * P],
                                             ps[:, 2 * b:2 * b + 2, :].rearrange("p a n -> p (a n)")[:, 0:(i + 1) * P],
                                             ACT.Exp, bias=nmax[:, i % 2, b:b + 1],
                                             accum_out=lsum[:, i % 2, b:b + 1]).then_inc(e_ready, 1)

                def head(h, slot, more):
                    for i in range(TT):
                        if more and NC3 < i <= 2 * NC3:
                            q_in(h + 1, 1 - slot, i - NC3 - 1)
                        if more and i == TT - 1:
                            k_tiles(h + 1, 0)
                        act.wait_ge(t_ready, h * TT + (i + 1))
                        nc.scalar.activation(pT[:, 0:i + 1, :].rearrange("p j n -> p (j n)"),
                                             ps[:, 4:6, :].rearrange("p a n -> p (a n)")[:, 0:(i + 1) * P],
                                             ACT.Copy).then_inc(t_free, 1)
                        if i + 1 < TT:
                            exps(h, i + 1)
                    if more:
                        k_tiles(h + 1, 1)
                        k_tiles(h + 1, 2)
                    act.wait_ge(ss_ready, h + 1)
                    nc.scalar.activation(ssq, ssq, ACT.Sqrt).then_inc(rt_ready, 1)
                    if more:
                        exps(h + 1, 0)
                    for r in range(2):
                        act.wait_ge(oT_ready, h * 2 + (r + 1))
                        nc.scalar.activation(one(attT[:, bass.ds(h, 1), 512 * r:512 * (r + 1)]), ps[:, 6 + r, :], ACT.Copy,
                                             scale=subln).then_inc(oT_free, 1)

                act.wait_ge(at_in, 32)
                for c in range(NC3):
                    q_in(0, 0, c)
                for r in range(3):
                    k_tiles(0, r)
                exps(0, 0)
                every_head(act, head)

            @block.vector
            def _(dve):
                def k_in(h, slot, c):
                    dve.wait_ge(acc_ready[1], h * 3 + (3 * pairs + c + 1))
                    nc.vector.tensor_copy(qk_slots[slot][1][:, chunk(c)], ps[:, 7, 0:CW]).then_inc(acc_free[1], 1)

                def samples_in(h, slot):
                    dve.wait_ge(acc_free[0], h * 3 + (3 * pairs + 6))
                    dve.wait_ge(acc_free[1], h * 3 + (3 * pairs + 6))
                    qh, kh = qk_slots[slot]
                    nc.vector.tensor_copy(one(qs[:, bass.ds(h, 1), :]), qh[:, SEQ:T])
                    nc.vector.tensor_copy(one(ks[:, bass.ds(h, 1), :]), kh[:, SEQ:T]).then_inc(qs_ready, 1)

                def maxima(h, i):
                    for b in range(2):
                        n = h * 16 + (2 * i + b + 1)
                        flat = ps[:, 2 * b:2 * b + 2, :].rearrange("p a n -> p (a n)")
                        dve.wait_ge(s_ready, n)
                        diag = flat[:, i * P:(i + 1) * P]
                        nc.vector.tensor_tensor(diag, diag, causal, ALU.add).then_inc(s_masked, 1)
                        dve.wait_ge(s_masked, n)
                        nc.vector.tensor_reduce(nmax[:, i % 2, b:b + 1], flat[:, 0:(i + 1) * P], AX.X, ALU.max,
                                                negate=True).then_inc(m_ready, 1)

                def probabilities(h, i):
                    dve.wait_ge(e_ready, h * 16 + (2 * i + 2))
                    nc.vector.reciprocal(lsum[:, i % 2, :], lsum[:, i % 2, :]).then_inc(l_ready, 1)
                    dve.wait_ge(l_ready, h * 3 * TT + (3 * i + 1))
                    nc.vector.tensor_tensor(lsum[:, i % 2, :], lsum[:, i % 2, :], neg_lam[:, :], ALU.mult).then_inc(l_ready, 1)
                    dve.wait_ge(l_ready, h * 3 * TT + (3 * i + 2))
                    e0, e1 = ex[:, i % 2, 0, 0:(i + 1) * P], ex[:, i % 2, 1, 0:(i + 1) * P]
                    nc.vector.tensor_scalar(e0, e0, lsum[:, i % 2, 0:1], None, ALU.mult).then_inc(l_ready, 1)
                    dve.wait_ge(l_ready, h * 3 * TT + (3 * i + 3))
                    nc.vector.scalar_tensor_tensor(e0, e1, lsum[:, i % 2, 1:2], e0, ALU.mult, ALU.add).then_inc(p_ready, 1)

                def output_in(h, i):
                    dve.wait_ge(o_ready, h * TT + (i + 1))
                    nc.vector.tensor_copy(osb[:, i, :], ps[:, 6, 0:P]).then_inc(o_free, 1)
                    dve.wait_ge(o_free, h * TT + (i + 1))
                    nc.vector.tensor_tensor_reduce(junk_a, osb[:, i, :], osb[:, i, :], 1.0, 0.0, ALU.mult, ALU.add,
                                                   ssq[:, i:i + 1]).then_inc(part, 1)

                def head(h, slot, more):
                    for i in range(TT):
                        probabilities(h, i)
                        if more and 1 <= i <= NC3:
                            k_in(h + 1, 1 - slot, i - 1)
                        if i + 1 < TT:
                            maxima(h, i + 1)
                        elif more:
                            samples_in(h + 1, 1 - slot)
                        if i:
                            output_in(h, i - 1)
                    output_in(h, TT - 1)
                    dve.wait_ge(part, h * TT + TT)
                    s2 = (1.0 - LAM_INIT) ** 2
                    nc.vector.tensor_scalar(ssq, ssq, 1 / (P * s2), EPS / s2, ALU.mult, ALU.add).then_inc(ss_ready, 1)
                    if more:
                        maxima(h + 1, 0)
                    dve.wait_ge(rt_ready, h * 2 + 1)
                    nc.vector.reciprocal(ssq, ssq).then_inc(rt_ready, 1)
                    dve.wait_ge(rt_ready, h * 2 + 2)
                    nc.vector.tensor_tensor(osb, osb, ssq.unsqueeze(2).broadcast_to([P, TT, P]), ALU.mult).then_inc(on_ready, 1)

                dve.wait_ge(at_in, 32)
                for c in range(NC3):
                    k_in(0, 0, c)
                samples_in(0, 0)
                maxima(0, 0)
                every_head(dve, head)
        pairs += H

        NK = SEQ + NS
        ROWS = 2 * H * NNEW
        vpg = lay(AT_V, [PAGES, D])
        v_new = vall[0:NS, TT, :]
        B = AT_MISC + 2 * T + 512
        qpad = lay(B, [H * (ROWS + 8)])
        es, pTs, o4 = lay(B + 576, [NK]), lay(B + 576 + NK, [PAGES + 1, NS]), lay(B + 576 + NK + 288, [D])
        B += 576 + NK + 288 + D
        sgn, c_new, nm_s, l_s, t_s, first_s = (lay(B + j, [1]) for j in range(6))
        pgs, pgv = lay(B + 8, [NSEQ * PAGES], I32), lay(B + 80, [NSEQ * PAGES], I32)
        ss_s = lay(B + 160, [H])
        kpg, kT = lay(AT_WB, [2, D]), lay(AT_WB + 2 * D, [2, H, P])
        C = AT_WB + 4 * D
        causal_new, pick = lay(C, [NSEQ, NS]), lay(C + 256, [NS])
        osm, osq = lay(C + 288, [H, P]), lay(C + 288 + D, [H, P])
        scr_o = nc.dram_tensor("scr_o", (NS, D), F32, kind="Internal").ap()
        n_phys = dr["cache_k"].shape[0]

        names = ("sc_in", "pg_in", "pgv_in", "vp_in", "q_zero", "qp_ready", "kt_ready", "kt_free", "page_used", "sn_ready",
                 "sn_masked", "mn_ready", "en_ready", "ln_ready", "pn_ready", "ptn_ready", "ptn_free", "on_acc", "on_free",
                 "o_out", "sgn_v", "o4_clear")
        (sc_in, pg_in, pgv_in, vp_in, q_zero, qp_ready, kt_ready, kt_free, page_used, sn_ready, sn_masked, mn_ready, en_ready,
         ln_ready, pn_ready, ptn_ready, ptn_free, on_acc, on_free, o_out, sgn_v, o4_clear) = (sem(n) for n in names)
        kp_in = [sem(f"kp_in{k}") for k in range(2)]
        flat_s = ps[0:ROWS, 4:7, :].rearrange("p a n -> p (a n)")
        with nc.Block() as block:
            @block.sync
            def _(sp):
                sp.dma_start(causal_new[0:ROWS].rearrange("p a b -> p (a b)"), dr["causal_new"]).then_inc(sc_in, 16)
                sp.dma_start(pick[0:ROWS, :], dr["pick"]).then_inc(sc_in, 16)
                sp.dma_start(first_s[0:ROWS, :], dr["first"]).then_inc(sc_in, 16)
                sp.dma_start(pgs[0:1, :], dr["pages"]).then_inc(pg_in, 16)
                sp.wait_ge(pg_in, 16)
                with sp.Fori(0, NSEQ) as s:
                    for p in range(PAGES):
                        page = sp.value_load(pgs[0:1, bass.ds(s * PAGES + p, 1)], min_val=0, max_val=n_phys - 1)
                        if p < 2:
                            sp.wait_ge(kt_ready, START + s * PAGES)
                        else:
                            sp.wait_ge(kt_ready, START + s * PAGES + (p - 1))
                        sp.dma_start(kpg[:, p % 2, :], dr["cache_k"][bass.ds(page, 1)].rearrange("a p n -> (a p) n")
                                     ).then_inc(kp_in[p % 2], 16)

            @block.gpsimd
            def _(pool):
                pool.dma_start(pgv[0:1, :], dr["pages"]).then_inc(pgv_in, 16)
                pool.wait_ge(pgv_in, 16)
                with pool.Fori(0, NSEQ) as s:
                    pool.wait_ge(on_acc, START + s)
                    for p in range(PAGES):
                        page = pool.value_load(pgv[0:1, bass.ds(s * PAGES + p, 1)], min_val=0, max_val=n_phys - 1)
                        pool.dma_start(vpg[:, p, :], dr["cache_v"][bass.ds(page, 1)].rearrange("a p n -> (a p) n")
                                       ).then_inc(vp_in, 16)

            def out_rows(h):
                return slice(32 * (h % 4), 32 * (h % 4) + NNEW), slice((1 + h // 4) * P, (2 + h // 4) * P)

            @block.tensor
            def _(pe):
                def page_scores(s, p):
                    pe.wait_ge(kt_free, START + s * PAGES + (p + 1))
                    for h in range(H):
                        last = nc.tensor.matmul(flat_s[:, p * P:(p + 1) * P], qpad[:, h * ROWS:(h + 1) * ROWS],
                                                kT[:, p % 2, h, :], start=(h == 0), stop=(h == H - 1))
                    last.then_inc(page_used, 1)

                def probabilities_back(s):
                    pe.wait_ge(pn_ready, s + 1)
                    pe.wait_ge(ptn_free, START + s)
                    for p in range(PAGES + 1):
                        w = P if p < PAGES else NS
                        last = nc.tensor.matmul(ps[0:w, 7, p * NS:(p + 1) * NS], es[0:ROWS, p * P:p * P + w], pick[0:ROWS, :],
                                                start=True, stop=True)
                    last.then_inc(ptn_ready, 1)

                def outputs(s):
                    pe.wait_ge(ptn_free, START + s + 1)
                    pe.wait_ge(vp_in, (s + 1) * 16 * PAGES)
                    alone(pe)
                    for half in range(H // 4):
                        for p in range(PAGES + 1):
                            for h in range(4 * half, 4 * half + 4):
                                rows, cols = out_rows(h)
                                k = P if p < PAGES else NS
                                values = vpg[:, p, h * P:(h + 1) * P] if p < PAGES else v_new[:, h * P:(h + 1) * P]
                                last = nc.tensor.matmul(ps[rows, 6, cols], pTs[0:k, p, NNEW * h:NNEW * (h + 1)], values,
                                                        start=(p == 0), stop=(p == PAGES), skip_group_check=True)
                    last.then_inc(on_acc, 1)

                def sequence(s, first):
                    pe.wait_ge(qp_ready, s + 1)
                    for p in range(PAGES):
                        pe.wait_ge(kp_in[p % 2], s * 64 + 16 * (p // 2 + 1))
                        pe.wait_ge(kt_free, START + s * PAGES + max(p - 1, 0))
                        for h in range(H):
                            last = nc.tensor.transpose(ps[:, 2 * (p % 2) + h // 4, (h % 4) * P:(h % 4 + 1) * P],
                                                       kpg[:, p % 2, h * P:(h + 1) * P], ident[:, :])
                        last.then_inc(kt_ready, 1)
                        if p == 1:
                            pe.wait_ge(en_ready, START + s)
                        if p:
                            page_scores(s, p - 1)
                        if p == 2 and not first:
                            probabilities_back(s - 1)
                        if p == 4 and not first:
                            outputs(s - 1)
                    page_scores(s, PAGES - 1)
                    pe.wait_ge(on_free, START + s)
                    for h in range(H):
                        last = nc.tensor.matmul(flat_s[:, SEQ:NK], qpad[:, h * ROWS:(h + 1) * ROWS], ks[:, h, :],
                                                start=(h == 0), stop=(h == H - 1))
                    last.then_inc(sn_ready, 1)

                pe.wait_ge(sc_in, 48)
                sequence(0, True)
                with pe.Fori(1, NSEQ) as s:
                    sequence(s, False)
                probabilities_back(NSEQ - 1)
                outputs(NSEQ - 1)

            @block.scalar
            def _(act):
                def o_store(s):
                    act.wait_ge(on_free, START + s + 1)
                    for g in range(4):
                        act.dma_start(scr_o[bass.ds(s * NNEW, NNEW), :].rearrange("r (b g n) -> r g b n", b=2, g=4)[:, g],
                                      o4[32 * g:32 * g + NNEW, 0:2 * P].rearrange("r (b n) -> r b n", b=2)).then_inc(o_out, 16)
                    act.wait_ge(o_out, s * 64 + 64)
                    act.sem_inc(o4_clear, 1)

                def sequence(s, first):
                    for p in range(PAGES):
                        act.wait_ge(kt_ready, START + s * PAGES + (p + 1))
                        act.wait_ge(page_used, START + s * PAGES + max(p - 1, 0))
                        nc.scalar.activation(kT[:, p % 2].rearrange("p h n -> p (h n)"),
                                             ps[:, 2 * (p % 2):2 * (p % 2) + 2, :].rearrange("p a n -> p (a n)"),
                                             ACT.Copy).then_inc(kt_free, 1)
                    act.wait_ge(mn_ready, s + 1)
                    act.wait_ge(ptn_ready, START + s)
                    nc.scalar.activation(es[0:ROWS, :], flat_s[:, 0:NK], ACT.Exp, bias=nm_s[0:ROWS, :],
                                         accum_out=l_s[0:ROWS, :]).then_inc(en_ready, 1)
                    if not first:
                        o_store(s - 1)

                sequence(0, True)
                with act.Fori(1, NSEQ) as s:
                    sequence(s, False)
                o_store(NSEQ - 1)

            @block.vector
            def _(dve):
                def values_out(s):
                    dve.wait_ge(ptn_ready, START + s + 1)
                    dve.wait_ge(on_acc, START + s)
                    nc.vector.tensor_copy(pTs[:, 0:PAGES, :].rearrange("p a b -> p (a b)"), ps[:, 7, 0:PAGES * NS])
                    nc.vector.tensor_copy(pTs[0:NS, PAGES, :], ps[0:NS, 7, PAGES * NS:(PAGES + 1) * NS]).then_inc(ptn_free, 1)
                    dve.wait_ge(on_acc, START + s + 1)
                    dve.wait_ge(o4_clear, START + s)
                    for g in range(4):
                        last = nc.vector.tensor_copy(o4[32 * g:32 * g + NNEW, 0:2 * P], ps[32 * g:32 * g + NNEW, 6, P:3 * P])
                    last.then_inc(on_free, 1)

                def sequence(s, first):
                    dve.wait_ge(sn_ready, START + s)
                    for b in range(2):
                        half = slice(64 * b, 64 * b + 64)
                        last = nc.vector.tensor_copy(diag[half, :, NNEW * b:NNEW * (b + 1)], qs[half, :, bass.ds(s * NNEW, NNEW)])
                    last.then_inc(qp_ready, 1)
                    if not first:
                        nc.vector.tensor_scalar(es[0:ROWS, :], es[0:ROWS, :], c_new[0:ROWS, 0:1], None, ALU.mult).then_inc(pn_ready, 1)
                        values_out(s - 1)
                    dve.wait_ge(sn_ready, START + s + 1)
                    new = flat_s[:, SEQ:NK]
                    nc.vector.tensor_tensor(new, new, one(causal_new[0:ROWS, bass.ds(s, 1), :]), ALU.add).then_inc(sn_masked, 1)
                    dve.wait_ge(sn_masked, s + 1)
                    nc.vector.tensor_reduce(nm_s[0:ROWS, :], flat_s[:, 0:NK], AX.X, ALU.max, negate=True).then_inc(mn_ready, 1)
                    dve.wait_ge(en_ready, START + s + 1)
                    nc.vector.reciprocal(l_s[0:ROWS, :], l_s[0:ROWS, :]).then_inc(ln_ready, 1)
                    dve.wait_ge(ln_ready, s * 2 + 1)
                    nc.vector.tensor_tensor(c_new[0:ROWS, :], l_s[0:ROWS, :], sgn[0:ROWS, :], ALU.mult).then_inc(ln_ready, 1)
                    dve.wait_ge(ln_ready, s * 2 + 2)

                nc.vector.memset(qpad, 0.0).then_inc(q_zero, 1)
                dve.wait_ge(q_zero, 1)
                dve.wait_ge(sc_in, 48)
                nl = neg_lam[0:ROWS, 1:2]
                nc.vector.tensor_scalar(t_s[0:ROWS, :], nl, -1.0, 1.0, ALU.mult, ALU.add).then_inc(sgn_v, 1)
                dve.wait_ge(sgn_v, 1)
                nc.vector.tensor_scalar(sgn[0:ROWS, :], first_s[0:ROWS, :], t_s[0:ROWS, 0:1], nl, ALU.mult, ALU.add).then_inc(sgn_v, 1)
                dve.wait_ge(sgn_v, 2)
                diag = qpad.rearrange("p (h x) -> p h x", x=ROWS + 2 * NNEW)
                sequence(0, True)
                with dve.Fori(1, NSEQ) as s:
                    sequence(s, False)
                nc.vector.tensor_scalar(es[0:ROWS, :], es[0:ROWS, :], c_new[0:ROWS, 0:1], None, ALU.mult).then_inc(pn_ready, 1)
                values_out(NSEQ - 1)

        os_in, n_v, n_a, n_pe = sem("os_in"), sem("n_v"), sem("n_a"), sem("n_pe")
        with nc.Block() as block:
            @block.sync
            def _(sp):
                sp.dma_start(osm[0:NS].rearrange("p h n -> p (h n)"), scr_o).then_inc(os_in, 16)

            @block.vector
            def _(dve):
                dve.wait_ge(os_in, 16)
                o, q, r = osm[0:NS], osq[0:NS], ss_s[0:NS]
                s2 = (1.0 - LAM_INIT) ** 2
                nc.vector.tensor_tensor(q, o, o, ALU.mult).then_inc(n_v, 1)
                dve.wait_ge(n_v, 1)
                nc.vector.tensor_reduce(r, q, AX.X, ALU.add).then_inc(n_v, 1)
                dve.wait_ge(n_v, 2)
                nc.vector.tensor_scalar(r, r, 1 / (P * s2), EPS / s2, ALU.mult, ALU.add).then_inc(n_v, 1)
                dve.wait_ge(n_a, 1)
                nc.vector.reciprocal(r, r).then_inc(n_v, 1)
                dve.wait_ge(n_v, 4)
                nc.vector.tensor_tensor(o, o, r.unsqueeze(2).broadcast_to([NS, H, P]), ALU.mult).then_inc(n_v, 1)

            @block.tensor
            def _(pe):
                pe.wait_ge(n_v, 5)
                for h in range(H):
                    last = nc.tensor.transpose(ps[:, 0, h * NS:(h + 1) * NS], osm[0:NS, h, :], ident[0:NS, 0:NS])
                last.then_inc(n_pe, 1)

            @block.scalar
            def _(act):
                act.wait_ge(n_v, 3)
                nc.scalar.activation(ss_s[0:NS], ss_s[0:NS], ACT.Sqrt).then_inc(n_a, 1)
                act.wait_ge(n_pe, 1)
                nc.scalar.activation(attT[:, :, SEQ:T], ps[:, 0, 0:H * NS].rearrange("p (h t) -> p h t", h=H), ACT.Copy,
                                     scale=subln).then_inc(n_a, 1)

        with nc.Block() as block:
            merge(block, T_GA, attT, True, pairs)
        pairs += KC

        w_q = [lay(AT_HT, [PH, D]), lay(AT_V, [PH, D])]
        h2t_out = lay(10 * D + 64, [2, KC, P])
        o_slab = lay(AT_WB, [2, KC, 512])
        xr, x1, hn = lay(0, [2, D]), lay(2 * D, [2, D]), lay(4 * D, [2, D])
        hg, g_row, junk6, ss6 = lay(6 * D, [2, D]), lay(8 * D, [D]), lay(9 * D, [D]), lay(10 * D, [2])
        scr_x1 = nc.dram_tensor("scr_x1", (T, D), F32, kind="Internal").ap()
        scr_h2 = nc.dram_tensor("scr_h2", (T, D), F32, kind="Internal").ap()
        scr_h2T = nc.dram_tensor("scr_h2T", (TT + 1, P, KC * P), F32, kind="Internal").ap()
        NB = TT + 1
        os_w, gr_in, wq_in = sem("os_w"), sem("gr_in"), sem("wq_in")
        x1_acc, x1_ready, hg_ready = sem("x1_acc"), sem("x1_ready"), sem("hg_ready")
        x1_out = [sem(f"x1_out{k}") for k in range(2)]

        NQ = 2 * PH
        keys_in = sem("keys_in")
        RING, STEP = 8, TOPK
        PAIR = 2
        ring = [lay(at + 2 * D * k, [2 * D]) for at in (0, AT_MT) for k in range(RING // 2)]
        A = 12 * D + 64
        def take(shape, dt=F32):
            nonlocal A
            at, A = A, A + int(np.prod(shape))
            return lay(at, shape, dt)
        keys = take([NQ, PK])
        h2t, q_tok = take([KC, P]), take([2 * P])
        qst = take([2, P])
        sct, s2t = take([2, PK]), take([2, PK])
        vals, idxu, idxf = take([2, TOPK]), take([2, TOPK], U32), take([2, TOPK])
        cand, cand2 = take([TOPK, TOPK]), take([TOPK * TOPK])
        sv, si, sab, sabf = take([TOPK]), take([TOPK], U32), take([2, TOPK], U32), take([2, TOPK])
        e12, iota = take([2, TOPK]), take([TOPK])
        logit_next, idx_next = take([PH * TOPK]), take([PH * TOPK], U32)
        assert A <= AT_MT
        A = AT_V + PH * D
        hot = take([2, TOPK, TOPK])
        assert A <= AT_WB
        h2, x1b, yo, g_fin, junk_y = (take([D]) for _ in range(5))
        junk = take([2, D])
        diag = take([4, P])
        gates, gsum = take([PH, TOPK]), take([PH])
        idx_cur, idx_st = take([PH * TOPK], U32), take([STEP], U32)
        act_in, act_out, wgt = take([STEP]), take([PAIR]), take([PAIR])
        ss8 = take([1])
        KCH = 16

        names = ("h2t_in", "q_acc", "q_out", "q_turned", "pc_in", "h2_in", "x1_in", "q_st", "s_acc", "sc_done", "tk_v", "tk_done", "idx_cp", "idx_stg",
                 "slot_free", "dots", "gelu_d", "wgt_d", "diag_d", "init_d", "ex_d", "gt_v",
                 "yo_d", "y_out", "acc_out", "yo_clear")
        (h2t_in, q_acc, q_out, q_turned, pc_in, h2_in, x1_in, q_st, s_acc, sc_done, tk_v, tk_done, idx_cp, idx_stg, slot_free, dots, gelu_d, wgt_d, diag_d,
         init_d, ex_d, gt_v, yo_d, y_out, acc_out, yo_clear) = (sem(n) for n in names)
        row_in = [sem(f"row_in{k}") for k in range(RING)]
        acc = ps[:, 0:2, :].rearrange("p a n -> p (a n)")

        def queries_pe(pe, t, b, h, halves=(0, 1)):
            pe.wait_ge(h2t_in, b * 16 + 16)
            for k in halves:
                for kc in range(KC):
                    last = nc.tensor.matmul(ps[:, 7, k * P:(k + 1) * P], h2t[:, kc, :],
                                            one(w_q[k][:, bass.ds(h, 1), kc * P:(kc + 1) * P]),
                                            start=(kc == 0), stop=(kc == KC - 1))
                if k:
                    last.then_inc(q_acc, 1)

        def queries_act(act, t):
            act.wait_ge(q_acc, t + 1)
            nc.scalar.activation(q_tok, ps[:, 7, 0:2 * P], ACT.Copy).then_inc(q_out, 1)

        def turn_pe(pe, t):
            pe.wait_ge(q_out, t + 1)
            pe.wait_ge(sc_done, START + t)
            for k in range(2):
                last = nc.tensor.transpose(ps[:, 6, k * P:(k + 1) * P], q_tok[:, k * P:(k + 1) * P], ident[:, :])
            last.then_inc(q_turned, 1)

        def turn_act(act, t):
            act.wait_ge(q_turned, t + 1)
            act.wait_ge(s_acc, START + t)
            nc.scalar.activation(qst.rearrange("p a n -> p (a n)"), ps[:, 6, 0:2 * P], ACT.Copy).then_inc(q_st, 1)

        def scores_pe(pe, t, h):
            pe.wait_ge(q_st, t + 1)
            for k in range(2):
                last = nc.tensor.matmul(ps[:, 6, k * PK:(k + 1) * PK], qst[:, k, :], one(keys[:, bass.ds(h * 2 + k, 1), :]),
                                        start=True, stop=True)
            last.then_inc(s_acc, 1)

        def scores_act(act, t):
            act.wait_ge(s_acc, START + t + 1)
            act.wait_ge(tk_done, START + t)
            nc.scalar.activation(sct.rearrange("p a n -> p (a n)"), ps[:, 6, 0:2 * PK], ACT.Copy).then_inc(sc_done, 1)

        FIRST_J = 6
        CHOICE = 6

        def choose_dve(dve, t, h, copied, parts=range(CHOICE)):
            links = (0, 3, 5, 8, 10, 13)
            link = [links[parts[0]]]

            def done(ins):
                link[0] += 1
                ins.then_inc(tk_v, 1)
                dve.wait_ge(tk_v, t * KCH + link[0])
                alone(dve)

            v = nc.vector
            flat = cand.rearrange("p a b -> p (a b)")
            mine = bass.ds(h * TOPK, TOPK)
            if 0 in parts:
                dve.wait_ge(sc_done, START + t + 1)
                alone(dve)
                for k in range(2):
                    last = v.max(vals[:, k, 0:8], sct[:, k, :])
                done(last)
                for k in range(2):
                    v.match_replace(s2t[:, k, :], vals[:, k, 0:8], sct[:, k, :], LOWEST)
                    last = v.max_index(idxu[:, k, 0:8], vals[:, k, 0:8], sct[:, k, :])
                done(last)
                for k in range(2):
                    last = v.max(vals[:, k, 8:16], s2t[:, k, :])
                done(last)
            if 1 in parts:
                for k in range(2):
                    v.max_index(idxu[:, k, 8:16], vals[:, k, 8:16], s2t[:, k, :])
                done(v.tensor_tensor(cand, vals[:, 0, :].unsqueeze(2).broadcast_to([P, TOPK, TOPK]),
                                     vals[:, 1, :].unsqueeze(1).broadcast_to([P, TOPK, TOPK]), ALU.add))
                v.tensor_copy(idxf.rearrange("p a b -> p (a b)"), idxu.rearrange("p a b -> p (a b)"))
                done(v.max(sv[:, 0:8], flat))
            if 2 in parts:
                v.match_replace(cand2, sv[:, 0:8], flat, LOWEST)
                done(v.max_index(si[:, 0:8], sv[:, 0:8], flat))
                done(v.max(sv[:, 8:16], cand2))
                done(v.max_index(si[:, 8:16], sv[:, 8:16], cand2))
            if 3 in parts:
                v.tensor_scalar(sab[:, 0, :], si, 4, None, ALU.logical_shift_right)
                done(v.tensor_scalar(sab[:, 1, :], si, 15, None, ALU.bitwise_and))
                done(v.tensor_copy(sabf.rearrange("p a b -> p (a b)"), sab.rearrange("p a b -> p (a b)")))
            if 4 in parts:
                for k in range(2):
                    last = v.tensor_tensor(hot[:, k], sabf[:, k, :].unsqueeze(2).broadcast_to([P, TOPK, TOPK]),
                                           iota.unsqueeze(1).broadcast_to([P, TOPK, TOPK]), ALU.is_equal)
                done(last)
                for k in range(2):
                    last = v.tensor_tensor(hot[:, k], hot[:, k], idxf[:, k, :].unsqueeze(1).broadcast_to([P, TOPK, TOPK]), ALU.mult)
                done(last)
                done(v.tensor_reduce(e12.rearrange("p a b -> p (a b)"), hot.rearrange("p k a b -> p (k a) b"), AX.X, ALU.add))
            if 5 in parts:
                done(v.tensor_scalar(logit_next[:, mine], sv, sv[:, 0:1], None, ALU.subtract))
                done(v.tensor_scalar(e12[:, 0, :], e12[:, 0, :], float(PK), None, ALU.mult))
                dve.wait_ge(idx_cp, START + copied)
                done(v.tensor_tensor(idx_next[:, mine], e12[:, 0, :], e12[:, 1, :], ALU.add))
                v.tensor_copy(e12[:, 0, 0:1], e12[:, 1, 0:1]).then_inc(tk_done, 1)
            assert link[0] == (*links, KCH)[parts[-1] + 1], link

        def h2t_load(sp, b):
            sp.dma_start(h2t.rearrange("p c t -> p (c t)"), scr_h2T[bass.ds(b, 1)].rearrange("a p n -> (a p) n")).then_inc(h2t_in, 16)

        with nc.Block() as block:
            @block.sync
            def _(sp):
                for k in range(2):
                    sp.dma_start(o_slab[:, k].rearrange("p a b -> p (a b)"), dr["w_mov"][4 + k]).then_inc(os_w, 16)
                sp.dma_start(g_row, dr["g_ffn_row"].broadcast_to([P, D])).then_inc(gr_in, 16)
                sp.dma_start(iota, dr["iota16"]).then_inc(pc_in, 16)

                def rows_out(t):
                    rows, tok = token_rows(t)
                    sp.wait_ge(x1_ready, t + 1)
                    sp.dma_start(scr_x1[tok, :], x1[0:rows, t % 2, :]).then_inc(x1_out[t % 2], 16)
                    sp.wait_ge(hg_ready, t + 1)
                    sp.dma_start(scr_h2[tok, :], hg[0:rows, t % 2, :]).then_inc(x1_out[t % 2], 16)
                    sp.wait_ge(hT_done, START + NB + t + 1)
                    sp.dma_start(scr_h2T[t], h2t_out[:, t % 2].rearrange("p c t -> p (c t)")).then_inc(x1_out[t % 2], 16)

                for t in range(TT + 1):
                    rows, tok = token_rows(t)
                    if t >= 2:
                        sp.wait_ge(x1_ready, t - 1)
                    if t == 2:
                        sp.wait_ge(x1_out[0], 48)
                        h2t_load(sp, 0)
                    sp.dma_start(xr[0:rows, t % 2, :], dr["x"][tok, :]).then_inc(x_in[t % 2], 16)
                    if t >= 1:
                        rows_out(t - 1)
                rows_out(TT)
                sp.wait_ge(x1_out[0], 48 * (TT // 2 + 1))
                sp.wait_ge(x1_out[1], 48 * (TT // 2))
                sp.wait_ge(wq_in, 32)

            @block.gpsimd
            def _(pool):
                pool.dma_start(keys.rearrange("p m k -> p (m k)"), dr["keys"]).then_inc(keys_in, 16)
                for k in range(2):
                    pool.dma_start(w_q[k], dr["w_stat"][T_QUERY + k:T_QUERY + 2 * PH:2].rearrange("a p n -> p a n")
                                   ).then_inc(wq_in, 16)

            @block.tensor
            def _(pe):
                def turn(t):
                    rows, tok = token_rows(t)
                    pe.wait_ge(xn_done, NB + t + 1)
                    pe.wait_ge(hT_done, START + NB + t)
                    for c in range(KC):
                        last = nc.tensor.transpose(ps[:, 4 + c // 4, (c % 4) * P:(c % 4) * P + rows],
                                                   hn[0:rows, t % 2, c * P:(c + 1) * P], ident[0:rows, 0:rows])
                    last.then_inc(xT_done, 1)

                def choice(h):
                    queries_pe(pe, h, 0, h)
                    if h:
                        scores_pe(pe, h - 1, h - 1)
                    turn_pe(pe, h)

                pe.wait_ge(os_w, 32)
                for t in range(TT + 1):
                    rows, tok = token_rows(t)
                    if t >= 2:
                        pe.wait_ge(x1_ready, t - 1)
                    for k in range(2):
                        for kc in range(KC):
                            last = nc.tensor.matmul(ps[0:rows, 2 * (t % 2) + k, :], mT[:, kc, tok], o_slab[:, k, kc, :],
                                                    start=(kc == 0), stop=(kc == KC - 1))
                    last.then_inc(x1_acc, 1)
                    if t:
                        turn(t - 1)
                    if t == 2:
                        pe.wait_ge(wq_in, 32)
                        pe.wait_ge(keys_in, 16)
                    if t >= 2:
                        choice(t - 2)
                turn(TT)
                for h in range(TT - 1, PH):
                    choice(h)
                scores_pe(pe, PH - 1, PH - 1)

            @block.vector
            def _(dve):
                dve.wait_ge(gr_in, 16)
                dve.wait_ge(pc_in, 16)
                for t in range(TT + 1):
                    rows, tok = token_rows(t)
                    k = t % 2
                    dve.wait_ge(x1_acc, t + 1)
                    dve.wait_ge(x_in[k], 16 * (t // 2 + 1) + 16 * (TT // 2 + 1 - k))
                    if t >= 2:
                        dve.wait_ge(x1_out[k], 48 * (t // 2))
                        dve.wait_ge(xn_done, NB + t - 1)
                    nc.vector.tensor_tensor(x1[0:rows, k, :], xr[0:rows, k, :],
                                            ps[0:rows, 2 * k:2 * k + 2, :].rearrange("p a n -> p (a n)"),
                                            ALU.add).then_inc(x1_ready, 1)
                    s = ss6[0:rows, k:k + 1]
                    dve.wait_ge(sq_done, NB + t + 1)
                    nc.vector.tensor_scalar(s, s, 1.0 / D, EPS, ALU.mult, ALU.add).then_inc(ms_done, 1)
                    dve.wait_ge(rt_done, NB + t + 1)
                    nc.vector.reciprocal(s, s).then_inc(rc_done, 1)
                    dve.wait_ge(xn_done, NB + t + 1)
                    nc.vector.tensor_tensor(hg[0:rows, k, :], hn[0:rows, k, :], g_row[0:rows, :], ALU.mult).then_inc(hg_ready, 1)
                    if t >= 3:
                        choose_dve(dve, t - 3, t - 3, 0)
                    dve.wait_ge(xT_done, NB + t + 1)
                    for b in range(2):
                        last = nc.vector.tensor_tensor(
                            h2t_out[:, k, 4 * b:4 * b + 4, 0:rows],
                            ps[:, 4 + b, :].rearrange("p (c t) -> p c t", c=4)[:, :, 0:rows],
                            g_ffn[:, 4 * b:4 * b + 4].unsqueeze(2).broadcast_to([P, 4, rows]), ALU.mult)
                    last.then_inc(hT_done, 1)
                for h in range(TT - 2, PH):
                    choose_dve(dve, h, h, 0)

            @block.scalar
            def _(act):
                def choice(h):
                    queries_act(act, h)
                    if h:
                        scores_act(act, h - 1)
                    turn_act(act, h)

                for t in range(TT + 1):
                    rows, tok = token_rows(t)
                    k = t % 2
                    s = ss6[0:rows, k:k + 1]
                    act.wait_ge(x1_ready, t + 1)
                    nc.scalar.activation(junk6[0:rows, :], x1[0:rows, k, :], ACT.Square, accum_out=s).then_inc(sq_done, 1)
                    act.wait_ge(ms_done, NB + t + 1)
                    nc.scalar.activation(s, s, ACT.Sqrt).then_inc(rt_done, 1)
                    act.wait_ge(rc_done, NB + t + 1)
                    if t >= 2:
                        act.wait_ge(xT_done, NB + t - 1)
                        act.wait_ge(hg_ready, t - 1)
                    nc.scalar.activation(hn[0:rows, k, :], x1[0:rows, k, :], ACT.Copy, scale=s).then_inc(xn_done, 1)
                    if t >= 2:
                        choice(t - 2)
                for h in range(TT - 1, PH):
                    choice(h)
                scores_act(act, PH - 1)

        def gather_pool(pool, g, col):
            for half in range(STEP // RING):
                cols = slice(half * RING, (half + 1) * RING)
                nc.gpsimd.tensor_copy(idx_st[:, cols], idx_cur[:, bass.ds(col + half * RING, RING)]).then_inc(idx_stg, 1)
                pool.wait_ge(idx_stg, g * 2 + (half + 1))
                alone(pool)
                for j in range(half * RING, (half + 1) * RING):
                    pool.wait_ge(slot_free, g * STEP + (j + 1))
                    alone(pool)
                    pool.indirect_dma_start(ring[j % RING], None, dr["uv"],
                                            bass.IndirectOffsetOnAxis(ap=idx_st[:, j:j + 1], axis=0)
                                            ).then_inc(row_in[j % RING], 16)

        def gather_dve(dve, g, j):
            dve.wait_ge(row_in[j % RING], g * (16 * STEP // RING) + 16 * (j // RING + 1))
            if j == 0:
                dve.wait_ge(gelu_d, START + g * (STEP // PAIR))
            dve.wait_ge(dots, START + g * STEP + max(j - 1, 0))
            nc.vector.tensor_tensor_reduce(junk[:, j % 2, :], ring[j % RING][:, 0:D], h2, 1.0, 0.0, ALU.mult, ALU.add,
                                           act_in[:, j:j + 1]).then_inc(dots, 1)

        def gather_act(act, g, col, p, gate_of, pattern, m):
            n = g * (STEP // PAIR) + p
            act.wait_ge(dots, START + g * STEP + PAIR * (p + 1))
            nc.scalar.activation(act_out, act_in[:, PAIR * p:PAIR * (p + 1)], ACT.Gelu).then_inc(gelu_d, 1)
            act.wait_ge(gelu_d, START + n + 1)
            alone(act)
            for q in range(PAIR):
                last = nc.scalar.activation(wgt[:, q:q + 1], gate_of[:, bass.ds(col + (PAIR * p + q), 1)], ACT.Copy,
                                            scale=act_out[:, q:q + 1])
            last.then_inc(wgt_d, 1)
            act.wait_ge(wgt_d, n + 1)
            for q in range(PAIR):
                j = PAIR * p + q
                act.wait_ge(slot_free, g * STEP + (j + RING - 3))
                nc.scalar.activation(diag[:, j % 4, 0:m], pattern, ACT.Copy, scale=wgt[:, q:q + 1]).then_inc(diag_d, 1)

        def gather_pe(pe, g, j, m):
            pe.wait_ge(diag_d, START + g * STEP + (j + 1))
            alone(pe)
            for c in range(2):
                last = nc.tensor.matmul(ps[0:m, c, :], diag[:, j % 4, 0:m],
                                        ring[j % RING][:, D + 512 * c:D + 512 * (c + 1)],
                                        start=False, stop=False, skip_group_check=True)
            last.then_inc(slot_free, 1)

        gates_flat = gates.rearrange("p a b -> p (a b)")

        def first_act(act, b):
            act.wait_ge(tk_done, START + b * PH + PH)
            act.wait_ge(diag_d, START + b * (PH * STEP))
            nc.scalar.activation(gates_flat, logit_next, ACT.Exp).then_inc(ex_d, 1)
            act.wait_ge(gt_v, b * 3 + 3)

        def first_dve(dve, b):
            dve.wait_ge(ex_d, b + 1)
            nc.vector.tensor_reduce(gsum, gates, AX.X, ALU.add).then_inc(gt_v, 1)
            dve.wait_ge(gt_v, b * 3 + 1)
            nc.vector.reciprocal(gsum, gsum).then_inc(gt_v, 1)
            dve.wait_ge(gt_v, b * 3 + 2)
            nc.vector.tensor_tensor(gates, gates, gsum.unsqueeze(2).broadcast_to([P, PH, TOPK]), ALU.mult).then_inc(gt_v, 1)
            dve.wait_ge(h2_in, b * 16 + 16)
            alone(dve)

        def first_pe(pe, b, m):
            pe.wait_ge(acc_out, START + b)
            pe.wait_ge(x1_in, b * 16 + 16)
            for c in range(2):
                last = nc.tensor.matmul(ps[0:m, c, :], ident[:, 0:m], x1b[:, 512 * c:512 * (c + 1)],
                                        start=True, stop=False, skip_group_check=True)
            last.then_inc(init_d, 1)

        def first_sp(sp, b):
            sp.wait_ge(dots, START + b * (PH * STEP))
            sp.dma_start(h2, scr_h2[bass.ds(b * P, P), :]).then_inc(h2_in, 16)
            sp.wait_ge(init_d, START + b)
            sp.dma_start(x1b, scr_x1[bass.ds(b * P, P), :]).then_inc(x1_in, 16)

        def first_pool(pool, b):
            pool.wait_ge(tk_done, START + b * PH + PH)
            alone(pool)
            nc.gpsimd.tensor_copy(idx_cur, idx_next).then_inc(idx_cp, 1)
            pool.wait_ge(idx_cp, START + b + 1)
            alone(pool)

        def last_act(act, b, rows):
            act.wait_ge(acc_out, START + b + 1)
            nc.scalar.activation(junk_y[0:rows], yo[0:rows], ACT.Square, accum_out=ss8[0:rows]).then_inc(sq_done, 1)
            act.wait_ge(ms_done, 2 * NB + b + 1)
            nc.scalar.activation(ss8[0:rows], ss8[0:rows], ACT.Sqrt).then_inc(rt_done, 1)

        def last_dve(dve, b, rows):
            dve.wait_ge(slot_free, b * (PH * STEP) + (PH * STEP if b is not TT else 2 * STEP) + RING)
            dve.wait_ge(yo_clear, START + b)
            nc.vector.tensor_copy(yo[0:rows], acc[0:rows]).then_inc(acc_out, 1)

        def norm_dve(dve, b, rows):
            s = ss8[0:rows]
            dve.wait_ge(sq_done, 2 * NB + b + 1)
            nc.vector.tensor_scalar(s, s, 1.0 / D, EPS, ALU.mult, ALU.add).then_inc(ms_done, 1)
            dve.wait_ge(rt_done, 2 * NB + b + 1)
            nc.vector.reciprocal(s, s).then_inc(rc_done, 1)
            dve.wait_ge(rc_done, 2 * NB + b + 1)
            nc.vector.scalar_tensor_tensor(yo[0:rows], yo[0:rows], s, g_fin[0:rows], ALU.mult, ALU.mult).then_inc(yo_d, 1)

        def store_sp(sp, b, rows):
            sp.wait_ge(yo_d, START + b + 1)
            sp.dma_start(out["y"][bass.ds(b * P, rows), :], yo[0:rows]).then_inc(y_out, 16)
            sp.wait_ge(y_out, b * 16 + 16)
            sp.sem_inc(yo_clear, 1)

        spread, gates_s = take([NS]), take([2 * STEP])
        spread_in, spread_i, spread_g, x1_zero = sem("spread_in"), sem("spread_i"), sem("spread_g"), sem("x1_zero")
        assert A <= AT_HT
        QS = P // NS

        with nc.Block() as block:
            @block.sync
            def _(sp):
                sp.dma_start(g_fin, dr["g_fin_row"].broadcast_to([P, D])).then_inc(pc_in, 16)
                sp.dma_start(spread, dr["spread"]).then_inc(pc_in, 16)
                first_sp(sp, 0)
                h2t_load(sp, 1)
                with sp.Fori(0, TT - 1) as b:
                    sp.wait_ge(q_acc, b * PH + 2 * PH)
                    h2t_load(sp, b + 2)
                    first_sp(sp, b + 1)
                    store_sp(sp, b, P)
                sp.wait_ge(tk_done, START + (TT + 1) * PH)
                sp.wait_ge(idx_stg, TT * PH * STEP // RING)
                for q in range(QS):
                    sp.dma_start(idx_cur[q * NS:(q + 1) * NS, 0:NS], idx_next[0:NS, q * NS:(q + 1) * NS]).then_inc(spread_i, 16)
                sp.wait_ge(gt_v, 3 * (TT + 1))
                for q in range(QS):
                    sp.dma_start(gates_s[q * NS:(q + 1) * NS], gates_flat[0:NS, q * NS:(q + 1) * NS]).then_inc(spread_g, 16)
                sp.wait_ge(dots, START + TT * PH * STEP)
                for q in range(QS):
                    sp.dma_start(h2[q * NS:(q + 1) * NS], scr_h2[SEQ:T, :]).then_inc(spread_in, 16)
                sp.wait_ge(x1_zero, 1)
                sp.dma_start(x1b[0:NS], scr_x1[SEQ:T, :]).then_inc(x1_in, 16)
                store_sp(sp, TT - 1, P)
                store_sp(sp, TT, NS)

            @block.gpsimd
            def _(pool):
                with pool.Fori(0, TT) as b:
                    first_pool(pool, b)
                    with pool.Fori(0, PH) as h:
                        gather_pool(pool, b * PH + h, h * STEP)
                pool.wait_ge(spread_i, 16 * QS)
                for s in range(2):
                    gather_pool(pool, TT * PH + s, s * STEP)

            @block.scalar
            def _(act):
                def steps(b):
                    with act.Fori(0, PH) as h:
                        t = b * PH + h + PH
                        for p in range(STEP // PAIR):
                            gather_act(act, b * PH + h, h * STEP, p, gates_flat, ident[:, :], P)
                            if p == 1:
                                queries_act(act, t)
                            if p == 2:
                                turn_act(act, t)
                                scores_act(act, t)

                first_act(act, 0)
                steps(0)
                with act.Fori(1, TT) as b:
                    first_act(act, b)
                    last_act(act, b - 1, P)
                    steps(b)
                first_act(act, TT)
                last_act(act, TT - 1, P)
                act.wait_ge(spread_g, 16 * QS)
                for s in range(2):
                    for p in range(STEP // PAIR):
                        gather_act(act, TT * PH + s, s * STEP, p, gates_s, spread, NS)
                last_act(act, TT, NS)

            @block.tensor
            def _(pe):
                pe.sem_inc(slot_free, RING)
                with pe.Fori(0, TT) as b:
                    first_pe(pe, b, P)
                    with pe.Fori(0, PH) as h:
                        t = b * PH + h + PH
                        queries_pe(pe, t, b + 1, h, (0,))
                        for j in range(STEP):
                            gather_pe(pe, b * PH + h, j, P)
                            if j == 0:
                                queries_pe(pe, t, b + 1, h, (1,))
                            if j == PAIR:
                                turn_pe(pe, t)
                            if j == 2 * PAIR:
                                scores_pe(pe, t, h)
                first_pe(pe, TT, NS)
                for s in range(2):
                    for j in range(STEP):
                        gather_pe(pe, TT * PH + s, j, NS)

            @block.vector
            def _(dve):
                def steps(b):
                    with dve.Fori(0, PH) as h:
                        for j in range(STEP):
                            gather_dve(dve, b * PH + h, j)
                            if FIRST_J <= j < FIRST_J + CHOICE:
                                choose_dve(dve, b * PH + h + PH, h, b + 1, (j - FIRST_J,))

                dve.wait_ge(pc_in, 48)
                first_dve(dve, 0)
                steps(0)
                with dve.Fori(1, TT) as b:
                    last_dve(dve, b - 1, P)
                    first_dve(dve, b)
                    norm_dve(dve, b - 1, P)
                    steps(b)
                last_dve(dve, TT - 1, P)
                dve.wait_ge(init_d, START + TT)
                nc.vector.memset(x1b, 0.0).then_inc(x1_zero, 1)
                dve.wait_ge(ex_d, TT + 1)
                nc.vector.tensor_reduce(gsum, gates, AX.X, ALU.add).then_inc(gt_v, 1)
                dve.wait_ge(gt_v, TT * 3 + 1)
                nc.vector.reciprocal(gsum, gsum).then_inc(gt_v, 1)
                dve.wait_ge(gt_v, TT * 3 + 2)
                nc.vector.tensor_tensor(gates, gates, gsum.unsqueeze(2).broadcast_to([P, PH, TOPK]), ALU.mult).then_inc(gt_v, 1)
                norm_dve(dve, TT - 1, P)
                dve.wait_ge(spread_in, 16 * QS)
                for s in range(2):
                    for j in range(STEP):
                        gather_dve(dve, TT * PH + s, j)
                last_dve(dve, TT, NS)
                norm_dve(dve, TT, NS)


def _layouts(a):
    import numpy as np
    def f(x):
        return np.ascontiguousarray(x)
    def stationary(w):
        n = w.shape[1] // 128
        return w.reshape(8, 128, n, 128).transpose(2, 1, 0, 3).reshape(n, 128, 1024)
    def moving(w):
        n = w.shape[1] // 512
        return w.reshape(8, 128, n, 512).transpose(2, 1, 0, 3).reshape(n, 128, 4096)
    def pairs(x, y):
        return np.stack([x, y], 1).reshape(-1, 128, 1024)
    def by_state(x):
        return np.moveaxis(x.reshape((32, 2, 64) + x.shape[2:]), 0, 2).reshape((128, 32) + x.shape[2:])
    w_in = a["w_in"][0]
    q, k, v, u, ga, gs = (w_in[:, i * 1024:(i + 1) * 1024] for i in range(6))
    g64 = (64, 64)
    d = {
        "x": np.concatenate([a["x_prompt"].reshape(1024, 1024), a["x_sample"].reshape(32, 1024)]),
        "ident": np.eye(128, dtype=np.float32),
        "g_mix": a["norm_mix_g"].reshape(8, 128).T,
        "g_ffn": a["norm_ffn_g"].reshape(8, 128).T,
        "b_glu": a["b_glu"].reshape(8, 128).T,
        "lam": np.concatenate([a["lambda_q1"], a["lambda_k1"], a["lambda_q2"], a["lambda_k2"]], 1),
        "w_stat": np.concatenate([pairs(stationary(q), stationary(k)),
                                  pairs(stationary(gs), stationary(a["w_proj_s5"][0])),
                                  stationary(a["w_glu"][0]),
                                  pairs(stationary(ga), stationary(a["w_proj_att"][0])),
                                  stationary(a["peer_w_query"][0])]),
        "w_mov": np.concatenate([moving(u), moving(v), moving(a["w_out"][0])]),
        "a_re": by_state(a["s5_a_re"][0]), "a_im": by_state(a["s5_a_im"][0]),
        "log_step": by_state(np.broadcast_to(a["s5_log_step"][0][:, None], g64)),
        "b_ri": np.stack([by_state(a["s5_b_re"][0]), by_state(a["s5_b_im"][0])], 1).reshape(128, -1),
        "c_ri": np.stack([by_state(a["s5_c_re"][0].transpose(0, 2, 1)),
                          by_state(a["s5_c_im"][0].transpose(0, 2, 1))], 1).reshape(128, -1),
        "h0": np.stack([by_state(a["state_s5_re"][0].transpose(1, 2, 0)),
                        by_state(a["state_s5_im"][0].transpose(1, 2, 0))], 1).reshape(128, -1),
        "d_s5": a["s5_d"][0].T,
        "keys": a["peer_sub_keys"][0].transpose(3, 0, 1, 2).reshape(128, 2048),
        "uv": np.concatenate([a["peer_u"][0], a["peer_v"][0]], 1),
        "g_ffn_row": a["norm_ffn_g"], "g_fin_row": a["norm_final_g"].reshape(1, 1024),
        "subln": a["subln_g"].reshape(128, 1),
        "cache_k": a["cache_k"][0].reshape(-1, 128, 1024), "cache_v": a["cache_v"][0].reshape(-1, 128, 1024),
        "pages": a["page_table"].reshape(1, 64),
    }
    i128 = np.arange(128)
    d["causal"] = np.where(i128[None, :] <= i128[:, None], 0, NEG).astype(np.float32)
    row = np.arange(64)
    tok = np.arange(32)
    d["causal_new"] = np.where((tok[None, None, :] // 4 == np.arange(8)[None, :, None])
                               & (tok[None, None, :] % 4 <= (row % 4)[:, None, None]), 0, NEG).astype(np.float32).reshape(64, 256)
    d["pick"] = ((row[:, None] // 8 == tok[None, :] // 4) & (row[:, None] % 4 == tok[None, :] % 4)).astype(np.float32)
    d["first"] = ((row % 8) < 4).astype(np.float32).reshape(64, 1)
    d["spread"] = np.tile(np.eye(32, dtype=np.float32), (4, 1))
    d["iota16"] = np.broadcast_to(np.arange(16, dtype=np.float32), (128, 16))
    return {k: f(v) for k, v in d.items()}


_OUTS = {
    "y": (1056, 1024), "k": (1056, 1024), "v": (1056, 1024), "s5_prompt": (128, 64), "s5_sample": (128, 512),
}


def kernel(**inputs):
    import concourse.bacc as bacc
    from concourse.bass_utils import run_bass_kernel_spmd

    arrays = _layouts({k: np.asarray(v) for k, v in inputs.items()})
    nc = bacc.Bacc("TRN2", target_bir_lowering=False, num_devices=1)
    dr = {n: nc.dram_tensor("in_" + n, a.shape, mybir.dt.from_np(a.dtype), kind="ExternalInput").ap()
          for n, a in arrays.items()}
    out = {n: nc.dram_tensor("out_" + n, s, F32, kind="ExternalOutput").ap() for n, s in _OUTS.items()}
    hybrid_step(nc, dr, out)
    r = run_bass_kernel_spmd(nc, [{"in_" + n: a for n, a in arrays.items()}], core_ids=[0]).results[0]
    y, k, v = r["out_y"], r["out_k"], r["out_v"]
    def by_group(x):
        return np.moveaxis(x.reshape((2, 64) + x.shape[1:]), 2, 0).reshape((64, 64) + x.shape[2:])
    sp = r["out_s5_prompt"].reshape(128, 2, 32)
    ss = r["out_s5_sample"].reshape(128, 2, 32, 8)
    hp = [by_group(sp[:, i]).reshape(1, 1, 64, 64) for i in range(2)]
    hsm = [by_group(ss[:, i]).transpose(2, 0, 1).reshape(1, 8, 64, 64) for i in range(2)]
    f = np.ascontiguousarray
    return (f(y[:1024].reshape(1, 1024, 1024)), f(y[1024:].reshape(8, 4, 1024)),
            f(k[:1024].reshape(1, 1, 1024, 8, 128)), f(v[:1024].reshape(1, 1, 1024, 8, 128)),
            f(hp[0]), f(hp[1]),
            f(k[1024:].reshape(1, 8, 4, 8, 128)), f(v[1024:].reshape(1, 8, 4, 8, 128)),
            f(hsm[0]), f(hsm[1]))
```
